# Optimizing a Trainium2 kernel written in Bass

```python
import math
import jax, jax.numpy as jnp
from jax import lax
import numpy as np
import jax
import jax.numpy as jnp

D_MODEL = 1024
BATCH = 1
SEQ = 256
DEPTH = 2

CHUNK = 64
D_MIX = D_MODEL
CONV_GROUPS = 8
CONV_GROUP_DIM = 64
W_CONV = CONV_GROUPS * CONV_GROUP_DIM
CONV_K = 3
LRU_HEADS = 8
LRU_HEAD_DIM = 64
W_LRU = LRU_HEADS * LRU_HEAD_DIM
LRU_CONV_K = 4
RG_C = 8.0
D_IN_TOT = 3 * W_CONV + 2 * W_LRU
D_FF = 3584
N_EXPERTS = 8
TOP_K = 2
N_DENSE = (DEPTH + 1) // 2
N_MOE = DEPTH // 2
EPS = 1e-6


def rms_norm(x, g):
    xf = x.astype(jnp.float32)
    y = xf * lax.rsqrt(jnp.mean(xf * xf, axis=-1, keepdims=True) + EPS)
    return (y * g.astype(jnp.float32)).astype(x.dtype)

def causal_depthwise_conv(x, w):
    k = w.shape[0]
    c = x.shape[-1]
    return lax.conv_general_dilated(
        x, w[:, None, :].astype(x.dtype), window_strides=(1,), padding=[(k - 1, 0)],
        dimension_numbers=("NWC", "WIO", "NWC"), feature_group_count=c)

def chunked_linear_scan(a, b):
    bsz, s, w = a.shape
    nc = s // CHUNK
    a_c = a.reshape(bsz, nc, CHUNK, w).transpose(1, 0, 2, 3)
    b_c = b.reshape(bsz, nc, CHUNK, w).transpose(1, 0, 2, 3)

    def combine(left, right):
        al, bl = left
        ar, br = right
        return al * ar, ar * bl + br

    def step(h_prev, ab):
        ac, bc = ab
        a_cum, b_cum = lax.associative_scan(combine, (ac, bc), axis=1)
        h = a_cum * h_prev[:, None, :] + b_cum
        return h[:, -1, :], h

    h0 = jnp.zeros((bsz, w), jnp.float32)
    _, hs = lax.scan(step, h0, (a_c, b_c))
    return hs.transpose(1, 0, 2, 3).reshape(bsz, s, w)

def rg_lru(x, wa, ba, wx, bx, lam):
    bsz, s, _ = x.shape
    xh = x.reshape(bsz, s, LRU_HEADS, LRU_HEAD_DIM)
    r = jax.nn.sigmoid((jnp.einsum("bshi,hij->bshj", xh, wa).reshape(bsz, s, W_LRU) + ba).astype(jnp.float32))
    i = jax.nn.sigmoid((jnp.einsum("bshi,hij->bshj", xh, wx).reshape(bsz, s, W_LRU) + bx).astype(jnp.float32))
    log_a = -RG_C * r * jax.nn.softplus(-lam.astype(jnp.float32))
    a = jnp.exp(log_a)
    b = jnp.sqrt(-jnp.expm1(2.0 * log_a)) * (i * x.astype(jnp.float32))
    return chunked_linear_scan(a, b).astype(x.dtype)

def hybrid_mixer(h, w_in, conv_w, lru_conv_w, lru_conv_b, wa, ba, wx, bx, lam, w_out):
    p = h @ w_in
    c_gate, b_gate, v, u, g = jnp.split(
        p, [W_CONV, 2 * W_CONV, 3 * W_CONV, 3 * W_CONV + W_LRU], axis=-1)
    y_a = b_gate * causal_depthwise_conv(c_gate * v, conv_w)
    uc = causal_depthwise_conv(u, lru_conv_w) + lru_conv_b
    y_b = rg_lru(uc, wa, ba, wx, bx, lam) * jax.nn.gelu(g)
    return jnp.concatenate([y_a, y_b], axis=-1) @ w_out

def swiglu(x, wg, wu, wd):
    return (jax.nn.silu(x @ wg) * (x @ wu)) @ wd

def moe_swiglu(h, w_router, wg, wu, wd):
    bsz, s, d = h.shape
    xt = h.reshape(-1, d)
    logits = (xt @ w_router).astype(jnp.float32)
    top_v, top_i = lax.top_k(logits, TOP_K)
    gates = jax.nn.softmax(top_v, axis=-1)
    comb = jnp.sum(jax.nn.one_hot(top_i, N_EXPERTS, dtype=jnp.float32) * gates[..., None], axis=1)
    comb = comb.astype(h.dtype)
    y = jnp.zeros_like(xt)
    for e in range(N_EXPERTS):
        y = y + comb[:, e:e + 1] * swiglu(xt, wg[e], wu[e], wd[e])
    return y.reshape(bsz, s, d)

def first_inputs(seed: int = 0) -> dict:
    key = jax.random.key(seed)
    ks = jax.random.split(key, 24)
    f32 = jnp.float32
    nrm = lambda k, shape, fan_in: jax.random.normal(k, shape, f32) * (fan_in ** -0.5)
    u = jax.random.uniform(ks[11], (DEPTH, W_LRU), f32, minval=0.9, maxval=0.999)
    a0 = u ** (1.0 / RG_C)
    lam = jnp.log(a0) - jnp.log1p(-a0)
    return {
        "x": jax.random.normal(ks[0], (BATCH, SEQ, D_MODEL), f32),
        "norm_mix": 1.0 + 0.02 * jax.random.normal(ks[1], (DEPTH, D_MODEL), f32),
        "norm_ffn": 1.0 + 0.02 * jax.random.normal(ks[2], (DEPTH, D_MODEL), f32),
        "norm_final": 1.0 + 0.02 * jax.random.normal(ks[3], (D_MODEL,), f32),
        "w_in": nrm(ks[4], (DEPTH, D_MODEL, D_IN_TOT), D_MODEL),
        "conv_w": nrm(ks[5], (DEPTH, CONV_K, W_CONV), CONV_K),
        "lru_conv_w": nrm(ks[6], (DEPTH, LRU_CONV_K, W_LRU), LRU_CONV_K),
        "lru_conv_b": 0.02 * jax.random.normal(ks[7], (DEPTH, W_LRU), f32),
        "lru_wa": nrm(ks[8], (DEPTH, LRU_HEADS, LRU_HEAD_DIM, LRU_HEAD_DIM), LRU_HEAD_DIM),
        "lru_ba": 0.02 * jax.random.normal(ks[9], (DEPTH, W_LRU), f32),
        "lru_wx": nrm(ks[10], (DEPTH, LRU_HEADS, LRU_HEAD_DIM, LRU_HEAD_DIM), LRU_HEAD_DIM),
        "lru_bx": 0.02 * jax.random.normal(ks[12], (DEPTH, W_LRU), f32),
        "lru_lambda": lam,
        "w_out": nrm(ks[13], (DEPTH, D_MIX, D_MODEL), D_MIX),
        "ffn_w_gate": nrm(ks[14], (N_DENSE, D_MODEL, D_FF), D_MODEL),
        "ffn_w_up": nrm(ks[15], (N_DENSE, D_MODEL, D_FF), D_MODEL),
        "ffn_w_down": nrm(ks[16], (N_DENSE, D_FF, D_MODEL), D_FF),
        "w_router": nrm(ks[17], (N_MOE, D_MODEL, N_EXPERTS), D_MODEL),
        "moe_w_gate": nrm(ks[18], (N_MOE, N_EXPERTS, D_MODEL, D_FF), D_MODEL),
        "moe_w_up": nrm(ks[19], (N_MOE, N_EXPERTS, D_MODEL, D_FF), D_MODEL),
        "moe_w_down": nrm(ks[20], (N_MOE, N_EXPERTS, D_FF, D_MODEL), D_FF),
    }

def first_block(x, norm_mix, norm_ffn, norm_final, w_in, conv_w, lru_conv_w, lru_conv_b,
              lru_wa, lru_ba, lru_wx, lru_bx, lru_lambda, w_out,
              ffn_w_gate, ffn_w_up, ffn_w_down,
              w_router, moe_w_gate, moe_w_up, moe_w_down):
    for l in range(DEPTH):
        h = rms_norm(x, norm_mix[l])
        x = x + hybrid_mixer(h, w_in[l], conv_w[l], lru_conv_w[l], lru_conv_b[l],
                             lru_wa[l], lru_ba[l], lru_wx[l], lru_bx[l], lru_lambda[l], w_out[l])
        h = rms_norm(x, norm_ffn[l])
        j = l // 2
        if l % 2 == 0:
            x = x + swiglu(h, ffn_w_gate[j], ffn_w_up[j], ffn_w_down[j])
        else:
            x = x + moe_swiglu(h, w_router[j], moe_w_gate[j], moe_w_up[j], moe_w_down[j])
    return rms_norm(x, norm_final)


RMS_EPS = 1e-6
SSD_WIDTH = D_MODEL
SSD_HEAD_DIM = 64
SSD_HEADS = SSD_WIDTH // SSD_HEAD_DIM
SSD_GROUPS = 2
SSD_HEADS_PER_GROUP = SSD_HEADS // SSD_GROUPS
SSD_STATE = 64
SSD_CONV = 4
SSD_CHUNK = 128
SSD_CONV_DIM = SSD_WIDTH + 2 * SSD_GROUPS * SSD_STATE
GLA_HEADS = 8
GLA_VALUE_WIDTH = D_MODEL
GLA_KEY_WIDTH = D_MODEL // 2
GLA_HEAD_K = GLA_KEY_WIDTH // GLA_HEADS
GLA_HEAD_V = GLA_VALUE_WIDTH // GLA_HEADS
GLA_GATE_RANK = 16
GLA_GATE_NORMALIZER = 16.0
GLA_CHUNK = 64
EVEN_SPLITS = (SSD_WIDTH, SSD_CONV_DIM, SSD_HEADS, GLA_KEY_WIDTH, GLA_KEY_WIDTH, GLA_VALUE_WIDTH, GLA_GATE_RANK, GLA_VALUE_WIDTH)
EVEN_IN_WIDTH = sum(EVEN_SPLITS)
EVEN_MIX_WIDTH = SSD_WIDTH + GLA_VALUE_WIDTH
MOBA_HEADS = 16
MOBA_HEAD_DIM = 64
MOBA_WIDTH = MOBA_HEADS * MOBA_HEAD_DIM
MOBA_BLOCK = 256
MOBA_TOPK = 3
MOBA_Q_CHUNK = 32
ODD_IN_WIDTH = 4 * MOBA_WIDTH
N_EVEN = (DEPTH + 1) // 2
N_ODD = DEPTH // 2


def rms_norm_2(x, w):
    x32 = x.astype(jnp.float32)
    y = x32 * lax.rsqrt(jnp.mean(x32 * x32, axis=-1, keepdims=True) + RMS_EPS)
    return y * w.astype(jnp.float32)

def split_cols(u, sizes):
    cuts = [int(c) for c in np.cumsum(sizes)[:-1]]
    return jnp.split(u, cuts, axis=-1)

def causal_depthwise_conv_2(u, w, b):
    k_width = w.shape[0]
    y = lax.conv_general_dilated(u, w.astype(u.dtype)[:, None, :], window_strides=(1,), padding=[(k_width - 1, 0)], dimension_numbers=('NWC', 'WIO', 'NWC'), feature_group_count=u.shape[-1])
    return y + b.astype(u.dtype)

def ssd_chunked_scan(xs, dt, a, bm, cm, d_skip):
    b, L, G, E, P = xs.shape
    N = bm.shape[-1]
    Q = SSD_CHUNK
    nc = L // Q
    x_c = xs.reshape(b, nc, Q, G, E, P)
    dt_c = dt.reshape(b, nc, Q, G, E)
    xdt = x_c * dt_c[..., None]
    b_c = bm.reshape(b, nc, Q, G, N)
    c_c = cm.reshape(b, nc, Q, G, N)
    a_cs = jnp.cumsum(dt_c * a, axis=2)
    a_t = jnp.moveaxis(a_cs, 2, -1)
    seg = a_t[..., :, None] - a_t[..., None, :]
    causal = jnp.tril(jnp.ones((Q, Q), dtype=bool))
    decay_ij = jnp.exp(jnp.where(causal, seg, -jnp.inf))
    cb = jnp.einsum('bcign,bcjgn->bcgij', c_c, b_c)
    y_diag = jnp.einsum('bcgeij,bcjgep->bcigep', cb[:, :, :, None] * decay_ij, xdt)
    a_last = a_cs[:, :, -1]
    decay_to_end = jnp.exp(a_last[:, :, None] - a_cs)
    chunk_states = jnp.einsum('bcjgn,bcjge,bcjgep->bcgepn', b_c, decay_to_end, xdt)

    def carry_state(h, inp):
        chunk_decay, s = inp
        return chunk_decay[..., None, None] * h + s, h

    _, prev_states = lax.scan(carry_state, jnp.zeros_like(chunk_states[:, 0]), (jnp.moveaxis(jnp.exp(a_last), 1, 0), jnp.moveaxis(chunk_states, 1, 0)))
    prev_states = jnp.moveaxis(prev_states, 0, 1)
    y_off = jnp.einsum('bcign,bcgepn->bcigep', c_c, prev_states) * jnp.exp(a_cs)[..., None]
    y = y_diag + y_off + d_skip[:, :, None] * x_c
    return y.reshape(b, L, G * E * P)

def gla_chunked(q, k, v, log_decay):
    b, L, H, dk = q.shape
    dv = v.shape[-1]
    C = GLA_CHUNK
    n = L // C
    q = q.reshape(b, n, C, H, dk)
    k = k.reshape(b, n, C, H, dk)
    v = v.reshape(b, n, C, H, dv)
    gcs = jnp.cumsum(log_decay.reshape(b, n, C, H, dk), axis=2)
    ref = gcs[:, :, C // 2:C // 2 + 1]
    scores = jnp.einsum('bnihd,bnjhd->bnhij', q * jnp.exp(gcs - ref), k * jnp.exp(ref - gcs))
    causal = jnp.tril(jnp.ones((C, C), dtype=bool))
    scores = jnp.where(causal, scores, 0.0)
    o_intra = jnp.einsum('bnhij,bnjhv->bnihv', scores, v)
    g_last = gcs[:, :, -1]
    chunk_kv = jnp.einsum('bnjhd,bnjhv->bnhdv', k * jnp.exp(g_last[:, :, None] - gcs), v)

    def carry_state(s, inp):
        decay, kv = inp
        return decay[..., None] * s + kv, s

    _, prev_states = lax.scan(carry_state, jnp.zeros_like(chunk_kv[:, 0]), (jnp.moveaxis(jnp.exp(g_last), 1, 0), jnp.moveaxis(chunk_kv, 1, 0)))
    prev_states = jnp.moveaxis(prev_states, 0, 1)
    o_inter = jnp.einsum('bnihd,bnhdv->bnihv', q * jnp.exp(gcs), prev_states)
    return (o_intra + o_inter).reshape(b, L, H, dv)

def ssd_gla_layer(x, norm_w, w_in, conv_w, conv_b, a_log, dt_bias, d_skip, ssd_norm_w, gate_w2, gate_b, gla_norm_w, w_out):
    bsz, L, _ = x.shape
    h = rms_norm_2(x, norm_w)
    u = h @ w_in.astype(jnp.float32)
    z_a, xbc, dt_raw, q_b, k_b, v_b, gate_lr, g_b = split_cols(u, EVEN_SPLITS)
    xbc = jax.nn.silu(causal_depthwise_conv_2(xbc, conv_w, conv_b))
    xs, bm, cm = split_cols(xbc, (SSD_WIDTH, SSD_GROUPS * SSD_STATE, SSD_GROUPS * SSD_STATE))
    xs = xs.reshape(bsz, L, SSD_GROUPS, SSD_HEADS_PER_GROUP, SSD_HEAD_DIM)
    bm = bm.reshape(bsz, L, SSD_GROUPS, SSD_STATE)
    cm = cm.reshape(bsz, L, SSD_GROUPS, SSD_STATE)
    dt = jax.nn.softplus(dt_raw + dt_bias.astype(jnp.float32)).reshape(bsz, L, SSD_GROUPS, SSD_HEADS_PER_GROUP)
    a = -jnp.exp(a_log.astype(jnp.float32)).reshape(SSD_GROUPS, SSD_HEADS_PER_GROUP)
    d = d_skip.astype(jnp.float32).reshape(SSD_GROUPS, SSD_HEADS_PER_GROUP)
    y_a = ssd_chunked_scan(xs, dt, a, bm, cm, d)
    y_a = rms_norm_2(y_a * jax.nn.silu(z_a), ssd_norm_w)
    q_b = q_b.reshape(bsz, L, GLA_HEADS, GLA_HEAD_K) * (GLA_HEAD_K ** -0.5)
    k_b = k_b.reshape(bsz, L, GLA_HEADS, GLA_HEAD_K)
    v_b = v_b.reshape(bsz, L, GLA_HEADS, GLA_HEAD_V)
    log_decay = jax.nn.log_sigmoid(gate_lr @ gate_w2.astype(jnp.float32) + gate_b.astype(jnp.float32)) / GLA_GATE_NORMALIZER
    log_decay = log_decay.reshape(bsz, L, GLA_HEADS, GLA_HEAD_K)
    o_b = gla_chunked(q_b, k_b, v_b, log_decay)
    o_b = rms_norm_2(o_b, gla_norm_w).reshape(bsz, L, GLA_VALUE_WIDTH) * jax.nn.silu(g_b)
    out = jnp.concatenate([y_a, o_b], axis=-1) @ w_out.astype(jnp.float32)
    return x + out.astype(x.dtype)

def moba_attention(q, k, v):
    b, H, L, d = q.shape
    nb = -(-L // MOBA_BLOCK)
    lp = nb * MOBA_BLOCK
    pad = ((0, 0), (0, 0), (0, lp - L), (0, 0))
    q = jnp.pad(q * (d ** -0.5), pad)
    k = jnp.pad(k, pad)
    v = jnp.pad(v, pad)
    kb = k.reshape(b, H, nb, MOBA_BLOCK, d)
    vb = v.reshape(b, H, nb, MOBA_BLOCK, d)
    k_mean = jnp.mean(kb, axis=3)
    gate = jnp.einsum('bhqd,bhnd->bhqn', q, k_mean).astype(jnp.float32)
    n_past_all = jnp.arange(lp) // MOBA_BLOCK
    fully_past = jnp.arange(nb)[None, :] < n_past_all[:, None]
    gate = jnp.where(fully_past, gate, -jnp.inf)
    k_sel = min(MOBA_TOPK, nb)
    _, top_idx = lax.top_k(gate, k_sel)
    bi = jnp.arange(b)[:, None, None]
    hi = jnp.arange(H)[None, :, None]

    def attend_chunk(start):
        qc = lax.dynamic_slice_in_dim(q, start, MOBA_Q_CHUNK, axis=2)
        idx_c = lax.dynamic_slice_in_dim(top_idx, start, MOBA_Q_CHUNK, axis=2)
        pos = start + jnp.arange(MOBA_Q_CHUNK)
        n_past = pos // MOBA_BLOCK
        logits = []
        for s in range(k_sel):
            ks = kb[bi, hi, idx_c[..., s]]
            ls = jnp.einsum('bhqd,bhqkd->bhqk', qc, ks).astype(jnp.float32)
            logits.append(jnp.where((s < n_past)[:, None], ls, -jnp.inf))
        own = start // MOBA_BLOCK
        ko = lax.dynamic_index_in_dim(kb, own, axis=2, keepdims=False)
        vo = lax.dynamic_index_in_dim(vb, own, axis=2, keepdims=False)
        lo = jnp.einsum('bhqd,bhkd->bhqk', qc, ko).astype(jnp.float32)
        key_pos = own * MOBA_BLOCK + jnp.arange(MOBA_BLOCK)
        logits.append(jnp.where(key_pos[None, :] <= pos[:, None], lo, -jnp.inf))
        p = jax.nn.softmax(jnp.concatenate(logits, axis=-1), axis=-1)
        p_parts = jnp.split(p, k_sel + 1, axis=-1)
        out = jnp.einsum('bhqk,bhkd->bhqd', p_parts[-1].astype(vo.dtype), vo)
        for s in range(k_sel):
            vs = vb[bi, hi, idx_c[..., s]]
            out = out + jnp.einsum('bhqk,bhqkd->bhqd', p_parts[s].astype(vs.dtype), vs)
        return out

    starts = jnp.arange(lp // MOBA_Q_CHUNK) * MOBA_Q_CHUNK
    outs = lax.map(attend_chunk, starts)
    out = jnp.moveaxis(outs, 0, 2).reshape(b, H, lp, d)
    return out[:, :, :L]

def moba_layer(x, norm_w, w_in, w_out):
    bsz, L, _ = x.shape
    h = rms_norm_2(x, norm_w)
    u = h @ w_in.astype(jnp.float32)
    q, k, v, z = split_cols(u, (MOBA_WIDTH, MOBA_WIDTH, MOBA_WIDTH, MOBA_WIDTH))
    to_heads = lambda t: t.reshape(bsz, L, MOBA_HEADS, MOBA_HEAD_DIM).transpose(0, 2, 1, 3)
    o = moba_attention(to_heads(q), to_heads(k), to_heads(v))
    o = o.transpose(0, 2, 1, 3).reshape(bsz, L, MOBA_WIDTH) * jax.nn.silu(z)
    return x + (o @ w_out.astype(jnp.float32)).astype(x.dtype)

def second_inputs(seed: int = 0) -> dict:
    key = jax.random.key(seed)
    ks = jax.random.split(key, 20)
    nrm = jax.random.normal
    f32 = jnp.float32
    dt_init = jnp.exp(jax.random.uniform(ks[6], (N_EVEN, SSD_HEADS), f32, np.log(1e-3), np.log(1e-1)))
    return {
        'x': nrm(ks[0], (BATCH, SEQ, D_MODEL), f32),
        'even_norm': 1.0 + 0.02 * nrm(ks[1], (N_EVEN, D_MODEL), f32),
        'even_w_in': nrm(ks[2], (N_EVEN, D_MODEL, EVEN_IN_WIDTH), f32) * D_MODEL ** -0.5,
        'even_conv_w': nrm(ks[3], (N_EVEN, SSD_CONV, SSD_CONV_DIM), f32) * SSD_CONV ** -0.5,
        'even_conv_b': 0.02 * nrm(ks[4], (N_EVEN, SSD_CONV_DIM), f32),
        'even_a_log': jnp.log(jax.random.uniform(ks[5], (N_EVEN, SSD_HEADS), f32, 1.0, 16.0)),
        'even_dt_bias': dt_init + jnp.log(-jnp.expm1(-dt_init)),
        'even_d_skip': 1.0 + 0.1 * nrm(ks[7], (N_EVEN, SSD_HEADS), f32),
        'even_ssd_norm': 1.0 + 0.02 * nrm(ks[8], (N_EVEN, SSD_WIDTH), f32),
        'even_gate_w2': nrm(ks[9], (N_EVEN, GLA_GATE_RANK, GLA_KEY_WIDTH), f32) * GLA_GATE_RANK ** -0.5,
        'even_gate_b': 0.1 * nrm(ks[10], (N_EVEN, GLA_KEY_WIDTH), f32),
        'even_gla_norm': 1.0 + 0.02 * nrm(ks[11], (N_EVEN, GLA_HEAD_V), f32),
        'even_w_out': nrm(ks[12], (N_EVEN, EVEN_MIX_WIDTH, D_MODEL), f32) * EVEN_MIX_WIDTH ** -0.5,
        'odd_norm': 1.0 + 0.02 * nrm(ks[13], (N_ODD, D_MODEL), f32),
        'odd_w_in': nrm(ks[14], (N_ODD, D_MODEL, ODD_IN_WIDTH), f32) * D_MODEL ** -0.5,
        'odd_w_out': nrm(ks[15], (N_ODD, MOBA_WIDTH, D_MODEL), f32) * MOBA_WIDTH ** -0.5,
        'final_norm': 1.0 + 0.02 * nrm(ks[16], (D_MODEL,), f32),
    }

def second_block(x, even_norm, even_w_in, even_conv_w, even_conv_b, even_a_log, even_dt_bias, even_d_skip, even_ssd_norm, even_gate_w2, even_gate_b, even_gla_norm, even_w_out, odd_norm, odd_w_in, odd_w_out, final_norm):
    for layer in range(DEPTH):
        i = layer // 2
        if layer % 2 == 0:
            x = ssd_gla_layer(x, even_norm[i], even_w_in[i], even_conv_w[i], even_conv_b[i], even_a_log[i], even_dt_bias[i], even_d_skip[i], even_ssd_norm[i], even_gate_w2[i], even_gate_b[i], even_gla_norm[i], even_w_out[i])
        else:
            x = moba_layer(x, odd_norm[i], odd_w_in[i], odd_w_out[i])
    return rms_norm_2(x, final_norm).astype(x.dtype)


def setup_inputs(seed=0):
    out = dict(first_inputs(seed))
    for name, value in second_inputs(seed + 1).items():
        if name != "x":
            out[name + "_2"] = value
    return out


def reference(
    x, norm_mix, norm_ffn, norm_final, w_in, conv_w, lru_conv_w, lru_conv_b, lru_wa, lru_ba,
    lru_wx, lru_bx, lru_lambda, w_out, ffn_w_gate, ffn_w_up, ffn_w_down, w_router, moe_w_gate,
    moe_w_up, moe_w_down, even_norm_2, even_w_in_2, even_conv_w_2, even_conv_b_2, even_a_log_2,
    even_dt_bias_2, even_d_skip_2, even_ssd_norm_2, even_gate_w2_2, even_gate_b_2,
    even_gla_norm_2, even_w_out_2, odd_norm_2, odd_w_in_2, odd_w_out_2, final_norm_2,
):
    x = first_block(
        x, norm_mix, norm_ffn, norm_final, w_in, conv_w, lru_conv_w, lru_conv_b, lru_wa, lru_ba,
        lru_wx, lru_bx, lru_lambda, w_out, ffn_w_gate, ffn_w_up, ffn_w_down, w_router,
        moe_w_gate, moe_w_up, moe_w_down,
    )
    return second_block(
        x, even_norm_2, even_w_in_2, even_conv_w_2, even_conv_b_2, even_a_log_2, even_dt_bias_2,
        even_d_skip_2, even_ssd_norm_2, even_gate_w2_2, even_gate_b_2, even_gla_norm_2,
        even_w_out_2, odd_norm_2, odd_w_in_2, odd_w_out_2, final_norm_2,
    )


_drawn_inputs = setup_inputs


def setup_inputs(seed=0):
    import zlib

    import numpy as np

    out = dict(_drawn_inputs(seed))
    spreads = {}
    factors = {'lru_ba': 8.0,
     'lru_bx': 8.0,
     'even_conv_b_2': 4.085,
     'even_ssd_norm_2': 4.984,
     'even_gate_b_2': 3.949,
     'even_gla_norm_2': 7.942,
     'odd_norm_2': 8.0,
     'final_norm_2': 2.727}
    for name, (base, spread) in spreads.items():
        noise = np.random.default_rng([zlib.crc32(name.encode()), seed]).standard_normal(out[name].shape)
        drawn = base * np.exp(spread * noise) if base else spread * noise
        out[name] = jnp.asarray(drawn.astype(out[name].dtype))
    for name, factor in factors.items():
        out[name] = (out[name] * factor).astype(out[name].dtype)
    return out
```

```python
from contextlib import ExitStack

import concourse.bass as bass
from concourse import mybir

F32 = mybir.dt.float32
F32R = mybir.dt.float32r
I32 = mybir.dt.int32
ALU = mybir.AluOpType
ACT = mybir.ActivationFunctionType
AX_X = mybir.AxisListType.X

P = 128
D = 1024
S = 256
NT = S // P
KD = D // P
EPS = 1e-6
FF = 3584
GW = 512
NG = FF // GW
NE = 8
NJMAX = 11
RAW, SPL = 6, 3
UW = 2048

U_LRU0 = 0
U_FFN = U_LRU0 + 14
U_LRU1 = U_FFN + 6 * NG
U_MOE = U_LRU1 + 14
U_SSD = U_MOE
U_MOBA = U_SSD + 29
U_END = U_MOBA + 20

C_NMIX, C_NFFN, C_CONV, C_LCONV, C_LCB, C_BA, C_BX, C_LAM = 0, 16, 32, 56, 88, 96, 104, 112
C_ENORM, C_ONORM, C_ECONV, C_ECB, C_SSDN, C_GB, C_GLAN = 0, 8, 16, 56, 66, 74, 78
R0, R1 = 120, 79

E_Z, E_XBC, E_DT, E_Q, E_K, E_V, E_LR, E_G = 0, 1024, 2304, 2320, 2832, 3344, 4368, 4384


def build(nc, a, out):
    with ExitStack() as ctx:
        def sb(name, shape, dt=F32):
            return ctx.enter_context(nc.sbuf_tensor(name, shape, dt))

        names = {}

        def sem(name):
            if name not in names:
                names[name] = ctx.enter_context(nc.semaphore(name))
            return names[name]

        raw = sb("raw", [P, RAW, UW])
        whi = sb("whi", [P, SPL, UW], F32R)
        wlo = sb("wlo", [P, SPL, UW], F32R)
        X = sb("X", [P, NT, D])
        hTf = sb("hTf", [P, KD, S])
        hhi = sb("hhi", [P, 2048], F32R)
        hlo = sb("hlo", [P, 2048], F32R)
        ya = sb("ya", [P, 4096], F32R)
        with nc.sbuf_tensor("gb", [P, 4096], F32) as gb:
            pass
        yb = sb("yb", [P, 4096], F32R)
        A = sb("arena", [P, 10752])
        ident = sb("ident", [P, P])
        utri = sb("utri", [P, P])
        ustr = sb("ustr", [P, P])
        ones = sb("ones", [P, P])
        iot = sb("iot", [P, P])
        bdm = sb("bdm", [P, P], I32)
        PT = sb("PT", [P, 2, P])
        m01 = sb("m01", [P, S])
        sm = sb("sm", [P, 256])
        tab = sb("tab", [P, 4], I32)
        ps = ctx.enter_context(nc.psum_tensor("ps", [P, 8, 512], F32))

        def ar(o, *shape):
            n = 1
            for s in shape:
                n *= s
            v = A[:, o:o + n]
            return v if len(shape) == 1 else v.rearrange(
                "p (a b) -> p a b" if len(shape) == 2 else "p (a b c) -> p a b c",
                **dict(zip("abc", shape)))

        def gbv(o, *shape):
            n = 1
            for s in shape:
                n *= s
            v = gb[:, o:o + n]
            return v if len(shape) == 1 else v.rearrange("p (a b) -> p a b", a=shape[0])

        H = 8224
        HTOK = ar(H, NT, D)
        ssq, rst, tpow, mhalf = sm[:, 0:16], sm[:, 16:32], sm[:, 32:48], sm[:, 48:64]
        s8 = sm[:, 64:72]
        one_col = ones[:, 0:1]

        UP, UC, GG, CV, CO = ar(0, 4, 259), ar(1040, 4, S), ar(2064, 4, S), ar(3088, 4, 258), ar(4128, 4, S)
        RR, II, TT, YF = ar(5152, 4, S), ar(6176, 4, S), ar(7200, 4, S), ar(H, KD, S)
        GT = ar(0, 4, S)

        w_loaded = [sem(f"w_loaded{i}") for i in range(RAW)]
        w_hi, w_lo, w_used = sem("w_hi"), sem("w_lo"), sem("w_used")

        def plus(c, k, d):
            return c if isinstance(d, int) and d == 0 else d * k + c

        def hi_of(u):
            return whi[:, u[0] % SPL, :]

        def lo_of(u):
            return wlo[:, u[0] % SPL, :]

        def cols(m, o, w, k0, k1):
            return m.rearrange("(k p) n -> p k n", p=P)[:, k0:k1, o:o + w]

        w_in, w_out = a["w_in"], a["w_out"]
        ewi, ewo = a["even_w_in_2"][0], a["even_w_out_2"][0]
        owi, owo = a["odd_w_in_2"][0], a["odd_w_out_2"][0]
        fg, fu, fd = a["ffn_w_gate"][0], a["ffn_w_up"][0], a["ffn_w_down"][0]
        LRU_ORDER = (3, 4, 0, 2, 1)
        TB = (0, 0, 0, 0, 0, 4, 0, 0, 0)
        BG = A[:, 5152:6176]

        s_par, s_x, s_out = sem("par_loaded"), sem("x_loaded"), sem("out_stored")
        s_bg = sem("gain_loaded")
        s_const = sem("consts_made")
        s_pt = sem("params_turned")
        s_ptc = sem("params_copied")
        N_PAR = 15 + 7 + 8
        block = ctx.enter_context(nc.Block())

        @block.sync
        def _(sp):
            def load(u, src):
                c, d = u
                if c >= RAW or not isinstance(d, int):
                    sp.wait_ge(w_lo, plus(c - RAW + 1, 6, d))
                dst = raw[:, c % RAW, :]
                if len(src.shape) == 3:
                    dst = dst.rearrange("p (k n) -> p k n", k=src.shape[1])
                sp.dma_start(dst, src).then_inc(w_loaded[c % RAW], 16)

            def load_group(c, m, o, d=0):
                for h in range(2):
                    load((c + h, d), cols(m, o, GW, 4 * h, 4 * h + 4))

            def load_rows(c, m, n, d=0):
                for q in range(n):
                    load((c + q, d), m[2 * P * q:2 * P * (q + 1), :].rearrange("(k p) n -> p k n", p=P))

            sp.dma_start(X[:, :, :], a["x"][0].rearrange("(i p) n -> p i n", p=P)).then_inc(s_x, 16)

            def lru(l, c):
                for n, g in enumerate(LRU_ORDER):
                    load_group(c + 2 * n, w_in[l], GW * g)
                load_rows(c + 10, w_out[l], 4)

            lru(0, U_LRU0)

            load_group(U_FFN, fg, 0)
            load_group(U_FFN + 2, fu, 0)
            with_down = fd.rearrange("(q k p) n -> q p k n", k=2, p=P)
            with sp.Fori(1, NG) as g:
                for h in range(2):
                    load((U_FFN + 4 + h, g - 1), fg.rearrange("(k p) n -> p k n", p=P)[:, 4 * h:4 * h + 4, bass.ds(g * GW, GW)])
                for h in range(2):
                    load((U_FFN + 6 + h, g - 1), with_down[bass.ds(g * 2 - 2 + h, 1)].rearrange("q p k n -> (q p) k n"))
                for h in range(2):
                    load((U_FFN + 8 + h, g - 1), fu.rearrange("(k p) n -> p k n", p=P)[:, 4 * h:4 * h + 4, bass.ds(g * GW, GW)])
            load_rows(U_FFN + 40, fd[6 * GW:7 * GW, :], 2)
            lru(1, U_LRU1)

            eg = a["moe_w_gate"].rearrange("a e (k p) n -> (a e) p k n", p=P)
            eu = a["moe_w_up"].rearrange("a e (k p) n -> (a e) p k n", p=P)
            ed = a["moe_w_down"].rearrange("a e (q k p) n -> (a e q) p k n", k=2, p=P)

            def job(e, j):
                def cut(m, h, o):
                    return m[bass.ds(e, 1), :, 4 * h:4 * h + 4, o].rearrange("q p k n -> (q p) k n")

                def rows(q):
                    return ed[bass.ds(q, 1)].rearrange("q p k n -> (q p) k n")
                for i, m in enumerate((eg, eu)):
                    for h in range(2):
                        load((U_MOE + 2 * i + h, j * NG), cut(m, h, slice(0, GW)))
                with sp.Fori(1, NG) as g:
                    dd = sp.snap(j * NG + g - 1)
                    for i, m in enumerate((eg, eu)):
                        for h in range(2):
                            load((U_MOE + 4 + 2 * i + h, dd), cut(m, h, bass.ds(g * GW, GW)))
                    for h in range(2):
                        load((U_MOE + 8 + h, dd), rows(e * (2 * NG) + g * 2 - 2 + h))
                for h in range(2):
                    load((U_MOE + 40 + h, j * NG), rows(e * (2 * NG) + 2 * NG - 2 + h))

            with sp.Fori(0, NE) as j:
                job(j, j)
            sp.wait_ge(sem("tab_ready"), 1)
            njobs = sp.value_load(tab[0:1, 3:4], min_val=NE, max_val=NJMAX)
            with sp.If(njobs > NE):
                with sp.Fori(NE, njobs) as j:
                    e = sp.value_load(tab[0:1, bass.ds(j - NE, 1)], min_val=0, max_val=NE - 1)
                    job(e, j)
            dn = sp.snap(njobs * NG)

            c = U_SSD
            for o in (E_XBC, E_XBC + 512):
                load_group(c, ewi, o, dn)
                c += 2
            load((c, dn), cols(ewi, E_XBC + 1024, 256, 0, 8))
            c += 1
            for o in (E_Z, E_Z + 512, E_Q, E_K, E_V, E_V + 512, E_G, E_G + 512):
                load_group(c, ewi, o, dn)
                c += 2
            load_rows(c, ewo, 8, dn)
            c += 8
            for n in range(8):
                load_group(c, owi, GW * n, dn)
                c += 2
            load_rows(c, owo, 4, dn)
            assert c + 4 == U_END

            sp.wait_ge(sem("res_ready"), 2)
            sp.dma_start(out[0].rearrange("(i p) n -> p i n", p=P), HTOK).then_inc(s_out, 16)
            sp.wait_ge(s_out, 16)

        @block.gpsimd
        def _(pool):
            steps = [0]
            s_pool = sem("pool_step")

            def link(ins):
                steps[0] += 1
                ins.then_inc(s_pool, 1)
                pool.wait_ge(s_pool, steps[0])

            link(pool.memset(ident[:, :], 0.0))
            link(pool.affine_select(out=ident[:, :], in_=ident[:, :], compare_op=ALU.not_equal, fill=1.0,
                                    base=0, pattern=[[-1, P]], channel_multiplier=1))
            link(pool.memset(ones[:, :], 1.0))
            link(pool.affine_select(out=utri[:, :], in_=ones[:, :], compare_op=ALU.is_ge, fill=0.0,
                                    base=0, pattern=[[1, P]], channel_multiplier=-1))
            link(pool.affine_select(out=ustr[:, :], in_=ones[:, :], compare_op=ALU.is_gt, fill=0.0,
                                    base=0, pattern=[[1, P]], channel_multiplier=-1))
            link(pool.memset(mhalf, -0.5))
            link(pool.iota(iot[:, :], pattern=[[1, P]], base=0, channel_multiplier=0,
                           allow_small_or_imprecise_dtypes=True))
            link(pool.memset(m01[:, :], 1.0))
            link(pool.memset(m01[:, :].rearrange("p (n c) -> p n c", c=64)[:, :, 0:1], 0.0))
            link(pool.tensor_copy(bdm[:, :], utri[:, :]))
            link(pool.affine_select(out=bdm[:, 64:128], in_=bdm[:, 64:128], compare_op=ALU.is_ge, fill=0.0,
                                    base=-64, pattern=[[0, 64]], channel_multiplier=1))
            pool.memset(tab[:, :], 0).then_inc(s_const, 1)

            def rstd(k, n, scale):
                pool.wait_ge(sem("ssq_a"), SSQ_A[k])
                pool.wait_ge(sem("ssq_v"), SSQ_V[k])
                link(pool.tensor_scalar(tpow[:, 0:n], ssq[:, 0:n], scale, EPS, ALU.mult, ALU.add))
                pool.tensor_tensor(rst[:, 0:n], tpow[:, 0:n], mhalf[:, 0:n], ALU.pow).then_inc(sem("rstd"), 1)

            SSQ_A = [1, 2, 3, 4, 5, 6, 7, 7, 8, 9]
            SSQ_V = [1, 2, 3, 4, 5, 6, 7, 8, 9, 10]
            for k in range(10):
                if k == 7:
                    rstd(k, 16, 1.0 / P)
                else:
                    rstd(k, NT, 1.0 / D)

        @block.scalar
        def _(act):
            steps = [0]
            s_act = sem("act_step")

            def link(ins):
                steps[0] += 1
                ins.then_inc(s_act, 1)
                act.wait_ge(s_act, steps[0])

            def split(u):
                c, d = u
                if c >= U_END:
                    return
                act.wait_ge(w_loaded[c % RAW], plus(16 * (c // RAW + 1), 16, d))
                if c >= SPL or not isinstance(d, int):
                    act.wait_ge(w_used, plus(c - SPL + 1, 6, d))
                act.activation(hi_of(u), raw[:, c % RAW, :], ACT.Copy).then_inc(w_hi, 1)

            def after(c, d=0, n=1):
                for i in range(n):
                    split((c + i + SPL, d))

            def par(dst, src):
                act.dma_start(dst, src).then_inc(s_par, 16)

            PR0, PR1 = A[:, 0:128], A[:, 128:256]

            def rows(t, o, src, pat):
                src = src.rearrange(pat, p=P)
                par(t[o:o + src.shape[0], :], src)

            rows(PR0, C_NMIX, a["norm_mix"], "l (c p) -> (l c) p")
            rows(PR0, C_NFFN, a["norm_ffn"], "l (c p) -> (l c) p")
            rows(PR0, C_CONV, a["conv_w"], "l k (c p) -> (l k c) p")
            rows(PR0, C_LCONV, a["lru_conv_w"], "l k (c p) -> (l k c) p")
            rows(PR0, C_LCB, a["lru_conv_b"], "l (c p) -> (l c) p")
            rows(PR0, C_BA, a["lru_ba"], "l (c p) -> (l c) p")
            rows(PR0, C_BX, a["lru_bx"], "l (c p) -> (l c) p")
            rows(PR0, C_LAM, a["lru_lambda"], "l (c p) -> (l c) p")
            rows(PR1, C_ENORM, a["even_norm_2"], "l (c p) -> (l c) p")
            rows(PR1, C_ONORM, a["odd_norm_2"], "l (c p) -> (l c) p")
            rows(PR1, C_ECONV, a["even_conv_w_2"], "l k (c p) -> (l k c) p")
            rows(PR1, C_ECB, a["even_conv_b_2"], "l (c p) -> (l c) p")
            rows(PR1, C_SSDN, a["even_ssd_norm_2"], "l (c p) -> (l c) p")
            rows(PR1, C_GB, a["even_gate_b_2"], "l (c p) -> (l c) p")
            rows(PR1, C_GLAN, a["even_gla_norm_2"], "l (c p) -> (l c) p")

            par(gbv(3072, KD, 32)[:, :, 0:16], cols(ewi, E_DT, 16, 0, 8))
            par(gbv(3072, KD, 32)[:, :, 16:32], cols(ewi, E_LR, 16, 0, 8))
            par(gb[0:16, 3328:3840], a["even_gate_w2_2"][0])
            par(gbv(2688, 16), a["even_a_log_2"][0].partition_broadcast(P))
            par(gbv(2768, 16), a["even_d_skip_2"][0].partition_broadcast(P))
            par(gbv(2928, 16), a["even_dt_bias_2"][0].partition_broadcast(P))
            par(gb[:, 2112:2176].rearrange("p (k n) -> p k n", k=8), cols(a["w_router"][0], 0, NE, 0, 8))
            act.wait_ge(sem("bd_zero"), 1)
            for l in range(2):
                for m, w in enumerate((a["lru_wa"], a["lru_wx"])):
                    for r in range(2):
                        dst = gb[64 * r:64 * r + 64, 1024 * l + 512 * m:1024 * l + 512 * (m + 1)]
                        par(dst.rearrange("p (j n) -> p j n", j=4)[:, :, 64 * r:64 * r + 64],
                            w[l].rearrange("(j r) i o -> r i j o", r=2)[r])

            for u in range(SPL):
                split((u, 0))

            act.wait_ge(sem("lam_abs"), 1)
            act.activation(sm[:, 80:88], sm[:, 72:80], ACT.Exp, scale=-1.0).then_inc(sem("lam_exp"), 1)

            def used(c, d=0):
                act.wait_ge(w_used, plus(c + 1, 6, d))

            def att_copy(c2):
                act.wait_ge(sem("a_pt"), c2 + 1)
                if c2 >= 2:
                    act.wait_ge(sem("a_o"), c2 - 1)
                act.activation(gbv(768 * (c2 % 2), 2, 384), ps[:, 0:2, 0:384], ACT.Copy).then_inc(sem("a_ptc"), 1)

            def load_gain(src):
                act.dma_start(BG, src.partition_broadcast(P)).then_inc(s_bg, 16)

            def norm_ssq(k, src):
                if k == 0:
                    act.wait_ge(s_x, 16)
                else:
                    act.wait_ge(sem("x_ready"), k)
                act.activation(A[:, 7200:8224], src, ACT.Square, accum_out=ssq[:, 0:1]).then_inc(sem("ssq_a"), 1)

            def turn(k, full, gain, hi, parts=True):
                b = TB[k]
                act.wait_ge(sem("turned"), 2 * k + 1)
                for c in range(4):
                    ins = act.activation(full[:, c, :], ps[:, b + c // 2, (c % 2) * S:(c % 2 + 1) * S],
                                         ACT.Copy, scale=gain(c))
                ins.then_inc(sem("full_a"), 1)
                if not parts:
                    return
                act.wait_ge(sem("full_a"), k + 1)
                act.activation(hi[:, 0:1024], full[:, 0:4, :], ACT.Copy).then_inc(sem("t_hi"), 1)
                act.wait_ge(sem("full_v"), k + 1)
                act.activation(hi[:, 1024:2048], full[:, 4:8, :], ACT.Copy).then_inc(sem("t_hi"), 1)

            def gcol(t, o):
                return lambda c: PT[:, t, o + c:o + c + 1]

            def lru(l, c0):
                after(c0, n=2)
                used(c0 + 1)
                for b in range(2):
                    ins = act.activation(UP[:, 2 * b:2 * b + 2, 3:259], ps[:, b, :].rearrange("p (c t) -> p c t", c=2), ACT.Copy)
                ins.then_inc(sem("lru_ev"), 1)
                after(c0 + 2, n=2)
                used(c0 + 3)
                act.activation(GG[:, :, :], ps[:, 2:4, :].rearrange("p b (c t) -> p (b c) t", c=2), ACT.Copy).then_inc(sem("lru_ev"), 1)
                after(c0 + 4, n=2)
                used(c0 + 5)
                act.activation(CO[:, :, :], ps[:, 0:2, :].rearrange("p b (c t) -> p (b c) t", c=2), ACT.Copy).then_inc(sem("lru_ev"), 1)
                act.wait_ge(sem("lru_gate"), 2 * l + 1)
                for c in range(4):
                    act.activation(RR[:, c, :], ps[:, 4 + c // 2, (c % 2) * S:(c % 2 + 1) * S], ACT.Sigmoid,
                                   bias=PT[:, 0, C_BA + 4 * l + c:C_BA + 4 * l + c + 1]).then_inc(sem("lru_r"), 1)
                act.wait_ge(sem("lru_gate"), 2 * l + 2)
                for c in range(4):
                    ins = act.activation(II[:, c, :], ps[:, 6 + c // 2, (c % 2) * S:(c % 2 + 1) * S], ACT.Sigmoid,
                                         bias=PT[:, 0, C_BX + 4 * l + c:C_BX + 4 * l + c + 1])
                ins.then_inc(sem("lru_i"), 1)
                after(c0 + 6)
                act.wait_ge(sem("lru_r"), 4 * l + 4)
                for c in range(4):
                    ins = act.activation(TT[:, c, :], RR[:, c, :], ACT.Tanh, scale=s8[:, 4 * l + c:4 * l + c + 1])
                ins.then_inc(sem("lru_th"), 1)
                act.wait_ge(sem("lru_gt"), l + 1)
                act.activation(GT[:, :, :], GT[:, :, :], ACT.Sigmoid, scale=1.5957691216057308).then_inc(sem("lru_sg"), 1)
                after(c0 + 7)
                act.wait_ge(sem("lru_th"), l + 1)
                for c in range(4):
                    ins = act.activation(RR[:, c, :], RR[:, c, :], ACT.Exp, scale=s8[:, 4 * l + c:4 * l + c + 1])
                ins.then_inc(sem("lru_a"), 1)
                after(c0 + 8, n=2)
                act.wait_ge(sem("lru_m"), l + 1)
                act.activation(TT[:, :, :], TT[:, :, :], ACT.Sqrt, scale=-1.0).then_inc(sem("lru_s"), 1)
                act.wait_ge(sem("lru_y"), l + 1)
                act.activation(ya[:, 0:2048], YF[:, :, :], ACT.Copy).then_inc(sem("lru_yhi"), 1)
                after(c0 + 10, n=4)

            norm_ssq(0, X[:, 0, :])
            turn(0, hTf, gcol(0, C_NMIX), hhi)
            lru(0, U_LRU0)
            norm_ssq(1, X[:, 0, :])
            turn(1, hTf, gcol(0, C_NFFN), hhi)

            SG, HF = ar(0, 4, S), ar(1024, 4, S)

            def silu(g):
                act.activation(SG[:, :, :], ps[:, 0:2, :].rearrange("p b (c t) -> p (b c) t", c=2), ACT.Silu).then_inc(sem("f_silu"), 1)

            def hparts(g):
                act.wait_ge(sem("f_h"), g + 1)
                act.activation(ya[:, 0:1024], HF[:, :, :], ACT.Copy).then_inc(sem("f_hi"), 1)

            after(U_FFN, n=2)
            used(U_FFN + 1)
            silu(0)
            after(U_FFN + 2, n=2)
            hparts(0)
            with act.Fori(1, NG) as g:
                dd = act.snap(g - 1)
                after(U_FFN + 4, dd, 2)
                used(U_FFN + 5, dd)
                silu(g)
                after(U_FFN + 6, dd, 4)
                hparts(g)
            after(U_FFN + 40, n=2)

            norm_ssq(2, X[:, 0, :])
            turn(2, hTf, gcol(0, C_NMIX + 8), hhi)
            lru(1, U_LRU1)
            norm_ssq(3, X[:, 0, :])
            load_gain(a["norm_ffn"][1])
            turn(3, hTf, gcol(0, C_NFFN + 8), None, parts=False)

            act.wait_ge(sem("htok"), 1)
            act.activation(hhi[:, :], HTOK.rearrange("p i n -> p (i n)"), ACT.Copy).then_inc(sem("htok_hi"), 1)
            act.wait_ge(sem("r_sub"), 1)
            act.activation(ar(256, NT, NE), ar(256, NT, NE), ACT.Exp).then_inc(sem("r_exp"), 1)
            XEh, HTh, Yh = ya[:, 0:1024], ya[:, 2048:2560], yb[:, 0:1024]
            MSG = ar(1024, 512)

            def gath_hi(k):
                act.wait_ge(sem("m_gth"), k + 1)
                act.activation(XEh, ps[:, 5:7, :].rearrange("p b n -> p (b n)"), ACT.Copy).then_inc(sem("m_xhi"), 1)

            def ht_hi(g):
                act.wait_ge(sem("m_tr"), g + 1)
                act.activation(HTh, ps[:, 4, :], ACT.Copy).then_inc(sem("m_hthi"), 1)

            act.wait_ge(sem("tab_ready"), 1)
            njobs = act.value_load(tab[0:1, 3:4], min_val=NE, max_val=NJMAX)
            gath_hi(0)
            with act.Fori(0, njobs) as j:
                dj = act.snap(j * NG)
                after(U_MOE, dj, 2)
                used(U_MOE + 1, dj)
                act.activation(MSG, ps[:, 0, :], ACT.Silu).then_inc(sem("m_silu"), 1)
                after(U_MOE + 2, dj, 2)
                with act.Fori(1, NG) as g:
                    dd = act.snap(dj + g - 1)
                    after(U_MOE + 4, dd, 2)
                    used(U_MOE + 5, dd)
                    act.wait_ge(sem("m_h"), dd + 1)
                    act.activation(MSG, ps[:, 0, :], ACT.Silu).then_inc(sem("m_silu"), 1)
                    ht_hi(dd)
                    after(U_MOE + 6, dd, 4)
                ht_hi(dj + (NG - 1))
                gath_hi(j + 1)
                after(U_MOE + 40, dj, 2)
                used(U_MOE + 41, dj)
                act.activation(Yh, ps[:, 2:4, :].rearrange("p b n -> p (b n)"), ACT.Copy).then_inc(sem("m_yhi"), 1)
            dn = act.snap(njobs * NG)

            norm_ssq(4, X[:, 0, :])
            load_gain(a["norm_final"])
            norm_ssq(5, X[:, 0, :])
            turn(4, hTf, gcol(1, C_ENORM), hhi)
            XP, CVV = ar(0, 10, 259), ar(2592, 10, S)
            Z = ar(7200, NT, D)
            c = U_SSD
            for n in range(2):
                after(c, dn, 2)
                c += 2
                used(c - 1, dn)
                act.activation(XP[:, 4 * n:4 * n + 4, 3:259], ps[:, 2 * n:2 * n + 2, :].rearrange("p b (c t) -> p (b c) t", c=2),
                               ACT.Copy).then_inc(sem("e_ev"), 1)
            after(c, dn)
            c += 1
            used(c - 1, dn)
            act.activation(XP[:, 8:10, 3:259], ps[:, 0, :].rearrange("p (c t) -> p c t", c=2), ACT.Copy).then_inc(sem("e_ev"), 1)
            for n in range(2):
                after(c, dn, 2)
                c += 2
                used(c - 1, dn)
                b = 2 if n == 0 else 0
                for i in range(NT):
                    ins = act.activation(Z[:, i, 512 * n:512 * (n + 1)], ps[:, b + i, :], ACT.Silu)
                ins.then_inc(sem("e_ev"), 1)
                if n == 0:
                    act.wait_ge(sem("d_abs"), 1)
                    act.activation(sm[:, 160:192], sm[:, 128:160], ACT.Exp, scale=-1.0).then_inc(sem("d_exp"), 1)
                    act.activation(gbv(2704, 16), gbv(2688, 16), ACT.Exp).then_inc(sem("d_exp"), 1)
            for h in range(2):
                act.wait_ge(sem("e_conv"), h + 1)
                lo, hi = ((0, 8), (8, 10))[h]
                act.activation(CVV[:, lo:hi, :], CVV[:, lo:hi, :], ACT.Silu).then_inc(sem("e_xbc"), 1)
            act.wait_ge(sem("d_acs"), 1)
            act.activation(gbv(2816, 32), gbv(2720, 32), ACT.Exp).then_inc(sem("d_ea"), 1)
            act.activation(gbv(2848, 16), gbv(2752, 16), ACT.Exp).then_inc(sem("d_ea"), 1)
            for q in range(8):
                act.wait_ge(sem("s_seg"), q + 1)
                mb = ar(9248 + 512 * (q % 2), 512)
                act.activation(mb, mb, ACT.Exp).then_inc(sem("s_exp"), 1)
            act.wait_ge(sem("x_ready"), 6)
            act.activation(ar(5152, 1024), ar(2592, 1024), ACT.Square, accum_out=ssq[:, 0:1]).then_inc(sem("ssq_a"), 1)
            Q, K = ar(0, 4, S), ar(1024, 4, S)
            after(c, dn, 2)
            c += 2
            used(c - 1, dn)
            act.activation(Q, ps[:, 2:4, :].rearrange("p b (c t) -> p (b c) t", c=2), ACT.Copy, scale=0.125).then_inc(sem("e_ev"), 1)
            after(c, dn, 2)
            c += 2
            used(c - 1, dn)
            act.activation(K, ps[:, 0:2, :].rearrange("p b (c t) -> p (b c) t", c=2), ACT.Copy).then_inc(sem("e_ev"), 1)
            act.wait_ge(sem("g_lr"), 1)
            act.activation(gb[0:16, 2048:2304], ps[0:16, 2, 0:S], ACT.Copy).then_inc(sem("g_lrc"), 1)
            turn(5, ar(7200, KD, S), gcol(1, C_SSDN), ya)
            TMP, GC, Q1, K1 = ar(2560, 4, S), ar(3584, 4, S), ar(4608, 4, S), ar(5632, 4, S)
            act.wait_ge(sem("g_abs"), 1)
            link(act.activation(TMP, TMP, ACT.Exp, scale=-1.0))
            act.activation(TMP, TMP, ACT.Ln, bias=1.0).then_inc(sem("g_ln"), 1)
            SGL = ar(8704, NT, D)
            V = gbv(0, NT, D)
            act.wait_ge(sem("g_ref"), 1)
            act.activation(Q1, TMP, ACT.Exp, scale=1.0 / 16).then_inc(sem("g_e"), 1)
            act.activation(K1, TMP, ACT.Exp, scale=-1.0 / 16).then_inc(sem("g_e"), 1)

            def v_group(c, n):
                after(c, dn, 2)
                used(c + 1, dn)
                b = 2 if n == 0 else 0
                for i in range(NT):
                    ins = act.activation(V[:, i, 512 * n:512 * (n + 1)], ps[:, b + i, :], ACT.Copy)
                ins.then_inc(sem("e_ev"), 1)

            v_group(c, 0)
            act.wait_ge(sem("g_ref"), 2)
            act.activation(TMP, TMP, ACT.Exp, scale=-1.0 / 16).then_inc(sem("g_e"), 1)
            act.activation(sm[:, 192:208].rearrange("p (a b) -> p a b", b=4),
                           GC.rearrange("p c (n t) -> p c n t", t=64)[:, :, :, 63], ACT.Exp, scale=1.0 / 16).then_inc(sem("g_e"), 1)
            act.wait_ge(sem("g_e"), 4)
            act.activation(GC, GC, ACT.Exp, scale=1.0 / 16).then_inc(sem("g_e"), 1)
            v_group(c + 2, 1)
            c += 4
            for n in range(2):
                after(c, dn, 2)
                c += 2
                used(c - 1, dn)
                b = 2 if n == 0 else 0
                if n == 0:
                    act.wait_ge(sem("t_lo"), 10)
                for i in range(NT):
                    ins = act.activation(SGL[:, i, 512 * n:512 * (n + 1)], ps[:, b + i, :], ACT.Silu)
                ins.then_inc(sem("e_ev"), 1)
            turn(6, ar(6656, KD, S), lambda c: PT[:, 1, C_GLAN:C_GLAN + 1], yb)
            after(c, dn, 8)
            c += 8

            norm_ssq(7, X[:, 0, :])
            turn(7, hTf, gcol(1, C_ONORM), hhi)
            MQ, MK, MV, MZ = ar(0, KD, S), ar(2048, KD, S), ar(4096, NT, D), ar(6144, NT, D)
            for n in range(8):
                after(c, dn, 2)
                c += 2
                used(c - 1, dn)
                b = 2 * (n % 2)
                kind, half = n // 2, n % 2
                if kind < 2:
                    ins = act.activation((MQ, MK)[kind][:, 4 * half:4 * half + 4, :],
                                         ps[:, b:b + 2, :].rearrange("p b (c t) -> p (b c) t", c=2), ACT.Copy,
                                         scale=0.125 if kind == 0 else 1.0)
                else:
                    for i in range(NT):
                        ins = act.activation((MV, MZ)[kind - 2][:, i, 512 * half:512 * (half + 1)], ps[:, b + i, :],
                                             ACT.Copy if kind == 2 else ACT.Silu)
                ins.then_inc(sem("o_ev"), 1)
            for c2 in range(8):
                PB = ar(8192 + 768 * (c2 % 2), 2, 384)
                act.wait_ge(sem("a_max"), c2 + 1)
                for r in range(2):
                    for i in range(NT):
                        v = PB[:, r, 0:128] if i == 0 else PB[:, r, 128:384]
                        k = 4 * c2 + 2 * i + r
                        ins = act.activation(v, v, ACT.Exp, bias=gbv(2048, 32)[:, k:k + 1],
                                             accum_out=gbv(2080, 32)[:, k:k + 1])
                ins.then_inc(sem("a_exp"), 1)
                if c2 >= 1:
                    att_copy(c2 - 1)
            att_copy(7)
            turn(8, MQ, lambda c: one_col, ya)
            after(c, dn, 4)
            norm_ssq(8, X[:, 0, :])
            load_gain(a["final_norm_2"])


        @block.vector
        def _(dve):
            steps = [0]
            s_dve = sem("dve_step")

            def link(ins):
                steps[0] += 1
                ins.then_inc(s_dve, 1)
                dve.wait_ge(s_dve, steps[0])

            def tt(o, x, y, op):
                return dve.tensor_tensor(o, x, y, op)

            def split(u):
                c, d = u
                if c >= U_END:
                    return
                dve.wait_ge(w_hi, plus(c + 1, 6, d))
                dve.tensor_tensor(lo_of(u), raw[:, c % RAW, :], hi_of(u).bitcast(F32), ALU.subtract).then_inc(w_lo, 1)

            def after(c, d=0, n=1):
                for i in range(n):
                    split((c + i + SPL, d))

            def used(c, d=0):
                dve.wait_ge(w_used, plus(c + 1, 6, d))

            def log1p_half(x, o, t, n):
                z, w = t[:, 0:n], t[:, 32:32 + n]
                link(dve.tensor_scalar(w, x, 2.0, None, ALU.add))
                link(dve.reciprocal(z, w))
                link(tt(z, z, x, ALU.mult))
                link(tt(w, z, z, ALU.mult))
                link(dve.tensor_scalar(o, w, 1.0 / 13, None, ALU.mult))
                for k in (11, 9, 7, 5, 3):
                    link(dve.scalar_tensor_tensor(o, o, 1.0 / k, w, ALU.add, ALU.mult))
                link(dve.scalar_tensor_tensor(o, o, 1.0, z, ALU.add, ALU.mult))

            dve.memset(gb[:, 0:2048], 0.0).then_inc(sem("bd_zero"), 1)
            dve.wait_ge(s_pt, 1)
            dve.tensor_copy(PT[:, 0, 0:R0], ps[:, 0, 0:R0])
            dve.tensor_copy(PT[:, 1, 0:R1], ps[:, 0, P:P + R1]).then_inc(s_ptc, 1)
            dve.wait_ge(s_ptc, 1)
            LAM = PT[:, 0, C_LAM:C_LAM + 8]
            dve.scalar_tensor_tensor(sm[:, 72:80], LAM, -1.0, LAM, ALU.mult, ALU.max).then_inc(sem("lam_abs"), 1)

            def ssq_of(k, src, junk):
                if k == 0:
                    dve.wait_ge(s_x, 16)
                dve.tensor_tensor_reduce(junk, src, src, 1.0, 0.0, ALU.mult, ALU.add, ssq[:, 1:2]).then_inc(sem("ssq_v"), 1)

            def normed(k, src):
                dve.wait_ge(sem("rstd"), k + 1)
                for i in range(NT):
                    dve.tensor_scalar(HTOK[:, i, :], src[:, i, :], rst[:, i:i + 1], None, ALU.mult).then_inc(sem("h_ready"), 1)

            def turn(k, full, gain, hi, lo, parts=True):
                b = TB[k]
                dve.wait_ge(sem("turned"), 2 * k + 2)
                for c in range(4, 8):
                    ins = dve.tensor_scalar(full[:, c, :], ps[:, b + c // 2, (c % 2) * S:(c % 2 + 1) * S],
                                            gain(c), None, ALU.mult)
                ins.then_inc(sem("full_v"), 1)
                if not parts:
                    return
                dve.wait_ge(sem("full_v"), k + 1)
                n = 2 * (k - (k > 3))
                for h in range(2):
                    dve.wait_ge(sem("t_hi"), n + h + 1)
                    tt(lo[:, 1024 * h:1024 * (h + 1)], full[:, 4 * h:4 * h + 4, :].rearrange("p c t -> p (c t)"),
                       hi[:, 1024 * h:1024 * (h + 1)].bitcast(F32), ALU.subtract).then_inc(sem("t_lo"), 1)

            def gcol(t, o):
                return lambda c: PT[:, t, o + c:o + c + 1]

            def residual():
                for i in range(NT):
                    for h in range(2):
                        ins = tt(X[:, i, 512 * h:512 * (h + 1)], X[:, i, 512 * h:512 * (h + 1)], ps[:, 4 + 2 * i + h, :], ALU.add)
                ins.then_inc(sem("x_ready"), 1)
                xr[0] += 1
                dve.wait_ge(sem("x_ready"), xr[0])

            xr = [0]

            def col(t, o):
                return PT[:, t, o:o + 1]

            def bank2(b):
                return ps[:, b:b + 2, :].rearrange("p b (c t) -> p (b c) t", c=2)

            def lru(l, c0):
                dve.memset(UP[:, :, 0:3], 0.0)
                link(dve.memset(CV[:, :, 0:2], 0.0))
                after(c0, n=2)
                dve.wait_ge(sem("lru_ev"), 3 * l + 1)
                w = C_LCONV + 16 * l
                for c in range(4):
                    ins = dve.tensor_scalar(UC[:, c, :], UP[:, c, 0:S], col(0, w + c), col(0, C_LCB + 4 * l + c), ALU.mult, ALU.add)
                link(ins)
                for k in range(1, 4):
                    for c in range(4):
                        ins = dve.scalar_tensor_tensor(UC[:, c, :], UP[:, c, k:k + S], col(0, w + 4 * k + c), UC[:, c, :], ALU.mult, ALU.add)
                    if k < 3:
                        link(ins)
                ins.then_inc(sem("lru_uc"), 1)
                dve.wait_ge(sem("lru_uc"), l + 1)
                after(c0 + 2, n=2)
                dve.wait_ge(sem("lru_ev"), 3 * l + 2)
                link(tt(GT, GG, GG, ALU.mult))
                link(dve.tensor_scalar(GT, GT, 0.044715, 1.0, ALU.mult, ALU.add))
                tt(GT, GT, GG, ALU.mult).then_inc(sem("lru_gt"), 1)
                after(c0 + 4, n=2)
                after(c0 + 6)
                used(c0 + 7)
                dve.wait_ge(sem("lru_ev"), 3 * l + 3)
                tt(CV[:, :, 2:258], CO, bank2(2), ALU.mult).then_inc(sem("lru_v"), 1)
                dve.wait_ge(sem("lru_v"), 2 * l + 1)
                after(c0 + 7)
                w = C_CONV + 12 * l
                for c in range(4):
                    ins = dve.tensor_scalar(CO[:, c, :], CV[:, c, 0:S], col(0, w + c), None, ALU.mult)
                link(ins)
                for k in range(1, 3):
                    for c in range(4):
                        ins = dve.scalar_tensor_tensor(CO[:, c, :], CV[:, c, k:k + S], col(0, w + 4 * k + c), CO[:, c, :], ALU.mult, ALU.add)
                    link(ins)
                dve.wait_ge(sem("lru_sg"), l + 1)
                link(tt(GG, GG, GT, ALU.mult))
                dve.wait_ge(sem("lru_a"), l + 1)
                link(tt(GT, RR, RR, ALU.mult))
                dve.scalar_tensor_tensor(TT, GT, 1.0, TT, ALU.add, ALU.mult).then_inc(sem("lru_m"), 1)
                dve.wait_ge(sem("lru_i"), l + 1)
                link(tt(II, II, UC, ALU.mult))
                after(c0 + 8, n=2)
                used(c0 + 9)
                tt(YF[:, 0:4, :], CO, bank2(0), ALU.mult).then_inc(sem("lru_v"), 1)
                dve.wait_ge(sem("lru_s"), l + 1)
                link(tt(TT, TT, II, ALU.mult))
                for c in range(4):
                    ins = dve.tensor_tensor_scan(UC[:, c, :], RR[:, c, :], TT[:, c, :], 0.0, ALU.mult, ALU.add)
                link(ins)
                tt(YF[:, 4:8, :], UC, GG, ALU.mult).then_inc(sem("lru_y"), 1)
                dve.wait_ge(sem("lru_yhi"), l + 1)
                tt(ya[:, 2048:4096], YF.rearrange("p c t -> p (c t)"), ya[:, 0:2048].bitcast(F32), ALU.subtract).then_inc(sem("lru_ylo"), 1)
                after(c0 + 10, n=4)
                used(c0 + 13)
                residual()

            for u in range(SPL):
                split((u, 0))
            dve.wait_ge(sem("lam_exp"), 1)
            TS1 = gb[:, 3840:3904]
            log1p_half(sm[:, 80:88], sm[:, 88:96], TS1, 8)
            link(dve.tensor_scalar(sm[:, 96:104], LAM, -1.0, 0.0, ALU.mult, ALU.max))
            link(dve.scalar_tensor_tensor(sm[:, 88:96], sm[:, 88:96], 2.0, sm[:, 96:104], ALU.mult, ALU.add))
            dve.tensor_scalar(s8, sm[:, 88:96], -8.0, None, ALU.mult).then_inc(sem("s8"), 1)

            ssq_of(0, X[:, 1, :], HTOK[:, 1, :])
            normed(0, X)
            turn(0, hTf, gcol(0, C_NMIX), hhi, hlo)
            lru(0, U_LRU0)
            ssq_of(1, X[:, 1, :], HTOK[:, 1, :])
            normed(1, X)
            turn(1, hTf, gcol(0, C_NFFN), hhi, hlo)

            SG, HF = ar(0, 4, S), ar(1024, 4, S)

            def hidden(g):
                dve.wait_ge(sem("f_silu"), g + 1)
                tt(HF, SG, bank2(2), ALU.mult).then_inc(sem("f_h"), 1)
                dve.wait_ge(sem("f_hi"), g + 1)
                tt(ya[:, 1024:2048], HF.rearrange("p c t -> p (c t)"), ya[:, 0:1024].bitcast(F32), ALU.subtract).then_inc(sem("f_lo"), 1)

            after(U_FFN, n=4)
            used(U_FFN + 3)
            hidden(0)
            with dve.Fori(1, NG) as g:
                dd = dve.snap(g - 1)
                after(U_FFN + 4, dd, 6)
                used(U_FFN + 9, dd)
                hidden(g)
            after(U_FFN + 40, n=2)
            used(U_FFN + 41)
            residual()

            ssq_of(2, X[:, 1, :], HTOK[:, 1, :])
            normed(2, X)
            turn(2, hTf, gcol(0, C_NMIX + 8), hhi, hlo)
            lru(1, U_LRU1)
            ssq_of(3, X[:, 1, :], HTOK[:, 1, :])
            normed(3, X)
            turn(3, hTf, gcol(0, C_NFFN + 8), None, None, parts=False)
            dve.wait_ge(s_bg, 16)
            for i in range(NT):
                ins = tt(HTOK[:, i, :], HTOK[:, i, :], BG, ALU.mult)
            ins.then_inc(sem("htok"), 1)

            L, EX = ar(0, NT, NE), ar(256, NT, NE)
            GT3, EQ3 = ar(512, NT, NE * NE), ar(640, NT, NE * NE)
            LTM = ar(768, NE * NE)
            CH, MX, SMX = ar(832, NT, NE), ar(848, NT), ar(852, NT)
            CNT, OV, OVR, SEL = ar(860, NE), ar(868, NE), ar(876, NE), ar(884, NE)
            T16, T8 = ar(900, NT, NE), ar(920, NE)
            POS, COMB = ar(2048, NT, 12), ar(2080, NT, 12)
            JP, JC = ar(2112, NT), ar(2116, NT)
            TF = ar(2120, 4)

            def e3(x):
                return x.rearrange("p i (e f) -> p i e f", e=NE)

            for e in range(NE):
                if e:
                    dve.memset(LTM[:, NE * e:NE * e + e], 1.0)
                ins = dve.memset(LTM[:, NE * e + e:NE * e + NE], 0.0)
            link(ins)
            dve.wait_ge(sem("r_log"), 1)
            link(dve.tensor_copy(L, ps[:, 4, 0:16].rearrange("p (i e) -> p i e", i=NT)))
            other = L.unsqueeze(2).to_broadcast([P, NT, NE, NE])
            own = L.unsqueeze(3).to_broadcast([P, NT, NE, NE])
            link(tt(e3(GT3), other, own, ALU.is_gt))
            link(tt(e3(EQ3), other, own, ALU.is_equal))
            link(tt(EQ3, EQ3, LTM.unsqueeze(1).to_broadcast([P, NT, NE * NE]), ALU.mult))
            link(tt(GT3, GT3, EQ3, ALU.add))
            link(dve.tensor_reduce(T16, e3(GT3), AX_X, ALU.add))
            dve.tensor_scalar(CH, T16, 2.0, None, ALU.is_lt).then_inc(sem("r_ch"), 1)
            link(dve.tensor_reduce(MX, L, AX_X, ALU.max))
            tt(EX, L, MX.unsqueeze(2).to_broadcast([P, NT, NE]), ALU.subtract).then_inc(sem("r_sub"), 1)
            dve.wait_ge(sem("r_ch"), 1)
            dve.wait_ge(sem("r_exp"), 1)
            link(tt(EX, EX, CH, ALU.mult))
            link(dve.tensor_reduce(SMX, EX, AX_X, ALU.add))
            link(dve.reciprocal(MX, SMX))
            link(tt(COMB[:, :, 0:NE], EX, MX.unsqueeze(2).to_broadcast([P, NT, NE]), ALU.mult))
            dve.wait_ge(sem("r_pos"), 1)
            R = ps[:, 5, 0:24].rearrange("p (i e) -> p i e", i=3)
            link(dve.tensor_copy(CNT, R[:, 2, :]))
            link(dve.scalar_tensor_tensor(T16, R[:, 0:2, :], 1.0, CH, ALU.add, ALU.mult))
            link(dve.tensor_scalar(POS[:, :, 0:NE], T16, -1.0, None, ALU.add))
            link(dve.tensor_scalar(OV, CNT, float(P), None, ALU.is_gt))
            link(tt(e3(GT3)[:, 0, :, :], OV.unsqueeze(1).to_broadcast([P, NE, NE]), LTM.rearrange("p (e f) -> p e f", e=NE), ALU.mult))
            link(dve.tensor_reduce(OVR, e3(GT3)[:, 0, :, :], AX_X, ALU.add))
            for m in range(3):
                link(dve.tensor_scalar(SEL, OVR, float(m), None, ALU.is_equal))
                link(tt(SEL, SEL, OV, ALU.mult))
                sel2 = SEL.unsqueeze(1).to_broadcast([P, NT, NE])
                link(tt(EX, T16, sel2, ALU.mult))
                link(dve.tensor_reduce(MX, EX, AX_X, ALU.add))
                link(dve.tensor_scalar(POS[:, :, NE + m], MX, -1.0 - P, None, ALU.add))
                link(tt(EX, COMB[:, :, 0:NE], sel2, ALU.mult))
                link(dve.tensor_reduce(COMB[:, :, NE + m], EX, AX_X, ALU.add))
                link(tt(T8, SEL, iot[:, 0:NE], ALU.mult))
                link(dve.tensor_reduce(TF[:, m:m + 1], T8, AX_X, ALU.add))
            link(dve.memset(POS[:, :, 11:12], -1.0))
            link(dve.tensor_reduce(TF[:, 3:4], OV, AX_X, ALU.add))
            link(dve.tensor_scalar(TF[:, 3:4], TF[:, 3:4], float(NE), None, ALU.add))
            dve.wait_ge(s_const, 1)
            dve.tensor_copy(tab[:, :], TF).then_inc(sem("tab_ready"), 1)
            dve.wait_ge(sem("tab_ready"), 1)

            dve.wait_ge(sem("htok_hi"), 1)
            tt(hlo[:, :], HTOK.rearrange("p i n -> p (i n)"), hhi[:, :].bitcast(F32), ALU.subtract).then_inc(sem("htok_lo"), 1)

            XEh, XEl = ya[:, 0:1024], ya[:, 1024:2048]
            HTh, HTl = ya[:, 2048:2560], ya[:, 2560:3072]
            SR = ya[:, 3072:3328].rearrange("p (i s) -> p i s", i=NT)
            ST = ya[:, 3328:3584]
            Yh, Yl = yb[:, 0:1024], yb[:, 1024:2048]
            MSG, MHF = ar(1024, 512), ar(1536, 512)
            njobs = dve.value_load(tab[0:1, 3:4], min_val=NE, max_val=NJMAX)

            def onehot(j):
                c0 = m_chain[0]
                dve.tensor_copy(JP, POS[:, :, bass.ds(j, 1)].rearrange("p i o -> p (i o)")).then_inc(sem("m_jp"), 1)
                dve.wait_ge(sem("m_jp"), j + 1)
                for i in range(NT):
                    ins = dve.tensor_scalar(SR[:, i, :], iot[:, :], JP[:, i:i + 1], None, ALU.is_equal)
                ins.then_inc(sem("m_s"), 1)

            m_chain = [0]

            def gath_lo(k):
                dve.wait_ge(sem("m_xhi"), k + 1)
                tt(XEl, ps[:, 5:7, :].rearrange("p b n -> p (b n)"), XEh.bitcast(F32), ALU.subtract).then_inc(sem("m_xlo"), 1)

            def ht_lo(g):
                dve.wait_ge(sem("m_hthi"), g + 1)
                tt(HTl, ps[:, 4, :], HTh.bitcast(F32), ALU.subtract).then_inc(sem("m_htlo"), 1)

            def hid(g):
                dve.wait_ge(sem("m_silu"), g + 1)
                tt(MHF, MSG, ps[:, 1, :], ALU.mult).then_inc(sem("m_h"), 1)

            def scatter(k):
                dve.wait_ge(sem("m_sct"), k + 1)
                for i in range(NT):
                    for h in range(2):
                        ins = dve.scalar_tensor_tensor(X[:, i, 512 * h:512 * (h + 1)], ps[:, 4 + 2 * i + h, :], JC[:, i:i + 1],
                                                       X[:, i, 512 * h:512 * (h + 1)], ALU.mult, ALU.add)
                ins.then_inc(sem("m_sev"), 1)

            dve.memset(Yh.bitcast(F32), 0.0)
            dve.memset(Yl.bitcast(F32), 0.0)
            dve.memset(JC, 0.0)
            dve.memset(ST.bitcast(F32), 0.0).then_inc(sem("m_st"), 1)
            dve.memset(ar(2120, 1), 0.0).then_inc(sem("m_ylo"), 1)
            onehot(0)
            gath_lo(0)
            with dve.Fori(0, njobs) as j:
                dj = dve.snap(j * NG)
                after(U_MOE, dj, 4)
                used(U_MOE + 3, dj)
                hid(dj)
                scatter(j)
                dve.wait_ge(sem("m_sev"), j + 1)
                dve.tensor_copy(JC, COMB[:, :, bass.ds(j, 1)].rearrange("p i o -> p (i o)"))
                with dve.Fori(1, NG) as g:
                    dd = dve.snap(dj + g - 1)
                    after(U_MOE + 4, dd, 2)
                    ht_lo(dd)
                    after(U_MOE + 6, dd, 2)
                    used(U_MOE + 7, dd)
                    hid(dd + 1)
                    after(U_MOE + 8, dd, 2)
                dve.wait_ge(sem("m_str"), j + 1)
                dve.tensor_copy(ST, ps[:, 7, 0:256]).then_inc(sem("m_st"), 1)
                onehot(j + 1)
                ht_lo(dj + (NG - 1))
                gath_lo(j + 1)
                after(U_MOE + 40, dj, 2)
                dve.wait_ge(sem("m_yhi"), j + 1)
                tt(Yl, ps[:, 2:4, :].rearrange("p b n -> p (b n)"), Yh.bitcast(F32), ALU.subtract).then_inc(sem("m_ylo"), 1)
            scatter(njobs)
            dve.wait_ge(sem("m_sev"), njobs + 1)
            dn = dve.snap(njobs * NG)
            dve.memset(ar(2124, 1), 0.0).then_inc(sem("x_ready"), 1)
            xr[0] += 1
            dve.wait_ge(sem("x_ready"), xr[0])

            ssq_of(4, X[:, 1, :], HTOK[:, 1, :])
            dve.wait_ge(sem("rstd"), 5)
            dve.wait_ge(s_bg, 32)
            for i in range(NT):
                ins = dve.scalar_tensor_tensor(X[:, i, :], X[:, i, :], rst[:, i:i + 1], BG, ALU.mult, ALU.mult)
            ins.then_inc(sem("x_ready"), 1)
            xr[0] += 1
            dve.wait_ge(sem("x_ready"), xr[0])

            ssq_of(5, X[:, 1, :], HTOK[:, 1, :])
            XP, CVV = ar(0, 10, 259), ar(2592, 10, S)
            link(dve.memset(XP[:, :, 0:3], 0.0))
            normed(5, X)
            turn(4, hTf, gcol(1, C_ENORM), hhi, hlo)
            c = U_SSD

            def conv(lo, hi):
                for q in range(lo, hi):
                    ins = dve.tensor_scalar(CVV[:, q, :], XP[:, q, 0:S], col(1, C_ECONV + q), col(1, C_ECB + q), ALU.mult, ALU.add)
                link(ins)
                for k in range(1, 4):
                    for q in range(lo, hi):
                        ins = dve.scalar_tensor_tensor(CVV[:, q, :], XP[:, q, k:k + S], col(1, C_ECONV + 10 * k + q),
                                                       CVV[:, q, :], ALU.mult, ALU.add)
                    if k < 3:
                        link(ins)
                return ins

            after(c, dn, 2)
            dve.wait_ge(sem("e_ev"), 1)
            link(conv(0, 4))
            after(c + 2, dn, 2)
            dve.wait_ge(sem("e_ev"), 2)
            conv(4, 8).then_inc(sem("e_conv"), 1)
            after(c + 4, dn, 1)
            DX, DTT, DTA = gbv(2944, NT, 16), gbv(2864, NT, 16), gbv(2896, NT, 16)
            ACS, DEC, EA = gbv(2720, 32), gbv(2752, 16), gbv(2816, 32)
            dve.wait_ge(sem("d_ps"), 1)
            link(tt(DX, ps[:, 4, 0:32].rearrange("p (i h) -> p i h", i=NT), gbv(2928, 16).unsqueeze(1).to_broadcast([P, NT, 16]), ALU.add))
            dve.scalar_tensor_tensor(sm[:, 128:160], gbv(2944, 32), -1.0, gbv(2944, 32), ALU.mult, ALU.max).then_inc(sem("d_abs"), 1)
            dve.wait_ge(sem("e_ev"), 3)
            conv(8, 10).then_inc(sem("e_conv"), 1)
            after(c + 5, dn, 2)
            dve.wait_ge(sem("d_exp"), 1)
            log1p_half(sm[:, 160:192], sm[:, 208:240], TS1, 32)
            link(dve.tensor_scalar(gbv(2944, 32), gbv(2944, 32), 0.0, None, ALU.max))
            link(dve.scalar_tensor_tensor(gbv(2864, 32), sm[:, 208:240], 2.0, gbv(2944, 32), ALU.mult, ALU.add))
            dve.wait_ge(sem("d_exp"), 2)
            dve.scalar_tensor_tensor(DTA, DTT, -1.0, gbv(2704, 16).unsqueeze(1).to_broadcast([P, NT, 16]), ALU.mult, ALU.mult).then_inc(sem("d_dta"), 1)
            after(c + 7, dn, 2)
            dve.wait_ge(sem("d_cum"), 1)
            link(dve.tensor_copy(ACS, ps[:, 5, 0:32]))
            tt(DEC, ps[:, 5, 32:48], ACS[:, 0:16], ALU.subtract).then_inc(sem("d_acs"), 1)
            XS, XDT, XDD = ar(5152, NT, D), ar(0, NT, D), ar(9248, D)

            def heads(x, n=32):
                return x.rearrange("p (h d) -> p h d", h=n)

            def per_head(x, n=32, d=64):
                return x.unsqueeze(2).to_broadcast([P, n, d])

            dve.wait_ge(sem("s_xtr"), 1)
            dve.tensor_copy(ar(5152, 2048), ps[:, 4:8, :].rearrange("p b n -> p (b n)")).then_inc(sem("s_xs"), 1)
            dve.wait_ge(sem("s_xs"), 1)
            link(tt(heads(ar(0, 2048)), heads(ar(5152, 2048)), per_head(gbv(2864, 32)), ALU.mult))
            dve.wait_ge(sem("d_ea"), 2)
            tt(heads(XDD, 16), heads(ar(0, 1024), 16), per_head(gbv(2848, 16), 16), ALU.mult).then_inc(sem("s_xdd"), 1)
            dve.wait_ge(sem("s_cbt"), 1)
            CBM = gb[:, 0:512].rearrange("p (i g t) -> p i g t", i=2, g=2)
            for gr in range(2):
                tt(CBM[:, :, gr, :], ps[:, 4 + gr, 0:256].rearrange("p (i t) -> p i t", i=2),
                   utri[:, :].unsqueeze(1).to_broadcast([P, 2, P]), ALU.mult)
            dve.tensor_copy(gbv(512, 128), ps[:, 6, 0:128]).then_inc(sem("s_cb"), 1)
            dve.wait_ge(sem("s_stp"), 1)
            dve.tensor_copy(gb[0:64, 640:1152], ps[0:64, 6, :])
            dve.tensor_copy(gb[64:128, 640:1152], ps[64:128, 7, :]).then_inc(sem("s_st"), 1)
            Y = ar(2592, NT, D)
            Z = ar(7200, NT, D)

            def mask_mul(q):
                dve.wait_ge(sem("s_exp"), q + 1)
                mb = ar(9248 + 512 * (q % 2), 4, P)
                tt(mb, mb, CBM[:, q // 4, (q % 4) // 2, :].unsqueeze(1).to_broadcast([P, 4, P]), ALU.mult).then_inc(sem("s_m"), 1)

            def y_out(i):
                dve.wait_ge(sem("s_yq"), 4 * i + 4)
                yi = ar(2592 + 1024 * i, D)
                tt(yi, yi, ps[:, 6:8, :].rearrange("p b n -> p (b n)"), ALU.add).then_inc(sem("s_ye"), 1)

            dve.wait_ge(sem("s_cb"), 1)
            dve.wait_ge(sem("s_st"), 1)
            for q in range(8):
                i = q // 4
                dve.wait_ge(sem("s_segp"), q + 1)
                if q >= 2:
                    dve.wait_ge(sem("s_yq"), q - 1)
                for h in range(4):
                    hh = 16 * i + 4 * (q % 4) + h
                    ins = dve.tensor_scalar(ar(9248 + 512 * (q % 2) + P * h, P), ps[:, 4 + q % 2, P * h:P * (h + 1)],
                                            ACS[:, hh:hh + 1], 0.0, ALU.subtract, ALU.min)
                ins.then_inc(sem("s_seg"), 1)
                if q >= 1:
                    mask_mul(q - 1)
                if q == 1:
                    for t in range(NT):
                        ins = tt(heads(ar(2592 + 1024 * t, D), 16), heads(ar(5152 + 1024 * t, D), 16), per_head(gbv(2768, 16), 16), ALU.mult)
                    link(ins)
                if q == 5:
                    y_out(0)
            mask_mul(7)
            y_out(1)
            dve.wait_ge(sem("s_yoff"), 1)
            dve.wait_ge(sem("s_ye"), 2)
            link(tt(heads(ar(5152, D), 16), ps[:, 4:6, :].rearrange("p b (h d) -> p (b h) d", d=64), per_head(EA[:, 16:32], 16), ALU.mult))
            link(tt(Y[:, 1, :], Y[:, 1, :], ar(5152, D), ALU.add))
            dve.wait_ge(sem("e_ev"), 5)
            tt(ar(2592, 2048), ar(2592, 2048), ar(7200, 2048), ALU.mult).then_inc(sem("x_ready"), 1)
            xr[0] += 1
            dve.wait_ge(sem("x_ready"), xr[0])
            ssq_of(6, Y[:, 1, :], ar(6176, D))
            normed(6, Y)
            after(c + 9, dn, 4)
            c += 13
            turn(5, ar(7200, KD, S), gcol(1, C_SSDN), ya[:, 0:2048], ya[:, 2048:4096])

            Q, K = ar(0, 4, S), ar(1024, 4, S)
            TMP, GC, Q1, K1 = ar(2560, 4, S), ar(3584, 4, S), ar(4608, 4, S), ar(5632, 4, S)
            Q4 = ar(6656, 2048)
            SCT = gb[:, 2048:3072]
            S1 = [None, gb[:, 3072:3584], gb[:, 3584:4096], ar(2048, 512)]
            dve.wait_ge(sem("g_x"), 1)
            for q in range(4):
                ins = dve.tensor_scalar(GC[:, q, :], ps[:, 4 + q // 2, (q % 2) * S:(q % 2 + 1) * S], col(1, C_GB + q), None, ALU.add)
            link(ins)
            dve.scalar_tensor_tensor(TMP, GC, -1.0, GC, ALU.mult, ALU.max).then_inc(sem("g_abs"), 1)
            dve.memset(Q4, 0.0)
            dve.memset(SCT, 0.0)
            dve.wait_ge(sem("g_ln"), 1)
            link(dve.scalar_tensor_tensor(TMP, GC, 0.0, TMP, ALU.min, ALU.subtract))
            for q in range(4):
                ins = dve.tensor_tensor_scan(GC[:, q, :], m01[:, :], TMP[:, q, :], 0.0, ALU.mult, ALU.add)
            link(ins)

            def ch(x):
                return x.rearrange("p c (n t) -> p (c n) t", t=64)

            tt(ch(TMP), ch(GC), ch(GC)[:, :, 32:33].to_broadcast([P, 16, 64]), ALU.subtract).then_inc(sem("g_ref"), 1)
            after(c, dn, 2)
            dve.wait_ge(sem("e_ev"), 7)
            dve.wait_ge(sem("g_e"), 2)
            tt(Q1, Q1, Q, ALU.mult)
            tt(K1, K1, K, ALU.mult)
            tt(ch(TMP), ch(GC), ch(GC)[:, :, 63:64].to_broadcast([P, 16, 64]), ALU.subtract).then_inc(sem("g_ref"), 1)
            after(c + 2, dn, 2)
            dve.wait_ge(sem("g_e"), 5)
            tt(K, K, TMP, ALU.mult).then_inc(sem("g_k2"), 1)
            qv = Q.rearrange("p c (i r t) -> p (c i) r t", i=2, r=2)
            gv = GC.rearrange("p c (i r t) -> p (c i) r t", i=2, r=2)
            Q5 = Q4.rearrange("p (ci r t) -> p ci r t", r=2, t=P)
            for r in range(2):
                ins = tt(Q5[:, :, r, 64 * r:64 * r + 64], qv[:, :, r, :], gv[:, :, r, :], ALU.mult)
            ins.then_inc(sem("g_q"), 1)
            after(c + 4, dn, 4)
            c += 8
            dve.wait_ge(sem("g_q"), 1)
            dve.wait_ge(sem("g_k2p"), 1)
            dve.tensor_copy(ar(3584, 1024), ps[:, 4:6, :].rearrange("p b n -> p (b n)")).then_inc(sem("g_k2t"), 1)
            bd4 = bdm[:, :].unsqueeze(1).to_broadcast([P, 4, P])

            def scores(i):
                dve.wait_ge(sem("g_sc"), i + 1)
                if i:
                    dve.wait_ge(sem("g_o"), i)
                for r in range(2):
                    ins = dve.copy_predicated(SCT[:, 512 * r:512 * (r + 1)].rearrange("p (c t) -> p c t", c=4), bd4,
                                              ps[:, 6 + r, :].rearrange("p (c t) -> p c t", c=4))
                ins.then_inc(sem("g_sct"), 1)

            def state(n):
                dve.wait_ge(sem("g_kv"), n)
                kv = ps[:, 0:2, :].rearrange("p b (c v) -> p (b c) v", c=2)
                new = S1[n].rearrange("p (c v) -> p c v", c=4)
                for r in range(2):
                    pr = slice(64 * r, 64 * r + 64)
                    if n == 1:
                        ins = dve.tensor_copy(new[pr], kv[pr, :, P * r:P * (r + 1)])
                    else:
                        old = S1[n - 1].rearrange("p (c v) -> p c v", c=4)
                        for q in range(4):
                            k = 192 + 4 * q + n - 1
                            ins = dve.scalar_tensor_tensor(new[pr, q, :], old[pr, q, :], sm[pr, k:k + 1],
                                                           kv[pr, q, P * r:P * (r + 1)], ALU.mult, ALU.add)
                ins.then_inc(sem("g_s"), 1)
                dve.wait_ge(sem("g_s"), n)

            def o_out(i):
                dve.wait_ge(sem("g_o"), i + 1)
                dve.tensor_copy(ar(1024 * i, 4, 2, P), ps[:, 2:4, :].rearrange("p r (c v) -> p c r v", c=4)).then_inc(sem("g_oe"), 1)

            scores(0)
            state(1)
            o_out(0)
            state(2)
            scores(1)
            state(3)
            o_out(1)
            dve.wait_ge(sem("g_oe"), 2)
            O = ar(0, 2048)
            link(tt(ar(4608, 2048), O, O, ALU.mult))
            dve.tensor_reduce(ssq[:, 0:16], ar(4608, 16, P), AX_X, ALU.add).then_inc(sem("ssq_v"), 1)
            dve.wait_ge(sem("rstd"), 8)
            link(tt(heads(O, 16), heads(O, 16), per_head(rst, 16, P), ALU.mult))
            dve.wait_ge(sem("e_ev"), 11)
            for i in range(NT):
                tt(ar(1024 * i, D), ar(1024 * i, D), ar(8704 + 1024 * i, D), ALU.mult).then_inc(sem("h_ready"), 1)
            turn(6, ar(6656, KD, S), lambda c: PT[:, 1, C_GLAN:C_GLAN + 1], yb[:, 0:2048], yb[:, 2048:4096])
            after(c, dn, 8)
            c += 8
            used(c - 1, dn)
            residual()

            ssq_of(8, X[:, 1, :], HTOK[:, 1, :])
            normed(8, X)
            turn(7, hTf, gcol(1, C_ONORM), hhi, hlo)
            after(c, dn, 16)
            c += 16
            M3, NM, RS = gb[:, 1600:1984], gb[:, 2048:2080], gb[:, 2080:2112]
            link(dve.memset(M3, 0.0))
            dve.tensor_scalar(M3[:, 0:P], ustr[:, :], -1e30, None, ALU.mult)
            link(dve.tensor_scalar(M3[:, 256:384], ustr[:, :], -1e30, None, ALU.mult))
            OT = hTf[:, :, :].rearrange("p c t -> p (c t)").rearrange("p (i n) -> p i n", i=NT)

            def o_norm(c2):
                dve.wait_ge(sem("a_o"), c2 + 1)
                link(dve.reciprocal(RS[:, 4 * c2:4 * c2 + 4], RS[:, 4 * c2:4 * c2 + 4]))
                tt(OT[:, :, P * c2:P * (c2 + 1)].rearrange("p i (r d) -> p i r d", r=2),
                   ps[:, 2 + c2 % 2, 0:256].rearrange("p (i r d) -> p i r d", i=2, r=2),
                   RS[:, 4 * c2:4 * c2 + 4].rearrange("p (i r) -> p i r", i=2).unsqueeze(3).to_broadcast([P, 2, 2, 64]),
                   ALU.mult).then_inc(sem("a_oe"), 1)

            for c2 in range(8):
                PB = ar(8192 + 768 * (c2 % 2), 2, 384)
                dve.wait_ge(sem("a_sc"), c2 + 1)
                if c2 >= 2:
                    dve.wait_ge(sem("a_pt"), c2 - 1)
                b = 4 + 2 * (c2 % 2)
                tt(PB, ps[:, b:b + 2, 0:384], M3.unsqueeze(1).to_broadcast([P, 2, 384]), ALU.add).then_inc(sem("a_sm"), 1)
                dve.wait_ge(sem("a_sm"), c2 + 1)
                dve.tensor_reduce(NM[:, 4 * c2:4 * c2 + 2], PB[:, :, 0:P], AX_X, ALU.max)
                link(dve.tensor_reduce(NM[:, 4 * c2 + 2:4 * c2 + 4], PB[:, :, P:384], AX_X, ALU.max))
                dve.tensor_scalar(NM[:, 4 * c2:4 * c2 + 4], NM[:, 4 * c2:4 * c2 + 4], -1.0, None, ALU.mult).then_inc(sem("a_max"), 1)
                if c2 >= 2:
                    o_norm(c2 - 2)
            o_norm(6)
            o_norm(7)
            dve.wait_ge(sem("a_oe"), 8)
            dve.wait_ge(sem("o_ev"), 8)
            MZ = ar(6144, NT, D)
            for i in range(NT):
                tt(OT[:, i, :], OT[:, i, :], MZ[:, i, :], ALU.mult).then_inc(sem("h_ready"), 1)
            turn(8, ar(0, KD, S), lambda c: one_col, ya[:, 0:2048], ya[:, 2048:4096])
            after(c, dn, 4)
            c += 4
            used(c - 1, dn)
            residual()
            ssq_of(9, X[:, 1, :], HTOK[:, 1, :])
            dve.wait_ge(sem("rstd"), 10)
            dve.wait_ge(s_bg, 48)
            for i in range(NT):
                dve.scalar_tensor_tensor(HTOK[:, i, :], X[:, i, :], rst[:, i:i + 1], BG, ALU.mult, ALU.mult).then_inc(sem("res_ready"), 1)

        @block.tensor
        def _(pe):
            def lo_ready(u):
                pe.wait_ge(w_lo, plus(u[0] + 1, 6, u[1]))

            def three(o, xh, xl, wh, wl, first, last, weights_stationary):
                if weights_stationary:
                    seq = ((wh, xh), (wh, xl), (wl, xh))
                else:
                    seq = ((xh, wh), (xh, wl), (xl, wh))
                for n, (s, m) in enumerate(seq):
                    ins = pe.matmul(o, s, m, start=first and n == 0, stop=last and n == 2, skip_group_check=True)
                return ins

            XH = hhi[:, :].rearrange("p (k t) -> p k t", k=KD)
            XL = hlo[:, :].rearrange("p (k t) -> p k t", k=KD)

            def group_f(c, bank, d=0):
                for h in range(2):
                    u = (c + h, d)
                    lo_ready(u)
                    wh, wl = (x.rearrange("p (k n) -> p k n", k=4) for x in (hi_of(u), lo_of(u)))
                    for k in range(4):
                        for q in range(4):
                            ins = three(ps[:, bank + q // 2, (q % 2) * S:(q % 2 + 1) * S], XH[:, 4 * h + k, :], XL[:, 4 * h + k, :],
                                        wh[:, k, P * q:P * (q + 1)], wl[:, k, P * q:P * (q + 1)],
                                        h == 0 and k == 0 and q % 2 == 0, h == 1 and k == 3, True)
                    ins.then_inc(w_used, 1)

            def group_t(c, bank, d=0):
                for h in range(2):
                    u = (c + h, d)
                    lo_ready(u)
                    wh, wl = (x.rearrange("p (k n) -> p k n", k=4) for x in (hi_of(u), lo_of(u)))
                    for k in range(4):
                        for i in range(NT):
                            t = slice(P * i, P * (i + 1))
                            ins = three(ps[:, bank + i, :], XH[:, 4 * h + k, t], XL[:, 4 * h + k, t], wh[:, k, :], wl[:, k, :],
                                        h == 0 and k == 0, h == 1 and k == 3, False)
                    ins.then_inc(w_used, 1)

            def rows_t(u, yh, yl, first, last):
                lo_ready(u)
                wh, wl = (x.rearrange("p (k n) -> p k n", k=2) for x in (hi_of(u), lo_of(u)))
                for k in range(2):
                    for i in range(NT):
                        t = slice(P * i, P * (i + 1))
                        for h in range(2):
                            n = slice(512 * h, 512 * (h + 1))
                            ins = three(ps[:, 4 + 2 * i + h, :], yh[:, k, t], yl[:, k, t], wh[:, k, n], wl[:, k, n],
                                        first and k == 0, last and k == 1, False)
                ins.then_inc(w_used, 1)

            def ck(x, n=KD):
                return x.rearrange("p (k t) -> p k t", k=n)

            def out_proj(c, d=0, both=False):
                n = 8 if both else 4
                for q in range(n):
                    y = ya if q < 4 else yb
                    k = 2 * (q % 4)
                    rows_t((c + q, d), ck(y[:, 0:2048])[:, k:k + 2, :], ck(y[:, 2048:4096])[:, k:k + 2, :], q == 0, q == n - 1)

            def turn(k, src):
                hr = 2 * k + 2
                pe.wait_ge(sem("h_ready"), hr)
                b = TB[k]
                for c in range(KD):
                    for i in range(NT):
                        o = (c % 2) * S + P * i
                        ins = pe.transpose(ps[:, b + c // 2, o:o + P], src[:, i, P * c:P * (c + 1)], ident[:, :])
                    if c % 4 == 3:
                        ins.then_inc(sem("turned"), 1)

            def parts(k):
                pe.wait_ge(sem("t_lo"), 2 * (k - (k > 3)) + 2)

            pe.wait_ge(s_const, 1)
            pe.wait_ge(s_par, 16 * N_PAR)
            pe.transpose(ps[:, 0, 0:R0], A[0:R0, 0:128], ident[0:R0, 0:R0])
            pe.transpose(ps[:, 0, P:P + R1], A[0:R1, 128:256], ident[0:R1, 0:R1]).then_inc(s_pt, 1)
            pe.wait_ge(s_ptc, 1)

            def lru(l, c0):
                group_f(c0, 0)
                group_f(c0 + 2, 2)
                pe.wait_ge(sem("lru_ev"), 3 * l + 1)
                group_f(c0 + 4, 0)
                pe.wait_ge(sem("lru_uc"), l + 1)
                for m in range(2):
                    for c in range(4):
                        o = 1024 * l + 512 * m + P * c
                        ins = pe.matmul(ps[:, 4 + 2 * m + c // 2, (c % 2) * S:(c % 2 + 1) * S], gb[:, o:o + P], UC[:, c, :],
                                        start=True, stop=True)
                    ins.then_inc(sem("lru_gate"), 1)
                pe.wait_ge(sem("lru_ev"), 3 * l + 2)
                group_f(c0 + 6, 2)
                pe.wait_ge(sem("lru_ev"), 3 * l + 3)
                group_f(c0 + 8, 0)
                pe.wait_ge(sem("lru_ylo"), l + 1)
                out_proj(c0 + 10)

            turn(0, HTOK)
            parts(0)
            lru(0, U_LRU0)
            turn(1, HTOK)
            parts(1)

            HH, HL = ck(ya[:, 0:1024], 4), ck(ya[:, 1024:2048], 4)

            def down(c, d, g, first, last):
                pe.wait_ge(sem("f_lo"), g + 1)
                for q in range(2):
                    rows_t((c + q, d), HH[:, 2 * q:2 * q + 2, :], HL[:, 2 * q:2 * q + 2, :], first and q == 0, last and q == 1)

            group_f(U_FFN, 0)
            group_f(U_FFN + 2, 2)
            def ffn_step(g, dd, first):
                pe.wait_ge(sem("f_silu"), g)
                group_f(U_FFN + 4, 0, dd)
                pe.wait_ge(sem("f_h"), g)
                down(U_FFN + 6, dd, g - 1, first, False)
                group_f(U_FFN + 8, 2, dd)
            ffn_step(1, 0, True)
            with pe.Fori(2, NG) as g:
                ffn_step(g, pe.snap(g - 1), False)
            down(U_FFN + 40, 0, NG - 1, False, True)

            turn(2, HTOK)
            parts(2)
            lru(1, U_LRU1)
            turn(3, HTOK)

            pe.wait_ge(sem("full_a"), 4)
            pe.wait_ge(sem("full_v"), 4)
            WR = gb[:, 2112:2176].rearrange("p (k n) -> p k n", k=8)
            for i in range(NT):
                for k in range(KD):
                    ins = pe.matmul(ps[:, 4, NE * i:NE * (i + 1)], hTf[:, k, P * i:P * (i + 1)], WR[:, k, :], start=k == 0, stop=k == KD - 1)
            ins.then_inc(sem("r_log"), 1)
            CH = ar(832, NT, NE)
            pe.wait_ge(sem("r_ch"), 1)
            pe.matmul(ps[:, 5, 0:8], ustr[:, :], CH[:, 0, :], start=True, stop=True)
            pe.matmul(ps[:, 5, 8:16], ones[:, :], CH[:, 0, :], start=True, stop=False)
            pe.matmul(ps[:, 5, 8:16], ustr[:, :], CH[:, 1, :], start=False, stop=True)
            pe.matmul(ps[:, 5, 16:24], ones[:, :], CH[:, 0, :], start=True, stop=False)
            pe.matmul(ps[:, 5, 16:24], ones[:, :], CH[:, 1, :], start=False, stop=True).then_inc(sem("r_pos"), 1)

            TKh = hhi[:, :].rearrange("p (i n) -> p i n", i=NT)
            TKl = hlo[:, :].rearrange("p (i n) -> p i n", i=NT)
            XEh, XEl = ck(ya[:, 0:1024]), ck(ya[:, 1024:2048])
            HTh, HTl = ck(ya[:, 2048:2560], 4), ck(ya[:, 2560:3072], 4)
            SR = ya[:, 3072:3328].rearrange("p (i s) -> p i s", i=NT)
            ST = ya[:, 3328:3584].rearrange("p (i s) -> p i s", i=NT)
            Yh, Yl = yb[:, 0:1024], yb[:, 1024:2048]
            MHF = ar(1536, 512)

            def gather(k):
                pe.wait_ge(sem("m_s"), k + 1)
                for c in range(KD):
                    o = ps[:, 5 + c // 4, P * (c % 4):P * (c % 4 + 1)]
                    n = 0
                    for i in range(NT):
                        for t in (TKh, TKl):
                            ins = pe.matmul(o, t[:, i, P * c:P * (c + 1)], SR[:, i, :], start=n == 0, stop=n == 3)
                            n += 1
                ins.then_inc(sem("m_gth"), 1)

            def moe_in(c, d, bank):
                for h in range(2):
                    u = (c + h, d)
                    lo_ready(u)
                    wh, wl = (x.rearrange("p (k n) -> p k n", k=4) for x in (hi_of(u), lo_of(u)))
                    for k in range(4):
                        ins = three(ps[:, bank, :], XEh[:, 4 * h + k, :], XEl[:, 4 * h + k, :], wh[:, k, :], wl[:, k, :],
                                    h == 0 and k == 0, h == 1 and k == 3, False)
                    ins.then_inc(w_used, 1)

            def moe_down(c, d, g, first, last):
                pe.wait_ge(sem("m_htlo"), g + 1)
                for q in range(2):
                    u = (c + q, d)
                    lo_ready(u)
                    wh, wl = (x.rearrange("p (k n) -> p k n", k=2) for x in (hi_of(u), lo_of(u)))
                    for k in range(2):
                        for h in range(2):
                            n = slice(512 * h, 512 * (h + 1))
                            ins = three(ps[:, 2 + h, :], HTh[:, 2 * q + k, :], HTl[:, 2 * q + k, :], wh[:, k, n], wl[:, k, n],
                                        first and q == 0 and k == 0, last and q == 1 and k == 1, False)
                    ins.then_inc(w_used, 1)

            def turn_h(g):
                pe.wait_ge(sem("m_h"), g + 1)
                for q in range(4):
                    ins = pe.transpose(ps[:, 4, P * q:P * (q + 1)], MHF[:, P * q:P * (q + 1)], ident[:, :])
                ins.then_inc(sem("m_tr"), 1)

            def scatter(k):
                pe.wait_ge(sem("m_ylo"), k + 1)
                pe.wait_ge(sem("m_st"), k + 1)
                for i in range(NT):
                    for h in range(2):
                        n = slice(512 * h, 512 * (h + 1))
                        pe.matmul(ps[:, 4 + 2 * i + h, :], ST[:, i, :], Yh[:, n], start=True, stop=False)
                        ins = pe.matmul(ps[:, 4 + 2 * i + h, :], ST[:, i, :], Yl[:, n], start=False, stop=True)
                ins.then_inc(sem("m_sct"), 1)

            pe.wait_ge(sem("tab_ready"), 1)
            njobs = pe.value_load(tab[0:1, 3:4], min_val=NE, max_val=NJMAX)
            pe.wait_ge(sem("htok_lo"), 1)
            gather(0)

            def moe_step(dj, dd, first):
                pe.wait_ge(sem("m_silu"), dd + 1)
                moe_in(U_MOE + 4, dd, 0)
                turn_h(dd)
                moe_in(U_MOE + 6, dd, 1)
                moe_down(U_MOE + 8, dd, dd, first, False)

            with pe.Fori(0, njobs) as j:
                dj = pe.snap(j * NG)
                pe.wait_ge(sem("m_xlo"), j + 1)
                moe_in(U_MOE, dj, 0)
                moe_in(U_MOE + 2, dj, 1)
                scatter(j)
                pe.wait_ge(sem("m_sev"), j + 1)
                moe_step(dj, dj, True)
                with pe.Fori(2, NG) as g:
                    moe_step(dj, pe.snap(dj + g - 1), False)
                for i in range(NT):
                    ins = pe.transpose(ps[:, 7, P * i:P * (i + 1)], SR[:, i, :].bitcast(F32), ident[:, :])
                ins.then_inc(sem("m_str"), 1)
                turn_h(dj + (NG - 1))
                gather(j + 1)
                moe_down(U_MOE + 40, dj, dj + (NG - 1), False, True)
            scatter(njobs)
            dn = pe.snap(njobs * NG)

            turn(4, HTOK)
            parts(4)
            c = U_SSD
            WS = gbv(3072, KD, 32)
            CVV = ar(2592, 10, S)
            group_f(c, 0, dn)
            group_f(c + 2, 2, dn)
            pe.wait_ge(sem("e_ev"), 1)
            u = (c + 4, dn)
            lo_ready(u)
            wh, wl = (x.rearrange("p (k n) -> p k n", k=8) for x in (hi_of(u), lo_of(u)))
            for k in range(KD):
                for q in range(2):
                    ins = three(ps[:, 0, S * q:S * (q + 1)], XH[:, k, :], XL[:, k, :], wh[:, k, P * q:P * (q + 1)],
                                wl[:, k, P * q:P * (q + 1)], k == 0 and q == 0, k == KD - 1, True)
            ins.then_inc(w_used, 1)
            c += 5
            for i in range(NT):
                for k in range(KD):
                    ins = pe.matmul(ps[:, 4, 16 * i:16 * (i + 1)], hTf[:, k, P * i:P * (i + 1)], WS[:, k, 0:16], start=k == 0, stop=k == KD - 1)
            ins.then_inc(sem("d_ps"), 1)
            pe.wait_ge(sem("e_ev"), 2)
            group_t(c, 2, dn)
            pe.wait_ge(sem("e_ev"), 3)
            group_t(c + 2, 0, dn)
            c += 4
            DTA = gbv(2896, NT, 16)
            pe.wait_ge(sem("d_dta"), 1)
            for i in range(NT):
                pe.matmul(ps[:, 5, 16 * i:16 * (i + 1)], utri[:, :], DTA[:, i, :], start=True, stop=True)
            pe.matmul(ps[:, 5, 32:48], ones[:, :], DTA[:, 0, :], start=True, stop=True).then_inc(sem("d_cum"), 1)
            pe.wait_ge(sem("e_xbc"), 1)
            pe.wait_ge(sem("d_acs"), 1)
            for i in range(NT):
                for q in range(8):
                    ins = pe.transpose(ps[:, 4 + 2 * i + q // 4, P * (q % 4):P * (q % 4 + 1)], CVV[:, q, P * i:P * (i + 1)], ident[:, :])
            ins.then_inc(sem("s_xtr"), 1)
            pe.wait_ge(sem("e_xbc"), 2)
            pe.wait_ge(sem("s_xs"), 1)
            for gr in range(2):
                pr = slice(64 * gr, 64 * gr + 64)
                for i in range(NT):
                    t = slice(P * i, P * (i + 1))
                    pe.matmul(ps[:, 4 + gr, t], CVV[pr, 8, t], CVV[pr, 9, t], start=True, stop=True)
            pe.transpose(ps[:, 6, 0:P], CVV[:, 8, 0:P], ident[:, :]).then_inc(sem("s_cbt"), 1)
            pe.wait_ge(sem("s_cb"), 1)
            pe.wait_ge(sem("s_xdd"), 1)
            for gr in range(2):
                ins = pe.matmul(ps[:, 6 + gr, :], gbv(512, 128), ar(9248 + 512 * gr, 512), start=True, stop=True)
            ins.then_inc(sem("s_stp"), 1)
            XDT = ar(0, NT, D)

            def seg(q):
                if q >= 2:
                    pe.wait_ge(sem("s_seg"), q - 1)
                i = q // 4
                for h in range(4):
                    hh = 4 * (q % 4) + h
                    ins = pe.matmul(ps[:, 4 + q % 2, P * h:P * (h + 1)], DTA[:, i, hh:hh + 1].to_broadcast([P, P]), utri[:, :],
                                    start=True, stop=True)
                ins.then_inc(sem("s_segp"), 1)

            def y_diag(q):
                i = q // 4
                pe.wait_ge(sem("s_m"), q + 1)
                if q == 0:
                    pe.wait_ge(sem("s_st"), 1)
                if q == 4:
                    pe.wait_ge(sem("s_ye"), 1)
                for h in range(4):
                    hh = 4 * (q % 4) + h
                    ins = pe.matmul(ps[:, 6 + (q % 4) // 2, 64 * (hh % 8):64 * (hh % 8 + 1)], ar(9248 + 512 * (q % 2) + P * h, P),
                                    XDT[:, i, 64 * hh:64 * (hh + 1)], start=True, stop=True)
                ins.then_inc(sem("s_yq"), 1)

            seg(0)
            for q in range(8):
                if q < 7:
                    seg(q + 1)
                y_diag(q)
            pe.wait_ge(sem("s_seg"), 8)
            for gr in range(2):
                pr = slice(64 * gr, 64 * gr + 64)
                ins = pe.matmul(ps[:, 4 + gr, :], CVV[pr, 9, P:S], gb[pr, 640:1152], start=True, stop=True)
            ins.then_inc(sem("s_yoff"), 1)
            pe.wait_ge(sem("e_ev"), 4)
            group_f(c, 2, dn)
            pe.wait_ge(sem("e_ev"), 5)
            group_f(c + 2, 0, dn)
            c += 4
            pe.wait_ge(sem("e_ev"), 6)
            for k in range(KD):
                ins = pe.matmul(ps[0:16, 2, 0:S], WS[:, k, 16:32], hTf[:, k, :], start=k == 0, stop=k == KD - 1)
            ins.then_inc(sem("g_lr"), 1)
            turn(5, HTOK)
            pe.wait_ge(sem("g_lrc"), 1)
            parts(5)
            for q in range(4):
                ins = pe.matmul(ps[:, 4 + q // 2, (q % 2) * S:(q % 2 + 1) * S], gb[0:16, 3328 + P * q:3328 + P * (q + 1)], gb[0:16, 2048:2304],
                                start=True, stop=True)
            ins.then_inc(sem("g_x"), 1)
            for n in range(4):
                if n:
                    pe.wait_ge(sem("e_ev"), 6 + n)
                group_t(c, 2 if n % 2 == 0 else 0, dn)
                c += 2
            K = ar(1024, 4, S)
            Q1, K1 = ar(4608, 4, S), ar(5632, 4, S)
            K2 = ar(3584, NT, 512)
            V = gbv(0, NT, D)
            SCT = gb[:, 2048:3072]
            S1 = [None, gb[:, 3072:3584], gb[:, 3584:4096], ar(2048, 512)]
            pe.wait_ge(sem("g_k2"), 1)
            for i in range(NT):
                for q in range(4):
                    ins = pe.transpose(ps[:, 4 + i, P * q:P * (q + 1)], K[:, q, P * i:P * (i + 1)], ident[:, :])
            ins.then_inc(sem("g_k2p"), 1)
            pe.wait_ge(sem("g_q"), 1)
            pe.wait_ge(sem("e_ev"), 11)

            def scores(i):
                if i:
                    pe.wait_ge(sem("g_sct"), i)
                t = slice(P * i, P * (i + 1))
                for q in range(4):
                    for r in range(2):
                        pr = slice(64 * r, 64 * r + 64)
                        ins = pe.matmul(ps[:, 6 + r, P * q:P * (q + 1)], K1[pr, q, t], Q1[pr, q, t], start=True, stop=True)
                ins.then_inc(sem("g_sc"), 1)

            def kv(n):
                if n:
                    pe.wait_ge(sem("g_s"), n)
                else:
                    pe.wait_ge(sem("g_k2t"), 1)
                pr = slice(64 * (n % 2), 64 * (n % 2) + 64)
                for q in range(4):
                    ins = pe.matmul(ps[:, q // 2, (q % 2) * S:(q % 2 + 1) * S], K2[pr, n // 2, P * q:P * (q + 1)],
                                    V[pr, n // 2, S * q:S * (q + 1)], start=True, stop=True)
                ins.then_inc(sem("g_kv"), 1)

            def gla_out(i):
                pe.wait_ge(sem("g_sct"), i + 1)
                pe.wait_ge(sem("g_s"), 2 * i + 1)
                if i:
                    pe.wait_ge(sem("g_oe"), i)
                Q5 = ar(6656, 2048).rearrange("p (c i r t) -> p c i r t", c=4, i=2, r=2)
                for q in range(4):
                    for r in range(2):
                        pr = slice(64 * r, 64 * r + 64)
                        o = ps[:, 2 + r, P * q:P * (q + 1)]
                        hh = 2 * q + r
                        pe.matmul(o, SCT[:, 512 * r + P * q:512 * r + P * (q + 1)], V[:, i, P * hh:P * (hh + 1)], start=True, stop=False)
                        for m in range(2):
                            n = 2 * i + m
                            if n:
                                ins = pe.matmul(o, Q5[pr, q, i, m, :], S1[n][pr, P * q:P * (q + 1)], start=False, stop=m == 1)
                ins.then_inc(sem("g_o"), 1)

            scores(0)
            kv(0)
            gla_out(0)
            kv(1)
            scores(1)
            kv(2)
            gla_out(1)
            turn(6, ar(0, NT, D))
            parts(6)
            out_proj(c, dn, both=True)
            c += 8

            turn(7, HTOK)
            parts(7)
            for n in range(8):
                if n >= 2:
                    pe.wait_ge(sem("o_ev"), n - 1)
                (group_f if n < 4 else group_t)(c, 2 * (n % 2), dn)
                c += 2
            MQ, MK, MV = ar(0, KD, S), ar(2048, KD, S), ar(4096, NT, D)

            def att_scores(c2):
                if c2 >= 2:
                    pe.wait_ge(sem("a_sm"), c2 - 1)
                for r in range(2):
                    pr = slice(64 * r, 64 * r + 64)
                    b = 4 + 2 * (c2 % 2) + r
                    pe.matmul(ps[:, b, 0:P], MQ[pr, c2, 0:P], MK[pr, c2, 0:P], start=True, stop=True)
                    ins = pe.matmul(ps[:, b, P:384], MQ[pr, c2, P:S], MK[pr, c2, :], start=True, stop=True)
                ins.then_inc(sem("a_sc"), 1)

            def att_turn(c2):
                pe.wait_ge(sem("a_exp"), c2 + 1)
                if c2:
                    pe.wait_ge(sem("a_ptc"), c2)
                PB = ar(8192 + 768 * (c2 % 2), 2, 384)
                for r in range(2):
                    for q in range(3):
                        ins = pe.transpose(ps[:, r, P * q:P * (q + 1)], PB[:, r, P * q:P * (q + 1)], ident[:, :])
                ins.then_inc(sem("a_pt"), 1)

            def att_out(c2):
                pe.wait_ge(sem("a_ptc"), c2 + 1)
                if c2 >= 2:
                    pe.wait_ge(sem("a_oe"), c2 - 1)
                PTB = gbv(768 * (c2 % 2), 2, 384)
                b = 2 + c2 % 2
                for r in range(2):
                    hh = slice(64 * (2 * c2 + r), 64 * (2 * c2 + r + 1))
                    pe.matmul(ps[:, b, 64 * r:64 * (r + 1)], PTB[:, r, 0:P], MV[:, 0, hh], start=True, stop=True)
                    o = ps[:, b, 128 + 64 * r:192 + 64 * r]
                    pe.matmul(o, PTB[:, r, P:256], MV[:, 0, hh], start=True, stop=False)
                    ins = pe.matmul(o, PTB[:, r, 256:384], MV[:, 1, hh], start=False, stop=True)
                ins.then_inc(sem("a_o"), 1)

            pe.wait_ge(sem("o_ev"), 8)
            att_scores(0)
            for c2 in range(8):
                if c2 < 7:
                    att_scores(c2 + 1)
                att_turn(c2)
                if c2:
                    att_out(c2 - 1)
            att_out(7)
            turn(8, hTf[:, :, :].rearrange("p c t -> p (c t)").rearrange("p (i n) -> p i n", i=NT))
            parts(8)
            out_proj(c, dn)


_INS = ["x", "norm_mix", "norm_ffn", "norm_final", "w_in", "conv_w", "lru_conv_w", "lru_conv_b", "lru_wa", "lru_ba",
        "lru_wx", "lru_bx", "lru_lambda", "w_out", "ffn_w_gate", "ffn_w_up", "ffn_w_down", "w_router", "moe_w_gate",
        "moe_w_up", "moe_w_down", "even_norm_2", "even_w_in_2", "even_conv_w_2", "even_conv_b_2", "even_a_log_2",
        "even_dt_bias_2", "even_d_skip_2", "even_ssd_norm_2", "even_gate_w2_2", "even_gate_b_2", "even_gla_norm_2",
        "even_w_out_2", "odd_norm_2", "odd_w_in_2", "odd_w_out_2", "final_norm_2"]


def kernel(**inputs):
    import numpy as np
    from concourse import bacc
    from concourse.bass_utils import run_bass_kernel_spmd

    nc = bacc.Bacc("TRN2", target_bir_lowering=False, num_devices=1, dynamic_dma_scratch_size=8192)
    arrays, aps = {}, {}
    for name in _INS:
        v = np.ascontiguousarray(inputs[name])
        arrays[f"in_{name}"] = v
        aps[name] = nc.dram_tensor(f"in_{name}", v.shape, mybir.dt.from_np(v.dtype), kind="ExternalInput").ap()
    out = nc.dram_tensor("out", (1, S, D), F32, kind="ExternalOutput").ap()
    build(nc, aps, out)
    return run_bass_kernel_spmd(nc, [arrays], core_ids=[0]).results[0]["out"]
```

```python
from contextlib import ExitStack

import concourse.bass as bass
from concourse import mybir

F32 = mybir.dt.float32
F32R = mybir.dt.float32r
I32 = mybir.dt.int32
ALU = mybir.AluOpType
ACT = mybir.ActivationFunctionType
AX_X = mybir.AxisListType.X

P = 128
D = 1024
S = 256
NT = S // P
KD = D // P
EPS = 1e-6
FF = 3584
GW = 512
NG = FF // GW
NE = 8
NJMAX = 11
RAW, SPL = 6, 3
UW = 2048

U_LRU0 = 0
U_FFN = U_LRU0 + 14
U_LRU1 = U_FFN + 6 * NG
U_MOE = U_LRU1 + 14
U_SSD = U_MOE
U_MOBA = U_SSD + 29
U_END = U_MOBA + 20

C_NMIX, C_NFFN, C_CONV, C_LCONV, C_LCB, C_BA, C_BX, C_LAM = 0, 16, 32, 56, 88, 96, 104, 112
C_ENORM, C_ONORM, C_ECONV, C_ECB, C_SSDN, C_GB, C_GLAN = 0, 8, 16, 56, 66, 74, 78
R0, R1 = 120, 79

E_Z, E_XBC, E_DT, E_Q, E_K, E_V, E_LR, E_G = 0, 1024, 2304, 2320, 2832, 3344, 4368, 4384


def build(nc, a, out):
    with ExitStack() as ctx:
        def sb(name, shape, dt=F32):
            return ctx.enter_context(nc.sbuf_tensor(name, shape, dt))

        made = {}

        def sem(name):
            if name not in made:
                made[name] = ctx.enter_context(nc.semaphore(name))
            return made[name]

        raw = sb("raw", [P, RAW, UW])
        whi = sb("whi", [P, SPL, UW], F32R)
        wlo = sb("wlo", [P, SPL, UW], F32R)
        X = sb("X", [P, NT, D])
        hTf = sb("hTf", [P, KD, S])
        hhi = sb("hhi", [P, 2048], F32R)
        hlo = sb("hlo", [P, 2048], F32R)
        ya = sb("ya", [P, 4096], F32R)
        with nc.sbuf_tensor("gb", [P, 4096], F32) as gb:
            pass
        yb = sb("yb", [P, 4096], F32R)
        A = sb("arena", [P, 10752])
        ident = sb("ident", [P, P])
        utri = sb("utri", [P, P])
        ustr = sb("ustr", [P, P])
        ones = sb("ones", [P, P])
        iot = sb("iot", [P, P])
        bdm = sb("bdm", [P, P], I32)
        PT = sb("PT", [P, 2, P])
        m01 = sb("m01", [P, S])
        sm = sb("sm", [P, 256])
        tab = sb("tab", [P, 4], I32)
        ps = ctx.enter_context(nc.psum_tensor("ps", [P, 8, 512], F32))

        def ar(o, *shape):
            n = 1
            for s in shape:
                n *= s
            v = A[:, o:o + n]
            return v if len(shape) == 1 else v.rearrange(
                "p (a b) -> p a b" if len(shape) == 2 else "p (a b c) -> p a b c",
                **dict(zip("abc", shape)))

        def gbv(o, *shape):
            n = 1
            for s in shape:
                n *= s
            v = gb[:, o:o + n]
            return v if len(shape) == 1 else v.rearrange("p (a b) -> p a b", a=shape[0])

        H = 8224
        HTOK = ar(H, NT, D)
        ssq, rst, tpow, mhalf = sm[:, 0:16], sm[:, 16:32], sm[:, 32:48], sm[:, 48:64]
        s8 = sm[:, 64:72]
        one_col = ones[:, 0:1]

        UP, UC, GG, CV, CO = ar(0, 4, 259), ar(1040, 4, S), ar(2064, 4, S), ar(3088, 4, 258), ar(4128, 4, S)
        RR, II, TT, YF = ar(5152, 4, S), ar(6176, 4, S), ar(7200, 4, S), ar(H, KD, S)
        GT = ar(0, 4, S)

        w_loaded = [sem(f"w_loaded{i}") for i in range(RAW)]
        w_hi, w_lo, w_used = sem("w_hi"), sem("w_lo"), sem("w_used")

        def plus(c, k, d):
            return c if isinstance(d, int) and d == 0 else d * k + c

        def hi_of(u):
            return whi[:, u[0] % SPL, :]

        def lo_of(u):
            return wlo[:, u[0] % SPL, :]

        def cols(m, o, w, k0, k1):
            return m.rearrange("(k p) n -> p k n", p=P)[:, k0:k1, o:o + w]

        w_in, w_out = a["w_in"], a["w_out"]
        ewi, ewo = a["even_w_in_2"][0], a["even_w_out_2"][0]
        owi, owo = a["odd_w_in_2"][0], a["odd_w_out_2"][0]
        fg, fu, fd = a["ffn_w_gate"][0], a["ffn_w_up"][0], a["ffn_w_down"][0]
        LRU_ORDER = (3, 4, 0, 2, 1)
        LRU_ROWS = (2, 3, 0, 1)
        TB = (0, 0, 0, 0, 4, 4, 0, 0, 0)
        BG = A[:, 5152:6176]

        s_par, s_x, s_out = sem("par_loaded"), sem("x_loaded"), sem("out_stored")
        s_bg = sem("gain_loaded")
        s_const = sem("consts_made")
        s_pt = sem("params_turned")
        s_ptc = sem("params_copied")
        s_par2, s_bd = sem("late_par_loaded"), sem("gate_w_loaded")
        N_PAR, N_PAR2, N_BD = 8, 14, 8
        block = ctx.enter_context(nc.Block())

        @block.sync
        def _(sp):
            def load(u, src):
                c, d = u
                if c >= RAW or not isinstance(d, int):
                    sp.wait_ge(w_lo, plus(c - RAW + 1, 6, d))
                dst = raw[:, c % RAW, :]
                if len(src.shape) == 3:
                    dst = dst.rearrange("p (k n) -> p k n", k=src.shape[1])
                sp.dma_start(dst, src).then_inc(w_loaded[c % RAW], 16)

            def load_group(c, m, o, d=0):
                for h in range(2):
                    load((c + h, d), cols(m, o, GW, 4 * h, 4 * h + 4))

            def load_rows(c, m, n, d=0, order=range(8)):
                for i, q in enumerate(order[0:n]):
                    load((c + i, d), m[2 * P * q:2 * P * (q + 1), :].rearrange("(k p) n -> p k n", p=P))

            sp.dma_start(X[:, :, :], a["x"][0].rearrange("(i p) n -> p i n", p=P)).then_inc(s_x, 16)

            def par(dst, src, s=s_par2):
                sp.dma_start(dst, src).then_inc(s, 16)

            def rows(o, src, pat):
                src = src.rearrange(pat, p=P)
                par(gb[o:o + src.shape[0], 2176:2304], src)

            def gate_weights():
                sp.wait_ge(sem("bd_zero"), 1)
                for l in range(2):
                    for m, w in enumerate((a["lru_wa"], a["lru_wx"])):
                        for r in range(2):
                            dst = gb[64 * r:64 * r + 64, 1024 * l + 512 * m:1024 * l + 512 * (m + 1)]
                            par(dst.rearrange("p (j n) -> p j n", j=4)[:, :, 64 * r:64 * r + 64],
                                w[l].rearrange("(j r) i o -> r i j o", r=2)[r], s_bd)

            def late_params():
                rows(C_ENORM, a["even_norm_2"], "l (c p) -> (l c) p")
                rows(C_ONORM, a["odd_norm_2"], "l (c p) -> (l c) p")
                rows(C_ECONV, a["even_conv_w_2"], "l k (c p) -> (l k c) p")
                rows(C_ECB, a["even_conv_b_2"], "l (c p) -> (l c) p")
                rows(C_SSDN, a["even_ssd_norm_2"], "l (c p) -> (l c) p")
                rows(C_GB, a["even_gate_b_2"], "l (c p) -> (l c) p")
                rows(C_GLAN, a["even_gla_norm_2"], "l (c p) -> (l c) p")
                par(gbv(3072, KD, 32)[:, :, 0:16], cols(ewi, E_DT, 16, 0, 8))
                par(gbv(3072, KD, 32)[:, :, 16:32], cols(ewi, E_LR, 16, 0, 8))
                par(gb[0:16, 3328:3840], a["even_gate_w2_2"][0])
                par(gbv(2688, 16), a["even_a_log_2"][0].partition_broadcast(P))
                par(gbv(2768, 16), a["even_d_skip_2"][0].partition_broadcast(P))
                par(gbv(2928, 16), a["even_dt_bias_2"][0].partition_broadcast(P))
                par(gb[:, 2112:2176].rearrange("p (k n) -> p k n", k=8), cols(a["w_router"][0], 0, NE, 0, 8))

            def lru(l, c):
                for n, g in enumerate(LRU_ORDER):
                    load_group(c + 2 * n, w_in[l], GW * g)
                    if l == 0 and n == 0:
                        sp.wait_ge(s_par, 16 * N_PAR)
                    if l == 0 and n == 2:
                        gate_weights()
                load_rows(c + 10, w_out[l], 4, order=LRU_ROWS)
                if l == 0:
                    late_params()

            lru(0, U_LRU0)

            load_group(U_FFN, fg, 0)
            load_group(U_FFN + 2, fu, 0)
            with_down = fd.rearrange("(q k p) n -> q p k n", k=2, p=P)
            with sp.Fori(1, NG) as g:
                for h in range(2):
                    load((U_FFN + 4 + h, g - 1), fg.rearrange("(k p) n -> p k n", p=P)[:, 4 * h:4 * h + 4, bass.ds(g * GW, GW)])
                for h in range(2):
                    load((U_FFN + 6 + h, g - 1), with_down[bass.ds(g * 2 - 2 + h, 1)].rearrange("q p k n -> (q p) k n"))
                for h in range(2):
                    load((U_FFN + 8 + h, g - 1), fu.rearrange("(k p) n -> p k n", p=P)[:, 4 * h:4 * h + 4, bass.ds(g * GW, GW)])
            load_rows(U_FFN + 40, fd[6 * GW:7 * GW, :], 2)
            lru(1, U_LRU1)

            eg = a["moe_w_gate"].rearrange("a e (k p) n -> (a e) p k n", p=P)
            eu = a["moe_w_up"].rearrange("a e (k p) n -> (a e) p k n", p=P)
            ed = a["moe_w_down"].rearrange("a e (q k p) n -> (a e q) p k n", k=2, p=P)

            def job(e, j):
                def cut(m, h, o):
                    return m[bass.ds(e, 1), :, 4 * h:4 * h + 4, o].rearrange("q p k n -> (q p) k n")

                def rows(q):
                    return ed[bass.ds(q, 1)].rearrange("q p k n -> (q p) k n")
                for i, m in enumerate((eg, eu)):
                    for h in range(2):
                        load((U_MOE + 2 * i + h, j * NG), cut(m, h, slice(0, GW)))
                with sp.Fori(1, NG) as g:
                    dd = sp.snap(j * NG + g - 1)
                    for i, m in enumerate((eg, eu)):
                        for h in range(2):
                            load((U_MOE + 4 + 2 * i + h, dd), cut(m, h, bass.ds(g * GW, GW)))
                    for h in range(2):
                        load((U_MOE + 8 + h, dd), rows(e * (2 * NG) + g * 2 - 2 + h))
                for h in range(2):
                    load((U_MOE + 40 + h, j * NG), rows(e * (2 * NG) + 2 * NG - 2 + h))

            with sp.Fori(0, NE) as j:
                job(j, j)
            sp.wait_ge(sem("tab_ready"), 1)
            njobs = sp.value_load(tab[0:1, 3:4], min_val=NE, max_val=NJMAX)
            with sp.If(njobs > NE):
                with sp.Fori(NE, njobs) as j:
                    e = sp.value_load(tab[0:1, bass.ds(j - NE, 1)], min_val=0, max_val=NE - 1)
                    job(e, j)
            dn = sp.snap(njobs * NG)

            c = U_SSD
            for o in (E_XBC, E_XBC + 512):
                load_group(c, ewi, o, dn)
                c += 2
            load((c, dn), cols(ewi, E_XBC + 1024, 256, 0, 8))
            c += 1
            for o in (E_Z, E_Z + 512, E_Q, E_K, E_V, E_V + 512, E_G, E_G + 512):
                load_group(c, ewi, o, dn)
                c += 2
            load_rows(c, ewo, 8, dn)
            c += 8
            for n in range(8):
                load_group(c, owi, GW * n, dn)
                c += 2
            load_rows(c, owo, 4, dn)
            assert c + 4 == U_END

            for i in range(NT):
                sp.wait_ge(sem("res_ready"), i + 1)
                sp.dma_start(out[0][P * i:P * (i + 1), :], HTOK[:, i, :]).then_inc(s_out, 16)
            sp.wait_ge(s_out, 16 * NT)

        @block.gpsimd
        def _(pool):
            steps = [0]
            s_pool = sem("pool_step")

            def link(ins):
                steps[0] += 1
                ins.then_inc(s_pool, 1)
                pool.wait_ge(s_pool, steps[0])

            link(pool.memset(ident[:, :], 0.0))
            link(pool.affine_select(out=ident[:, :], in_=ident[:, :], compare_op=ALU.not_equal, fill=1.0,
                                    base=0, pattern=[[-1, P]], channel_multiplier=1))
            link(pool.memset(ones[:, :], 1.0))
            link(pool.affine_select(out=utri[:, :], in_=ones[:, :], compare_op=ALU.is_ge, fill=0.0,
                                    base=0, pattern=[[1, P]], channel_multiplier=-1))
            link(pool.affine_select(out=ustr[:, :], in_=ones[:, :], compare_op=ALU.is_gt, fill=0.0,
                                    base=0, pattern=[[1, P]], channel_multiplier=-1))
            link(pool.memset(mhalf, -0.5))
            link(pool.iota(iot[:, :], pattern=[[1, P]], base=0, channel_multiplier=0,
                           allow_small_or_imprecise_dtypes=True))
            link(pool.memset(m01[:, :], 1.0))
            link(pool.memset(m01[:, :].rearrange("p (n c) -> p n c", c=64)[:, :, 0:1], 0.0))
            link(pool.tensor_copy(bdm[:, :], utri[:, :]))
            link(pool.affine_select(out=bdm[:, 64:128], in_=bdm[:, 64:128], compare_op=ALU.is_ge, fill=0.0,
                                    base=-64, pattern=[[0, 64]], channel_multiplier=1))
            pool.memset(tab[:, :], 0).then_inc(s_const, 1)

            def rstd(k, n, scale):
                pool.wait_ge(sem("ssq_a"), SSQ_A[k])
                pool.wait_ge(sem("ssq_v"), SSQ_V[k])
                link(pool.tensor_scalar(tpow[:, 0:n], ssq[:, 0:n], scale, EPS, ALU.mult, ALU.add))
                pool.tensor_tensor(rst[:, 0:n], tpow[:, 0:n], mhalf[:, 0:n], ALU.pow).then_inc(sem("rstd"), 1)

            SSQ_A = [1, 2, 3, 4, 5, 6, 7, 7, 8, 9]
            SSQ_V = [1, 2, 3, 4, 5, 6, 7, 8, 9, 10]
            for k in range(10):
                if k == 6:
                    pool.wait_ge(sem("s_xs"), 2)
                    for t in range(NT):
                        ins = pool.tensor_tensor(ar(2592 + 1024 * t, 16, 64), ar(5152 + 1024 * t, 16, 64),
                                                 gbv(2768, 16).unsqueeze(2).to_broadcast([P, 16, 64]), ALU.mult)
                    ins.then_inc(sem("s_skip"), 1)
                if k == 7:
                    rstd(k, 16, 1.0 / P)
                else:
                    rstd(k, NT, 1.0 / D)

        @block.scalar
        def _(act):
            steps = [0]
            s_act = sem("act_step")

            def link(ins):
                steps[0] += 1
                ins.then_inc(s_act, 1)
                act.wait_ge(s_act, steps[0])

            def split(u):
                c, d = u
                if c >= U_END:
                    return
                act.wait_ge(w_loaded[c % RAW], plus(16 * (c // RAW + 1), 16, d))
                if c >= SPL or not isinstance(d, int):
                    act.wait_ge(w_used, plus(c - SPL + 1, 6, d))
                act.activation(hi_of(u), raw[:, c % RAW, :], ACT.Copy).then_inc(w_hi, 1)

            def after(c, d=0, n=1):
                for i in range(n):
                    split((c + i + SPL, d))

            def rows(o, src, pat):
                src = src.rearrange(pat, p=P)
                act.dma_start(A[o:o + src.shape[0], 0:128], src).then_inc(s_par, 16)

            rows(C_NMIX, a["norm_mix"], "l (c p) -> (l c) p")
            rows(C_NFFN, a["norm_ffn"], "l (c p) -> (l c) p")
            rows(C_CONV, a["conv_w"], "l k (c p) -> (l k c) p")
            rows(C_LCONV, a["lru_conv_w"], "l k (c p) -> (l k c) p")
            rows(C_LCB, a["lru_conv_b"], "l (c p) -> (l c) p")
            rows(C_BA, a["lru_ba"], "l (c p) -> (l c) p")
            rows(C_BX, a["lru_bx"], "l (c p) -> (l c) p")
            rows(C_LAM, a["lru_lambda"], "l (c p) -> (l c) p")

            act.wait_ge(s_x, 16)
            act.activation(A[:, 7200:8224], X[:, 0, :], ACT.Square, accum_out=ssq[:, 0:1]).then_inc(sem("ssq_a"), 1)
            split((0, 0))

            def used(c, d=0):
                act.wait_ge(w_used, plus(c + 1, 6, d))

            def att_copy(c2):
                act.wait_ge(sem("a_pt"), c2 + 1)
                if c2 >= 2:
                    act.wait_ge(sem("a_o"), c2 - 1)
                act.activation(gbv(768 * (c2 % 2), 2, 384), ps[:, 0:2, 0:384], ACT.Copy).then_inc(sem("a_ptc"), 1)

            def load_gain(src):
                act.dma_start(BG, src.partition_broadcast(P)).then_inc(s_bg, 16)

            X0 = (1, 2, 3, 5, 7, 8)

            def norm_ssq(k, src):
                if k in X0:
                    act.wait_ge(sem("x0_ready"), X0.index(k) + 1)
                else:
                    act.wait_ge(sem("x_ready"), k)
                act.activation(A[:, 7200:8224], src, ACT.Square, accum_out=ssq[:, 0:1]).then_inc(sem("ssq_a"), 1)

            def turn(k, gain, hi=None, full=None):
                b = TB[k]
                for q in range(4 if hi is not None else 2):
                    act.wait_ge(sem("turned"), 4 * k + q + 1)
                    for c in (2 * q, 2 * q + 1):
                        dst = full[:, c, :] if hi is None else hi[:, S * c:S * (c + 1)]
                        ins = act.activation(dst, ps[:, b + q, (c % 2) * S:(c % 2 + 1) * S], ACT.Copy, scale=gain(c))
                    if hi is not None:
                        ins.then_inc(sem("t_hi"), 1)
                if hi is None:
                    ins.then_inc(sem("full_a"), 1)
                elif full is not None:
                    for c in range(KD):
                        if c % 4 == 0:
                            act.wait_ge(sem("t_lo"), 2 * (k - (k > 3)) + c // 4 + 1)
                        ins = act.activation(full[:, c, :], ps[:, b + c // 2, (c % 2) * S:(c % 2 + 1) * S], ACT.Copy, scale=gain(c))
                    ins.then_inc(sem("full_a"), 1)

            def gcol(t, o):
                return lambda c: PT[:, t, o + c:o + c + 1]

            def lru(l, c0):
                after(c0, n=2)
                used(c0 + 1)
                for b in range(2):
                    ins = act.activation(UP[:, 2 * b:2 * b + 2, 3:259], ps[:, b, :].rearrange("p (c t) -> p c t", c=2), ACT.Copy)
                ins.then_inc(sem("lru_ev"), 1)
                after(c0 + 2, n=2)
                used(c0 + 3)
                act.activation(GG[:, :, :], ps[:, 2:4, :].rearrange("p b (c t) -> p (b c) t", c=2), ACT.Copy).then_inc(sem("lru_ev"), 1)
                act.wait_ge(sem("lru_gate"), 2 * l + 1)
                for c in range(4):
                    act.activation(RR[:, c, :], ps[:, 4 + c // 2, (c % 2) * S:(c % 2 + 1) * S], ACT.Sigmoid,
                                   bias=PT[:, 0, C_BA + 4 * l + c:C_BA + 4 * l + c + 1]).then_inc(sem("lru_r"), 1)
                act.wait_ge(sem("lru_gate"), 2 * l + 2)
                for c in range(4):
                    ins = act.activation(II[:, c, :], ps[:, 6 + c // 2, (c % 2) * S:(c % 2 + 1) * S], ACT.Sigmoid,
                                         bias=PT[:, 0, C_BX + 4 * l + c:C_BX + 4 * l + c + 1])
                ins.then_inc(sem("lru_i"), 1)
                act.wait_ge(sem("lru_gt"), l + 1)
                act.activation(GT[:, :, :], GT[:, :, :], ACT.Sigmoid, scale=1.5957691216057308).then_inc(sem("lru_sg"), 1)
                after(c0 + 4)
                act.wait_ge(sem("lru_r"), 4 * l + 4)
                for c in range(4):
                    ins = act.activation(TT[:, c, :], RR[:, c, :], ACT.Tanh, scale=s8[:, 4 * l + c:4 * l + c + 1])
                ins.then_inc(sem("lru_th"), 1)
                act.wait_ge(sem("lru_th"), l + 1)
                for c in range(4):
                    ins = act.activation(RR[:, c, :], RR[:, c, :], ACT.Exp, scale=s8[:, 4 * l + c:4 * l + c + 1])
                ins.then_inc(sem("lru_a"), 1)
                after(c0 + 5)
                used(c0 + 5)
                act.activation(CO[:, :, :], ps[:, 0:2, :].rearrange("p b (c t) -> p (b c) t", c=2), ACT.Copy).then_inc(sem("lru_ev"), 1)
                after(c0 + 6)
                act.wait_ge(sem("lru_m"), l + 1)
                act.activation(TT[:, :, :], TT[:, :, :], ACT.Sqrt, scale=-1.0).then_inc(sem("lru_s"), 1)
                after(c0 + 7)
                act.wait_ge(sem("lru_y"), 2 * l + 1)
                act.activation(ya[:, 1024:2048], YF[:, 4:8, :], ACT.Copy).then_inc(sem("lru_yhi"), 1)
                after(c0 + 8, n=2)
                act.wait_ge(sem("lru_y"), 2 * l + 2)
                act.activation(ya[:, 0:1024], YF[:, 0:4, :], ACT.Copy).then_inc(sem("lru_yhi"), 1)
                after(c0 + 10, n=3)

            turn(0, gcol(0, C_NMIX), hhi)
            for u in range(1, SPL):
                split((u, 0))
            act.wait_ge(sem("lam_abs"), 1)
            act.activation(sm[:, 80:88], sm[:, 72:80], ACT.Exp, scale=-1.0).then_inc(sem("lam_exp"), 1)
            lru(0, U_LRU0)
            norm_ssq(1, X[:, 0, :])
            after(U_LRU0 + 13)
            turn(1, gcol(0, C_NFFN), hhi)

            SG, HF = ar(0, 4, S), ar(1024, 4, S)

            def silu(g):
                act.activation(SG[:, :, :], ps[:, 0:2, :].rearrange("p b (c t) -> p (b c) t", c=2), ACT.Silu).then_inc(sem("f_silu"), 1)

            def hparts(g):
                act.wait_ge(sem("f_h"), g + 1)
                act.activation(ya[:, 0:1024], HF[:, :, :], ACT.Copy).then_inc(sem("f_hi"), 1)

            after(U_FFN, n=2)
            used(U_FFN + 1)
            silu(0)
            after(U_FFN + 2, n=2)
            hparts(0)
            with act.Fori(1, NG) as g:
                dd = act.snap(g - 1)
                after(U_FFN + 4, dd, 2)
                used(U_FFN + 5, dd)
                silu(g)
                after(U_FFN + 6, dd, 3)
                hparts(g)
                after(U_FFN + 9, dd)
            after(U_FFN + 40)
            norm_ssq(2, X[:, 0, :])
            after(U_FFN + 41)
            turn(2, gcol(0, C_NMIX + 8), hhi)
            lru(1, U_LRU1)
            norm_ssq(3, X[:, 0, :])
            after(U_LRU1 + 13)
            load_gain(a["norm_ffn"][1])
            turn(3, gcol(0, C_NFFN + 8), full=hTf)

            act.wait_ge(sem("htok"), 1)
            act.activation(hhi[:, :], HTOK.rearrange("p i n -> p (i n)"), ACT.Copy).then_inc(sem("htok_hi"), 1)
            load_gain(a["norm_final"])
            act.wait_ge(sem("r_sub"), 1)
            act.activation(ar(256, NT, NE), ar(256, NT, NE), ACT.Exp).then_inc(sem("r_exp"), 1)
            XEh, HTh, Yh = ya[:, 0:1024], ya[:, 2048:2560], yb[:, 0:1024]
            MSG = ar(1024, 512)

            def gath_hi(k):
                act.wait_ge(sem("m_gth"), k + 1)
                act.activation(XEh, ps[:, 5:7, :].rearrange("p b n -> p (b n)"), ACT.Copy).then_inc(sem("m_xhi"), 1)

            def ht_hi(g):
                act.wait_ge(sem("m_tr"), g + 1)
                act.activation(HTh, ps[:, 4, :], ACT.Copy).then_inc(sem("m_hthi"), 1)

            gath_hi(0)
            act.wait_ge(sem("tab_ready"), 1)
            njobs = act.value_load(tab[0:1, 3:4], min_val=NE, max_val=NJMAX)
            with act.Fori(0, njobs) as j:
                dj = act.snap(j * NG)
                after(U_MOE, dj, 2)
                used(U_MOE + 1, dj)
                act.activation(MSG, ps[:, 0, :], ACT.Silu).then_inc(sem("m_silu"), 1)
                after(U_MOE + 2, dj, 2)
                with act.Fori(1, NG) as g:
                    dd = act.snap(dj + g - 1)
                    after(U_MOE + 4, dd, 2)
                    used(U_MOE + 5, dd)
                    act.wait_ge(sem("m_h"), dd + 1)
                    act.activation(MSG, ps[:, 0, :], ACT.Silu).then_inc(sem("m_silu"), 1)
                    ht_hi(dd)
                    after(U_MOE + 6, dd, 4)
                ht_hi(dj + (NG - 1))
                gath_hi(j + 1)
                after(U_MOE + 40, dj)
                used(U_MOE + 41, dj)
                act.activation(Yh, ps[:, 2:4, :].rearrange("p b n -> p (b n)"), ACT.Copy).then_inc(sem("m_yhi"), 1)
                after(U_MOE + 41, dj)
            dn = act.snap(njobs * NG)

            norm_ssq(4, X[:, 0, :])
            norm_ssq(5, X[:, 0, :])
            turn(4, gcol(1, C_ENORM), hhi, hTf)
            XP, CVV = ar(0, 10, 259), ar(2592, 10, S)
            Z = ar(7200, NT, D)
            c = U_SSD
            for n in range(2):
                after(c, dn, 2)
                c += 2
                used(c - 1, dn)
                act.activation(XP[:, 4 * n:4 * n + 4, 3:259], ps[:, 2 * n:2 * n + 2, :].rearrange("p b (c t) -> p (b c) t", c=2),
                               ACT.Copy).then_inc(sem("e_ev"), 1)
            after(c, dn)
            c += 1
            used(c - 1, dn)
            act.activation(XP[:, 8:10, 3:259], ps[:, 0, :].rearrange("p (c t) -> p c t", c=2), ACT.Copy).then_inc(sem("e_ev"), 1)
            for n in range(2):
                after(c, dn, 2)
                c += 2
                used(c - 1, dn)
                b = 2 if n == 0 else 0
                for i in range(NT):
                    ins = act.activation(Z[:, i, 512 * n:512 * (n + 1)], ps[:, b + i, :], ACT.Silu)
                ins.then_inc(sem("e_ev"), 1)
                if n == 0:
                    act.wait_ge(sem("d_abs"), 1)
                    act.activation(sm[:, 160:192], sm[:, 128:160], ACT.Exp, scale=-1.0).then_inc(sem("d_exp"), 1)
                    act.activation(gbv(2704, 16), gbv(2688, 16), ACT.Exp).then_inc(sem("d_exp"), 1)
                    for h in range(2):
                        act.wait_ge(sem("e_conv"), h + 1)
                        lo, hi = ((0, 8), (8, 10))[h]
                        act.activation(CVV[:, lo:hi, :], CVV[:, lo:hi, :], ACT.Silu).then_inc(sem("e_xbc"), 1)
            act.wait_ge(sem("d_acs"), 1)
            act.activation(gbv(2816, 32), gbv(2720, 32), ACT.Exp).then_inc(sem("d_ea"), 1)
            act.activation(gbv(2848, 16), gbv(2752, 16), ACT.Exp).then_inc(sem("d_ea"), 1)
            act.wait_ge(sem("s_xtr"), 1)
            act.activation(ar(6176, 1024), ps[:, 6:8, :].rearrange("p b n -> p (b n)"), ACT.Copy).then_inc(sem("s_xs"), 1)
            for q in range(8):
                act.wait_ge(sem("s_seg"), q + 1)
                mb = ar(9248 + 512 * (q % 2), 512)
                act.activation(mb, mb, ACT.Exp).then_inc(sem("s_exp"), 1)
            act.wait_ge(sem("x_ready"), 6)
            act.activation(ar(5152, 1024), ar(2592, 1024), ACT.Square, accum_out=ssq[:, 0:1]).then_inc(sem("ssq_a"), 1)
            Q, K = ar(0, 4, S), ar(1024, 4, S)
            after(c, dn, 2)
            c += 2
            used(c - 1, dn)
            act.activation(Q, ps[:, 2:4, :].rearrange("p b (c t) -> p (b c) t", c=2), ACT.Copy, scale=0.125).then_inc(sem("e_ev"), 1)
            after(c, dn, 2)
            c += 2
            used(c - 1, dn)
            act.activation(K, ps[:, 0:2, :].rearrange("p b (c t) -> p (b c) t", c=2), ACT.Copy).then_inc(sem("e_ev"), 1)
            act.wait_ge(sem("g_lr"), 1)
            act.activation(gb[0:16, 2048:2304], ps[0:16, 2, 0:S], ACT.Copy).then_inc(sem("g_lrc"), 1)
            turn(5, gcol(1, C_SSDN), ya)
            TMP, GC, Q1, K1 = ar(2560, 4, S), ar(3584, 4, S), ar(4608, 4, S), ar(5632, 4, S)
            act.wait_ge(sem("g_abs"), 1)
            link(act.activation(TMP, TMP, ACT.Exp, scale=-1.0))
            act.activation(TMP, TMP, ACT.Ln, bias=1.0).then_inc(sem("g_ln"), 1)
            SGL = ar(8704, NT, D)
            V = gbv(0, NT, D)
            act.wait_ge(sem("g_ref"), 1)
            act.activation(Q1, TMP, ACT.Exp, scale=1.0 / 16).then_inc(sem("g_e"), 1)
            act.activation(K1, TMP, ACT.Exp, scale=-1.0 / 16).then_inc(sem("g_e"), 1)

            def v_group(c, n):
                after(c, dn, 2)
                used(c + 1, dn)
                b = 2 if n == 0 else 0
                for i in range(NT):
                    ins = act.activation(V[:, i, 512 * n:512 * (n + 1)], ps[:, b + i, :], ACT.Copy)
                ins.then_inc(sem("e_ev"), 1)

            v_group(c, 0)
            act.wait_ge(sem("g_ref"), 2)
            act.activation(TMP, TMP, ACT.Exp, scale=-1.0 / 16).then_inc(sem("g_e"), 1)
            act.activation(sm[:, 192:208].rearrange("p (a b) -> p a b", b=4),
                           GC.rearrange("p c (n t) -> p c n t", t=64)[:, :, :, 63], ACT.Exp, scale=1.0 / 16).then_inc(sem("g_e"), 1)
            act.wait_ge(sem("g_e"), 4)
            act.activation(GC, GC, ACT.Exp, scale=1.0 / 16).then_inc(sem("g_e"), 1)
            v_group(c + 2, 1)
            c += 4
            for n in range(2):
                after(c, dn, 2)
                c += 2
                used(c - 1, dn)
                b = 2 if n == 0 else 0
                if n == 0:
                    act.wait_ge(sem("t_lo"), 10)
                for i in range(NT):
                    ins = act.activation(SGL[:, i, 512 * n:512 * (n + 1)], ps[:, b + i, :], ACT.Silu)
                ins.then_inc(sem("e_ev"), 1)
            after(c, dn, 2)
            turn(6, lambda c: PT[:, 1, C_GLAN:C_GLAN + 1], yb)
            after(c + 2, dn, 5)
            c += 8

            norm_ssq(7, X[:, 0, :])
            after(c - 1, dn)
            turn(7, gcol(1, C_ONORM), hhi)
            MQ, MK, MV, MZ = ar(0, KD, S), ar(2048, KD, S), ar(4096, NT, D), ar(6144, NT, D)

            def att_exp(c2):
                PB = ar(8192 + 768 * (c2 % 2), 2, 384)
                act.wait_ge(sem("a_max"), c2 + 1)
                for r in range(2):
                    for i in range(NT):
                        v = PB[:, r, 0:128] if i == 0 else PB[:, r, 128:384]
                        k = 4 * c2 + 2 * i + r
                        ins = act.activation(v, v, ACT.Exp, bias=gbv(2048, 32)[:, k:k + 1],
                                             accum_out=gbv(2080, 32)[:, k:k + 1])
                ins.then_inc(sem("a_exp"), 1)

            for n in range(8):
                if n == 6:
                    att_exp(0)
                    att_exp(1)
                after(c, dn, 2)
                c += 2
                used(c - 1, dn)
                b = 2 * (n % 2)
                kind, half = n // 2, n % 2
                if kind < 2:
                    ins = act.activation((MQ, MK)[kind][:, 4 * half:4 * half + 4, :],
                                         ps[:, b:b + 2, :].rearrange("p b (c t) -> p (b c) t", c=2), ACT.Copy,
                                         scale=0.125 if kind == 0 else 1.0)
                else:
                    for i in range(NT):
                        ins = act.activation((MV, MZ)[kind - 2][:, i, 512 * half:512 * (half + 1)], ps[:, b + i, :],
                                             ACT.Copy if kind == 2 else ACT.Silu)
                ins.then_inc(sem("o_ev"), 1)
            for c2 in range(8):
                if c2 >= 2:
                    att_exp(c2)
                if c2 >= 1:
                    att_copy(c2 - 1)
            att_copy(7)
            turn(8, lambda c: one_col, ya)
            load_gain(a["final_norm_2"])
            after(c, dn, 4)
            norm_ssq(8, X[:, 0, :])


        @block.vector
        def _(dve):
            steps = [0]
            s_dve = sem("dve_step")

            def link(ins):
                steps[0] += 1
                ins.then_inc(s_dve, 1)
                dve.wait_ge(s_dve, steps[0])

            def tt(o, x, y, op):
                return dve.tensor_tensor(o, x, y, op)

            def split(u):
                c, d = u
                if c >= U_END:
                    return
                dve.wait_ge(w_hi, plus(c + 1, 6, d))
                dve.tensor_tensor(lo_of(u), raw[:, c % RAW, :], hi_of(u).bitcast(F32), ALU.subtract).then_inc(w_lo, 1)

            def after(c, d=0, n=1):
                for i in range(n):
                    split((c + i + SPL, d))

            def used(c, d=0):
                dve.wait_ge(w_used, plus(c + 1, 6, d))

            def log1p_half(x, o, t, n):
                z, w = t[:, 0:n], t[:, 32:32 + n]
                link(dve.tensor_scalar(w, x, 2.0, None, ALU.add))
                link(dve.reciprocal(z, w))
                link(tt(z, z, x, ALU.mult))
                link(tt(w, z, z, ALU.mult))
                link(dve.tensor_scalar(o, w, 1.0 / 13, None, ALU.mult))
                for k in (11, 9, 7, 5, 3):
                    link(dve.scalar_tensor_tensor(o, o, 1.0 / k, w, ALU.add, ALU.mult))
                link(dve.scalar_tensor_tensor(o, o, 1.0, z, ALU.add, ALU.mult))

            dve.memset(gb[:, 0:2048], 0.0).then_inc(sem("bd_zero"), 1)
            def ssq_of(k, src, junk):
                if k == 0:
                    dve.wait_ge(s_x, 16)
                dve.tensor_tensor_reduce(junk, src, src, 1.0, 0.0, ALU.mult, ALU.add, ssq[:, 1:2]).then_inc(sem("ssq_v"), 1)

            def normed(k, src):
                dve.wait_ge(sem("rstd"), k + 1)
                for i in range(NT):
                    dve.tensor_scalar(HTOK[:, i, :], src[:, i, :], rst[:, i:i + 1], None, ALU.mult).then_inc(sem("h_ready"), 1)

            def turn(k, gain, hi=None, lo=None, full=None):
                b = TB[k]
                if hi is None:
                    dve.wait_ge(sem("turned"), 4 * k + 4)
                    for c in range(4, 8):
                        ins = dve.tensor_scalar(full[:, c, :], ps[:, b + c // 2, (c % 2) * S:(c % 2 + 1) * S], gain(c), None, ALU.mult)
                    ins.then_inc(sem("full_v"), 1)
                    return
                for c in range(KD):
                    if c % 2 == 0:
                        dve.wait_ge(sem("t_hi"), 4 * (k - (k > 3)) + c // 2 + 1)
                    ins = dve.scalar_tensor_tensor(lo[:, S * c:S * (c + 1)], ps[:, b + c // 2, (c % 2) * S:(c % 2 + 1) * S], gain(c),
                                                   hi[:, S * c:S * (c + 1)].bitcast(F32), ALU.mult, ALU.subtract)
                    if c % 4 == 3:
                        ins.then_inc(sem("t_lo"), 1)

            def gcol(t, o):
                return lambda c: PT[:, t, o + c:o + c + 1]

            def residual(last, d=0):
                xp[0] += 1
                for i in range(NT):
                    if i == 0:
                        dve.wait_ge(sem("proj0"), xp[0])
                    else:
                        used(last, d)
                    for h in range(2):
                        ins = tt(X[:, i, 512 * h:512 * (h + 1)], X[:, i, 512 * h:512 * (h + 1)], ps[:, 4 + 2 * i + h, :], ALU.add)
                    ins.then_inc(sem("x_ready" if i else "x0_ready"), 1)
                xr[0] += 1
                dve.wait_ge(sem("x_ready"), xr[0])

            xp = [0]
            xr = [0]

            def col(t, o):
                return PT[:, t, o:o + 1]

            def bank2(b):
                return ps[:, b:b + 2, :].rearrange("p b (c t) -> p (b c) t", c=2)

            def lru(l, c0):
                dve.memset(UP[:, :, 0:3], 0.0)
                link(dve.memset(CV[:, :, 0:2], 0.0))
                after(c0, n=2)
                dve.wait_ge(sem("lru_ev"), 3 * l + 1)
                w = C_LCONV + 16 * l
                for c in range(4):
                    ins = dve.tensor_scalar(UC[:, c, :], UP[:, c, 0:S], col(0, w + c), col(0, C_LCB + 4 * l + c), ALU.mult, ALU.add)
                link(ins)
                for k in range(1, 4):
                    for c in range(4):
                        ins = dve.scalar_tensor_tensor(UC[:, c, :], UP[:, c, k:k + S], col(0, w + 4 * k + c), UC[:, c, :], ALU.mult, ALU.add)
                    if k < 3:
                        link(ins)
                ins.then_inc(sem("lru_uc"), 1)
                dve.wait_ge(sem("lru_uc"), l + 1)
                after(c0 + 2, n=2)
                dve.wait_ge(sem("lru_ev"), 3 * l + 2)
                link(tt(GT, GG, GG, ALU.mult))
                link(dve.tensor_scalar(GT, GT, 0.044715, 1.0, ALU.mult, ALU.add))
                tt(GT, GT, GG, ALU.mult).then_inc(sem("lru_gt"), 1)
                after(c0 + 4)
                dve.wait_ge(sem("lru_i"), l + 1)
                tt(II, II, UC, ALU.mult)
                dve.wait_ge(sem("lru_sg"), l + 1)
                link(tt(GG, GG, GT, ALU.mult))
                dve.wait_ge(sem("lru_a"), l + 1)
                link(tt(GT, RR, RR, ALU.mult))
                dve.scalar_tensor_tensor(TT, GT, 1.0, TT, ALU.add, ALU.mult).then_inc(sem("lru_m"), 1)
                after(c0 + 5, n=2)
                dve.wait_ge(sem("lru_s"), l + 1)
                link(tt(TT, TT, II, ALU.mult))
                for c in range(4):
                    ins = dve.tensor_tensor_scan(UC[:, c, :], RR[:, c, :], TT[:, c, :], 0.0, ALU.mult, ALU.add)
                link(ins)
                tt(YF[:, 4:8, :], UC, GG, ALU.mult).then_inc(sem("lru_y"), 1)
                after(c0 + 7)

                def lo_half(h):
                    dve.wait_ge(sem("lru_yhi"), 2 * l + 2 - h)
                    tt(ya[:, 2048 + 1024 * h:3072 + 1024 * h], YF[:, 4 * h:4 * h + 4, :].rearrange("p c t -> p (c t)"),
                       ya[:, 1024 * h:1024 * (h + 1)].bitcast(F32), ALU.subtract).then_inc(sem("lru_ylo"), 1)

                used(c0 + 7)
                dve.wait_ge(sem("lru_ev"), 3 * l + 3)
                tt(CV[:, :, 2:258], CO, bank2(2), ALU.mult).then_inc(sem("lru_v"), 1)
                dve.wait_ge(sem("lru_v"), l + 1)
                w = C_CONV + 12 * l
                for c in range(4):
                    ins = dve.tensor_scalar(CO[:, c, :], CV[:, c, 0:S], col(0, w + c), None, ALU.mult)
                link(ins)
                for k in range(1, 3):
                    for c in range(4):
                        ins = dve.scalar_tensor_tensor(CO[:, c, :], CV[:, c, k:k + S], col(0, w + 4 * k + c), CO[:, c, :], ALU.mult, ALU.add)
                    link(ins)
                lo_half(1)
                after(c0 + 8, n=2)
                used(c0 + 9)
                tt(YF[:, 0:4, :], CO, bank2(0), ALU.mult).then_inc(sem("lru_y"), 1)
                lo_half(0)
                after(c0 + 10, n=3)
                residual(c0 + 13)

            ssq_of(0, X[:, 1, :], HTOK[:, 1, :])
            normed(0, X)
            split((0, 0))
            dve.wait_ge(s_pt, 1)
            dve.tensor_copy(PT[:, 0, 0:R0], ps[:, 0, 0:R0]).then_inc(s_ptc, 1)
            dve.wait_ge(s_ptc, 1)
            LAM = PT[:, 0, C_LAM:C_LAM + 8]
            dve.scalar_tensor_tensor(sm[:, 72:80], LAM, -1.0, LAM, ALU.mult, ALU.max).then_inc(sem("lam_abs"), 1)

            turn(0, gcol(0, C_NMIX), hhi, hlo)
            for u in range(1, SPL):
                split((u, 0))
            dve.wait_ge(sem("lam_exp"), 1)
            TS1 = gb[:, 3840:3904]
            log1p_half(sm[:, 80:88], sm[:, 88:96], TS1, 8)
            link(dve.tensor_scalar(sm[:, 96:104], LAM, -1.0, 0.0, ALU.mult, ALU.max))
            link(dve.scalar_tensor_tensor(sm[:, 88:96], sm[:, 88:96], 2.0, sm[:, 96:104], ALU.mult, ALU.add))
            dve.tensor_scalar(s8, sm[:, 88:96], -8.0, None, ALU.mult).then_inc(sem("s8"), 1)

            lru(0, U_LRU0)
            ssq_of(1, X[:, 1, :], HTOK[:, 1, :])
            dve.wait_ge(s_pt, 2)
            dve.tensor_copy(PT[:, 1, 0:R1], ps[:, 0, 0:R1]).then_inc(s_ptc, 1)
            normed(1, X)
            after(U_LRU0 + 13)
            turn(1, gcol(0, C_NFFN), hhi, hlo)

            SG, HF = ar(0, 4, S), ar(1024, 4, S)

            def hidden(g):
                dve.wait_ge(sem("f_silu"), g + 1)
                tt(HF, SG, bank2(2), ALU.mult).then_inc(sem("f_h"), 1)
                dve.wait_ge(sem("f_hi"), g + 1)
                tt(ya[:, 1024:2048], HF.rearrange("p c t -> p (c t)"), ya[:, 0:1024].bitcast(F32), ALU.subtract).then_inc(sem("f_lo"), 1)

            after(U_FFN, n=4)
            used(U_FFN + 3)
            hidden(0)
            with dve.Fori(1, NG) as g:
                dd = dve.snap(g - 1)
                after(U_FFN + 4, dd, 5)
                used(U_FFN + 9, dd)
                hidden(g)
                after(U_FFN + 9, dd)
            after(U_FFN + 40)
            residual(U_FFN + 41)

            ssq_of(2, X[:, 1, :], HTOK[:, 1, :])
            normed(2, X)
            after(U_FFN + 41)
            turn(2, gcol(0, C_NMIX + 8), hhi, hlo)
            lru(1, U_LRU1)
            ssq_of(3, X[:, 1, :], HTOK[:, 1, :])
            normed(3, X)
            after(U_LRU1 + 13)
            turn(3, gcol(0, C_NFFN + 8), full=hTf)
            dve.wait_ge(s_bg, 16)
            for i in range(NT):
                ins = tt(HTOK[:, i, :], HTOK[:, i, :], BG, ALU.mult)
            ins.then_inc(sem("htok"), 1)

            L, EX = ar(0, NT, NE), ar(256, NT, NE)
            GT3, EQ3 = ar(512, NT, NE * NE), ar(640, NT, NE * NE)
            LTM = ar(768, NE * NE)
            CH, MX, SMX = ar(832, NT, NE), ar(848, NT), ar(852, NT)
            CNT, OV, OVR, SEL = ar(860, NE), ar(868, NE), ar(876, NE), ar(884, NE)
            T16, T8 = ar(900, NT, NE), ar(920, NE)
            POS, COMB = ar(2048, NT, 12), ar(2080, NT, 12)
            JP, JC = ar(2112, NT), ar(2116, NT)
            TF = ar(2120, 4)

            def e3(x):
                return x.rearrange("p i (e f) -> p i e f", e=NE)

            for e in range(NE):
                if e:
                    dve.memset(LTM[:, NE * e:NE * e + e], 1.0)
                ins = dve.memset(LTM[:, NE * e + e:NE * e + NE], 0.0)
            link(ins)
            dve.wait_ge(sem("htok_hi"), 1)
            tt(hlo[:, :], HTOK.rearrange("p i n -> p (i n)"), hhi[:, :].bitcast(F32), ALU.subtract).then_inc(sem("htok_lo"), 1)
            XEh, XEl = ya[:, 0:1024], ya[:, 1024:2048]
            HTh, HTl = ya[:, 2048:2560], ya[:, 2560:3072]
            SR = ya[:, 3072:3328].rearrange("p (i s) -> p i s", i=NT)
            ST = ya[:, 3328:3584]
            Yh, Yl = yb[:, 0:1024], yb[:, 1024:2048]
            MSG, MHF = ar(1024, 512), ar(1536, 512)
            dve.memset(Yh.bitcast(F32), 0.0)
            dve.memset(Yl.bitcast(F32), 0.0)
            dve.memset(JC, 0.0)
            dve.memset(ST.bitcast(F32), 0.0).then_inc(sem("m_st"), 1)
            dve.memset(ar(2120, 1), 0.0).then_inc(sem("m_ylo"), 1)
            dve.wait_ge(sem("r_log"), 1)
            link(dve.tensor_copy(L, ps[:, 4, 0:16].rearrange("p (i e) -> p i e", i=NT)))
            other = L.unsqueeze(2).to_broadcast([P, NT, NE, NE])
            own = L.unsqueeze(3).to_broadcast([P, NT, NE, NE])
            link(tt(e3(GT3), other, own, ALU.is_gt))
            link(tt(e3(EQ3), other, own, ALU.is_equal))
            link(tt(EQ3, EQ3, LTM.unsqueeze(1).to_broadcast([P, NT, NE * NE]), ALU.mult))
            link(tt(GT3, GT3, EQ3, ALU.add))
            link(dve.tensor_reduce(T16, e3(GT3), AX_X, ALU.add))
            dve.tensor_scalar(CH, T16, 2.0, None, ALU.is_lt).then_inc(sem("r_ch"), 1)
            link(dve.tensor_reduce(MX, L, AX_X, ALU.max))
            tt(EX, L, MX.unsqueeze(2).to_broadcast([P, NT, NE]), ALU.subtract).then_inc(sem("r_sub"), 1)
            dve.wait_ge(sem("r_ch"), 1)
            dve.wait_ge(sem("r_exp"), 1)
            link(tt(EX, EX, CH, ALU.mult))
            link(dve.tensor_reduce(SMX, EX, AX_X, ALU.add))
            link(dve.reciprocal(MX, SMX))
            link(tt(COMB[:, :, 0:NE], EX, MX.unsqueeze(2).to_broadcast([P, NT, NE]), ALU.mult))
            dve.wait_ge(sem("r_pos"), 1)
            R = ps[:, 5, 0:24].rearrange("p (i e) -> p i e", i=3)
            link(dve.tensor_copy(CNT, R[:, 2, :]))
            link(dve.scalar_tensor_tensor(T16, R[:, 0:2, :], 1.0, CH, ALU.add, ALU.mult))
            link(dve.tensor_scalar(POS[:, :, 0:NE], T16, -1.0, None, ALU.add))
            def onehot(j):
                dve.tensor_copy(JP, POS[:, :, bass.ds(j, 1)].rearrange("p i o -> p (i o)")).then_inc(sem("m_jp"), 1)
                dve.wait_ge(sem("m_jp"), j + 1)
                for i in range(NT):
                    ins = dve.tensor_scalar(SR[:, i, :], iot[:, :], JP[:, i:i + 1], None, ALU.is_equal)
                ins.then_inc(sem("m_s"), 1)

            onehot(0)
            link(dve.tensor_scalar(OV, CNT, float(P), None, ALU.is_gt))
            link(tt(e3(GT3)[:, 0, :, :], OV.unsqueeze(1).to_broadcast([P, NE, NE]), LTM.rearrange("p (e f) -> p e f", e=NE), ALU.mult))
            link(dve.tensor_reduce(OVR, e3(GT3)[:, 0, :, :], AX_X, ALU.add))
            for m in range(3):
                link(dve.tensor_scalar(SEL, OVR, float(m), None, ALU.is_equal))
                link(tt(SEL, SEL, OV, ALU.mult))
                sel2 = SEL.unsqueeze(1).to_broadcast([P, NT, NE])
                link(tt(EX, T16, sel2, ALU.mult))
                link(dve.tensor_reduce(MX, EX, AX_X, ALU.add))
                link(dve.tensor_scalar(POS[:, :, NE + m], MX, -1.0 - P, None, ALU.add))
                link(tt(EX, COMB[:, :, 0:NE], sel2, ALU.mult))
                link(dve.tensor_reduce(COMB[:, :, NE + m], EX, AX_X, ALU.add))
                link(tt(T8, SEL, iot[:, 0:NE], ALU.mult))
                link(dve.tensor_reduce(TF[:, m:m + 1], T8, AX_X, ALU.add))
            link(dve.memset(POS[:, :, 11:12], -1.0))
            link(dve.tensor_reduce(TF[:, 3:4], OV, AX_X, ALU.add))
            link(dve.tensor_scalar(TF[:, 3:4], TF[:, 3:4], float(NE), None, ALU.add))
            dve.wait_ge(s_const, 1)
            dve.tensor_copy(tab[:, :], TF).then_inc(sem("tab_ready"), 1)
            dve.wait_ge(sem("tab_ready"), 1)

            njobs = dve.value_load(tab[0:1, 3:4], min_val=NE, max_val=NJMAX)

            def gath_lo(k):
                dve.wait_ge(sem("m_xhi"), k + 1)
                tt(XEl, ps[:, 5:7, :].rearrange("p b n -> p (b n)"), XEh.bitcast(F32), ALU.subtract).then_inc(sem("m_xlo"), 1)

            def ht_lo(g):
                dve.wait_ge(sem("m_hthi"), g + 1)
                tt(HTl, ps[:, 4, :], HTh.bitcast(F32), ALU.subtract).then_inc(sem("m_htlo"), 1)

            def hid(g):
                dve.wait_ge(sem("m_silu"), g + 1)
                tt(MHF, MSG, ps[:, 1, :], ALU.mult).then_inc(sem("m_h"), 1)

            def scatter(k):
                dve.wait_ge(sem("m_sct"), k + 1)
                for i in range(NT):
                    for h in range(2):
                        ins = dve.scalar_tensor_tensor(X[:, i, 512 * h:512 * (h + 1)], ps[:, 4 + 2 * i + h, :], JC[:, i:i + 1],
                                                       X[:, i, 512 * h:512 * (h + 1)], ALU.mult, ALU.add)
                ins.then_inc(sem("m_sev"), 1)

            def group_end(dd):
                after(U_MOE + 6, dd, 2)
                used(U_MOE + 7, dd)
                hid(dd + 1)
                after(U_MOE + 8, dd, 2)

            gath_lo(0)
            with dve.Fori(0, njobs) as j:
                dj = dve.snap(j * NG)
                after(U_MOE, dj, 4)
                used(U_MOE + 3, dj)
                hid(dj)
                scatter(j)
                dve.wait_ge(sem("m_sev"), j + 1)
                dve.tensor_copy(JC, COMB[:, :, bass.ds(j, 1)].rearrange("p i o -> p (i o)"))
                after(U_MOE + 4, dj, 2)
                ht_lo(dj)
                dve.wait_ge(sem("m_str"), j + 1)
                dve.tensor_copy(ST, ps[:, 7, 0:256]).then_inc(sem("m_st"), 1)
                onehot(j + 1)
                group_end(dj)
                with dve.Fori(2, NG) as g:
                    dd = dve.snap(dj + g - 1)
                    after(U_MOE + 4, dd, 2)
                    ht_lo(dd)
                    group_end(dd)
                ht_lo(dj + (NG - 1))
                gath_lo(j + 1)
                after(U_MOE + 40, dj)
                dve.wait_ge(sem("m_yhi"), j + 1)
                tt(Yl, ps[:, 2:4, :].rearrange("p b n -> p (b n)"), Yh.bitcast(F32), ALU.subtract).then_inc(sem("m_ylo"), 1)
                after(U_MOE + 41, dj)
            scatter(njobs)
            dve.wait_ge(sem("m_sev"), njobs + 1)
            dn = dve.snap(njobs * NG)
            dve.memset(ar(2124, 1), 0.0).then_inc(sem("x_ready"), 1)
            xr[0] += 1
            dve.wait_ge(sem("x_ready"), xr[0])

            ssq_of(4, X[:, 1, :], HTOK[:, 1, :])
            dve.wait_ge(sem("rstd"), 5)
            dve.wait_ge(s_bg, 32)
            for i in range(NT):
                ins = dve.scalar_tensor_tensor(X[:, i, :], X[:, i, :], rst[:, i:i + 1], BG, ALU.mult, ALU.mult)
                ins.then_inc(sem("x_ready" if i else "x0_ready"), 1)
            xr[0] += 1
            dve.wait_ge(sem("x_ready"), xr[0])

            ssq_of(5, X[:, 1, :], HTOK[:, 1, :])
            XP, CVV = ar(0, 10, 259), ar(2592, 10, S)
            link(dve.memset(XP[:, :, 0:3], 0.0))
            normed(5, X)
            turn(4, gcol(1, C_ENORM), hhi, hlo)
            c = U_SSD

            def conv(lo, hi):
                for q in range(lo, hi):
                    ins = dve.tensor_scalar(CVV[:, q, :], XP[:, q, 0:S], col(1, C_ECONV + q), col(1, C_ECB + q), ALU.mult, ALU.add)
                link(ins)
                for k in range(1, 4):
                    for q in range(lo, hi):
                        ins = dve.scalar_tensor_tensor(CVV[:, q, :], XP[:, q, k:k + S], col(1, C_ECONV + 10 * k + q),
                                                       CVV[:, q, :], ALU.mult, ALU.add)
                    if k < 3:
                        link(ins)
                return ins

            after(c, dn, 2)
            dve.wait_ge(sem("e_ev"), 1)
            link(conv(0, 4))
            after(c + 2, dn, 2)
            dve.wait_ge(sem("e_ev"), 2)
            conv(4, 8).then_inc(sem("e_conv"), 1)
            after(c + 4, dn, 1)
            DX, DTT, DTA = gbv(2944, NT, 16), gbv(2864, NT, 16), gbv(2896, NT, 16)
            ACS, DEC, EA = gbv(2720, 32), gbv(2752, 16), gbv(2816, 32)
            dve.wait_ge(sem("d_ps"), 1)
            link(tt(DX, ps[:, 4, 0:32].rearrange("p (i h) -> p i h", i=NT), gbv(2928, 16).unsqueeze(1).to_broadcast([P, NT, 16]), ALU.add))
            dve.scalar_tensor_tensor(sm[:, 128:160], gbv(2944, 32), -1.0, gbv(2944, 32), ALU.mult, ALU.max).then_inc(sem("d_abs"), 1)
            dve.wait_ge(sem("e_ev"), 3)
            conv(8, 10).then_inc(sem("e_conv"), 1)
            after(c + 5, dn, 2)
            dve.wait_ge(sem("d_exp"), 1)
            log1p_half(sm[:, 160:192], sm[:, 208:240], TS1, 32)
            link(dve.tensor_scalar(gbv(2944, 32), gbv(2944, 32), 0.0, None, ALU.max))
            link(dve.scalar_tensor_tensor(gbv(2864, 32), sm[:, 208:240], 2.0, gbv(2944, 32), ALU.mult, ALU.add))
            dve.wait_ge(sem("d_exp"), 2)
            dve.scalar_tensor_tensor(DTA, DTT, -1.0, gbv(2704, 16).unsqueeze(1).to_broadcast([P, NT, 16]), ALU.mult, ALU.mult).then_inc(sem("d_dta"), 1)
            after(c + 7, dn, 2)
            dve.wait_ge(sem("d_cum"), 1)
            link(dve.tensor_copy(ACS, ps[:, 5, 0:32]))
            tt(DEC, ps[:, 5, 32:48], ACS[:, 0:16], ALU.subtract).then_inc(sem("d_acs"), 1)
            XS, XDT, XDD = ar(5152, NT, D), ar(0, NT, D), ar(9248, D)

            def heads(x, n=32):
                return x.rearrange("p (h d) -> p h d", h=n)

            def per_head(x, n=32, d=64):
                return x.unsqueeze(2).to_broadcast([P, n, d])

            dve.wait_ge(sem("s_xtr"), 1)
            dve.tensor_copy(ar(5152, 1024), ps[:, 4:6, :].rearrange("p b n -> p (b n)")).then_inc(sem("s_xs"), 1)
            dve.wait_ge(sem("s_xs"), 2)
            link(tt(heads(ar(0, 1024), 16), heads(ar(5152, 1024), 16), per_head(gbv(2864, 16), 16), ALU.mult))
            dve.wait_ge(sem("d_ea"), 2)
            tt(heads(XDD, 16), heads(ar(0, 1024), 16), per_head(gbv(2848, 16), 16), ALU.mult).then_inc(sem("s_xdd"), 1)
            dve.wait_ge(sem("s_cbt"), 1)
            CBM = gb[:, 0:512].rearrange("p (i g t) -> p i g t", i=2, g=2)
            for gr in range(2):
                tt(CBM[:, :, gr, :], ps[:, 4 + gr, 0:256].rearrange("p (i t) -> p i t", i=2),
                   utri[:, :].unsqueeze(1).to_broadcast([P, 2, P]), ALU.mult)
            dve.tensor_copy(gbv(512, 128), ps[:, 6, 0:128]).then_inc(sem("s_cb"), 1)
            dve.wait_ge(sem("s_stp"), 1)
            dve.tensor_copy(gb[0:64, 640:1152], ps[0:64, 6, :])
            dve.tensor_copy(gb[64:128, 640:1152], ps[64:128, 7, :]).then_inc(sem("s_st"), 1)
            Y = ar(2592, NT, D)
            Z = ar(7200, NT, D)

            def mask_mul(q):
                dve.wait_ge(sem("s_exp"), q + 1)
                mb = ar(9248 + 512 * (q % 2), 4, P)
                tt(mb, mb, CBM[:, q // 4, (q % 4) // 2, :].unsqueeze(1).to_broadcast([P, 4, P]), ALU.mult).then_inc(sem("s_m"), 1)

            def y_out(i):
                dve.wait_ge(sem("s_yq"), 4 * i + 4)
                dve.wait_ge(sem("s_skip"), 1)
                yi = ar(2592 + 1024 * i, D)
                tt(yi, yi, ps[:, 6:8, :].rearrange("p b n -> p (b n)"), ALU.add).then_inc(sem("s_ye"), 1)

            dve.wait_ge(sem("s_cb"), 1)
            dve.wait_ge(sem("s_st"), 1)
            for q in range(8):
                i = q // 4
                dve.wait_ge(sem("s_segp"), q + 1)
                if q >= 2:
                    dve.wait_ge(sem("s_yq"), q - 1)
                for h in range(4):
                    hh = 16 * i + 4 * (q % 4) + h
                    ins = dve.tensor_scalar(ar(9248 + 512 * (q % 2) + P * h, P), ps[:, 4 + q % 2, P * h:P * (h + 1)],
                                            ACS[:, hh:hh + 1], 0.0, ALU.subtract, ALU.min)
                ins.then_inc(sem("s_seg"), 1)
                mask_mul(q)
                if q == 0:
                    tt(heads(ar(1024, D), 16), heads(ar(6176, D), 16), per_head(gbv(2880, 16), 16), ALU.mult).then_inc(sem("s_xdt1"), 1)
                if q == 5:
                    y_out(0)
            y_out(1)
            dve.wait_ge(sem("s_yoff"), 1)
            dve.wait_ge(sem("s_ye"), 2)
            link(tt(heads(ar(5152, D), 16), ps[:, 4:6, :].rearrange("p b (h d) -> p (b h) d", d=64), per_head(EA[:, 16:32], 16), ALU.mult))
            link(tt(Y[:, 1, :], Y[:, 1, :], ar(5152, D), ALU.add))
            dve.wait_ge(sem("e_ev"), 5)
            tt(ar(2592, 2048), ar(2592, 2048), ar(7200, 2048), ALU.mult).then_inc(sem("x_ready"), 1)
            xr[0] += 1
            dve.wait_ge(sem("x_ready"), xr[0])
            ssq_of(6, Y[:, 1, :], ar(6176, D))
            normed(6, Y)
            after(c + 9, dn, 4)
            c += 13
            turn(5, gcol(1, C_SSDN), ya[:, 0:2048], ya[:, 2048:4096])

            Q, K = ar(0, 4, S), ar(1024, 4, S)
            TMP, GC, Q1, K1 = ar(2560, 4, S), ar(3584, 4, S), ar(4608, 4, S), ar(5632, 4, S)
            Q4 = ar(6656, 2048)
            SCT = gb[:, 2048:3072]
            S1 = [None, gb[:, 3072:3584], gb[:, 3584:4096], ar(2048, 512)]
            dve.wait_ge(sem("g_x"), 1)
            for q in range(4):
                ins = dve.tensor_scalar(GC[:, q, :], ps[:, 4 + q // 2, (q % 2) * S:(q % 2 + 1) * S], col(1, C_GB + q), None, ALU.add)
            link(ins)
            dve.scalar_tensor_tensor(TMP, GC, -1.0, GC, ALU.mult, ALU.max).then_inc(sem("g_abs"), 1)
            dve.memset(Q4, 0.0)
            dve.memset(SCT, 0.0)
            dve.wait_ge(sem("g_ln"), 1)
            link(dve.scalar_tensor_tensor(TMP, GC, 0.0, TMP, ALU.min, ALU.subtract))
            for q in range(4):
                ins = dve.tensor_tensor_scan(GC[:, q, :], m01[:, :], TMP[:, q, :], 0.0, ALU.mult, ALU.add)
            link(ins)

            def ch(x):
                return x.rearrange("p c (n t) -> p (c n) t", t=64)

            tt(ch(TMP), ch(GC), ch(GC)[:, :, 32:33].to_broadcast([P, 16, 64]), ALU.subtract).then_inc(sem("g_ref"), 1)
            after(c, dn, 2)
            dve.wait_ge(sem("e_ev"), 7)
            dve.wait_ge(sem("g_e"), 2)
            tt(Q1, Q1, Q, ALU.mult)
            tt(K1, K1, K, ALU.mult)
            tt(ch(TMP), ch(GC), ch(GC)[:, :, 63:64].to_broadcast([P, 16, 64]), ALU.subtract).then_inc(sem("g_ref"), 1)
            after(c + 2, dn, 2)
            dve.wait_ge(sem("g_e"), 5)
            tt(K, K, TMP, ALU.mult).then_inc(sem("g_k2"), 1)
            qv = Q.rearrange("p c (i r t) -> p (c i) r t", i=2, r=2)
            gv = GC.rearrange("p c (i r t) -> p (c i) r t", i=2, r=2)
            Q5 = Q4.rearrange("p (ci r t) -> p ci r t", r=2, t=P)
            for r in range(2):
                ins = tt(Q5[:, :, r, 64 * r:64 * r + 64], qv[:, :, r, :], gv[:, :, r, :], ALU.mult)
            ins.then_inc(sem("g_q"), 1)
            after(c + 4, dn, 4)
            c += 8
            dve.wait_ge(sem("g_q"), 1)
            dve.wait_ge(sem("g_k2p"), 1)
            dve.tensor_copy(ar(3584, 1024), ps[:, 4:6, :].rearrange("p b n -> p (b n)")).then_inc(sem("g_k2t"), 1)
            bd4 = bdm[:, :].unsqueeze(1).to_broadcast([P, 4, P])

            def scores(i):
                dve.wait_ge(sem("g_sc"), i + 1)
                if i:
                    dve.wait_ge(sem("g_o"), i)
                for r in range(2):
                    ins = dve.copy_predicated(SCT[:, 512 * r:512 * (r + 1)].rearrange("p (c t) -> p c t", c=4), bd4,
                                              ps[:, 6 + r, :].rearrange("p (c t) -> p c t", c=4))
                ins.then_inc(sem("g_sct"), 1)

            def state(n):
                dve.wait_ge(sem("g_kv"), n)
                kv = ps[:, 0:2, :].rearrange("p b (c v) -> p (b c) v", c=2)
                new = S1[n].rearrange("p (c v) -> p c v", c=4)
                for r in range(2):
                    pr = slice(64 * r, 64 * r + 64)
                    if n == 1:
                        ins = dve.tensor_copy(new[pr], kv[pr, :, P * r:P * (r + 1)])
                    else:
                        old = S1[n - 1].rearrange("p (c v) -> p c v", c=4)
                        for q in range(4):
                            k = 192 + 4 * q + n - 1
                            ins = dve.scalar_tensor_tensor(new[pr, q, :], old[pr, q, :], sm[pr, k:k + 1],
                                                           kv[pr, q, P * r:P * (r + 1)], ALU.mult, ALU.add)
                ins.then_inc(sem("g_s"), 1)
                dve.wait_ge(sem("g_s"), n)

            def o_out(i):
                dve.wait_ge(sem("g_o"), i + 1)
                dve.tensor_copy(ar(1024 * i, 4, 2, P), ps[:, 2:4, :].rearrange("p r (c v) -> p c r v", c=4)).then_inc(sem("g_oe"), 1)

            scores(0)
            state(1)
            o_out(0)
            state(2)
            scores(1)
            state(3)
            o_out(1)
            dve.wait_ge(sem("g_oe"), 2)
            O = ar(0, 2048)
            link(tt(ar(4608, 2048), O, O, ALU.mult))
            dve.tensor_reduce(ssq[:, 0:16], ar(4608, 16, P), AX_X, ALU.add).then_inc(sem("ssq_v"), 1)
            after(c, dn)
            dve.wait_ge(sem("rstd"), 8)
            link(tt(heads(O, 16), heads(O, 16), per_head(rst, 16, P), ALU.mult))
            dve.wait_ge(sem("e_ev"), 11)
            for i in range(NT):
                tt(ar(1024 * i, D), ar(1024 * i, D), ar(8704 + 1024 * i, D), ALU.mult).then_inc(sem("h_ready"), 1)
            after(c + 1, dn)
            turn(6, lambda c: PT[:, 1, C_GLAN:C_GLAN + 1], yb[:, 0:2048], yb[:, 2048:4096])
            after(c + 2, dn, 5)
            c += 8
            residual(c - 1, dn)

            ssq_of(8, X[:, 1, :], HTOK[:, 1, :])
            normed(8, X)
            after(c - 1, dn)
            turn(7, gcol(1, C_ONORM), hhi, hlo)
            after(c, dn, 12)
            M3, NM, RS = gb[:, 1600:1984], gb[:, 2048:2080], gb[:, 2080:2112]
            link(dve.memset(M3, 0.0))
            dve.tensor_scalar(M3[:, 0:P], ustr[:, :], -1e30, None, ALU.mult)
            link(dve.tensor_scalar(M3[:, 256:384], ustr[:, :], -1e30, None, ALU.mult))
            OT = hTf[:, :, :].rearrange("p c t -> p (c t)").rearrange("p (i n) -> p i n", i=NT)

            def o_norm(c2):
                dve.wait_ge(sem("a_o"), c2 + 1)
                link(dve.reciprocal(RS[:, 4 * c2:4 * c2 + 4], RS[:, 4 * c2:4 * c2 + 4]))
                tt(OT[:, :, P * c2:P * (c2 + 1)].rearrange("p i (r d) -> p i r d", r=2),
                   ps[:, 2 + c2 % 2, 0:256].rearrange("p (i r d) -> p i r d", i=2, r=2),
                   RS[:, 4 * c2:4 * c2 + 4].rearrange("p (i r) -> p i r", i=2).unsqueeze(3).to_broadcast([P, 2, 2, 64]),
                   ALU.mult).then_inc(sem("a_oe"), 1)

            def att_max(c2):
                PB = ar(8192 + 768 * (c2 % 2), 2, 384)
                dve.wait_ge(sem("a_sc"), c2 + 1)
                if c2 >= 2:
                    dve.wait_ge(sem("a_pt"), c2 - 1)
                b = 4 + 2 * (c2 % 2)
                tt(PB, ps[:, b:b + 2, 0:384], M3.unsqueeze(1).to_broadcast([P, 2, 384]), ALU.add).then_inc(sem("a_sm"), 1)
                dve.wait_ge(sem("a_sm"), c2 + 1)
                dve.tensor_reduce(NM[:, 4 * c2:4 * c2 + 2], PB[:, :, 0:P], AX_X, ALU.max)
                link(dve.tensor_reduce(NM[:, 4 * c2 + 2:4 * c2 + 4], PB[:, :, P:384], AX_X, ALU.max))
                dve.tensor_scalar(NM[:, 4 * c2:4 * c2 + 4], NM[:, 4 * c2:4 * c2 + 4], -1.0, None, ALU.mult).then_inc(sem("a_max"), 1)

            att_max(0)
            att_max(1)
            after(c + 12, dn, 4)
            c += 16
            for c2 in range(2, 8):
                att_max(c2)
                o_norm(c2 - 2)
            o_norm(6)
            o_norm(7)
            dve.wait_ge(sem("a_oe"), 8)
            dve.wait_ge(sem("o_ev"), 8)
            MZ = ar(6144, NT, D)
            for i in range(NT):
                tt(OT[:, i, :], OT[:, i, :], MZ[:, i, :], ALU.mult).then_inc(sem("h_ready"), 1)
            turn(8, lambda c: one_col, ya[:, 0:2048], ya[:, 2048:4096])
            after(c, dn, 4)
            c += 4
            residual(c - 1, dn)
            ssq_of(9, X[:, 1, :], HTOK[:, 1, :])
            dve.wait_ge(sem("rstd"), 10)
            dve.wait_ge(s_bg, 48)
            for i in range(NT):
                dve.scalar_tensor_tensor(HTOK[:, i, :], X[:, i, :], rst[:, i:i + 1], BG, ALU.mult, ALU.mult).then_inc(sem("res_ready"), 1)

        @block.tensor
        def _(pe):
            def lo_ready(u):
                pe.wait_ge(w_lo, plus(u[0] + 1, 6, u[1]))

            def three(o, xh, xl, wh, wl, first, last, weights_stationary):
                if weights_stationary:
                    seq = ((wh, xh), (wh, xl), (wl, xh))
                else:
                    seq = ((xh, wh), (xh, wl), (xl, wh))
                for n, (s, m) in enumerate(seq):
                    ins = pe.matmul(o, s, m, start=first and n == 0, stop=last and n == 2, skip_group_check=True)
                return ins

            XH = hhi[:, :].rearrange("p (k t) -> p k t", k=KD)
            XL = hlo[:, :].rearrange("p (k t) -> p k t", k=KD)

            def group_f(c, bank, d=0, new=None):
                for h in range(2):
                    u = (c + h, d)
                    lo_ready(u)
                    if h == 1 and new is not None:
                        parts(new)
                    wh, wl = (x.rearrange("p (k n) -> p k n", k=4) for x in (hi_of(u), lo_of(u)))
                    for k in range(4):
                        for q in range(4):
                            ins = three(ps[:, bank + q // 2, (q % 2) * S:(q % 2 + 1) * S], XH[:, 4 * h + k, :], XL[:, 4 * h + k, :],
                                        wh[:, k, P * q:P * (q + 1)], wl[:, k, P * q:P * (q + 1)],
                                        h == 0 and k == 0 and q % 2 == 0, h == 1 and k == 3, True)
                    ins.then_inc(w_used, 1)

            def group_t(c, bank, d=0):
                for h in range(2):
                    u = (c + h, d)
                    lo_ready(u)
                    wh, wl = (x.rearrange("p (k n) -> p k n", k=4) for x in (hi_of(u), lo_of(u)))
                    for k in range(4):
                        for i in range(NT):
                            t = slice(P * i, P * (i + 1))
                            ins = three(ps[:, bank + i, :], XH[:, 4 * h + k, t], XL[:, 4 * h + k, t], wh[:, k, :], wl[:, k, :],
                                        h == 0 and k == 0, h == 1 and k == 3, False)
                    ins.then_inc(w_used, 1)

            def rows_t(u, yh, yl, first, last):
                lo_ready(u)
                wh, wl = (x.rearrange("p (k n) -> p k n", k=2) for x in (hi_of(u), lo_of(u)))
                for i in range(NT):
                    t = slice(P * i, P * (i + 1))
                    for k in range(2):
                        for h in range(2):
                            n = slice(512 * h, 512 * (h + 1))
                            ins = three(ps[:, 4 + 2 * i + h, :], yh[:, k, t], yl[:, k, t], wh[:, k, n], wl[:, k, n],
                                        first and k == 0, last and k == 1, False)
                    if last and i == 0:
                        ins.then_inc(sem("proj0"), 1)
                ins.then_inc(w_used, 1)

            def ck(x, n=KD):
                return x.rearrange("p (k t) -> p k t", k=n)

            def out_proj(c, d, n, q0, q1):
                for q in range(q0, q1):
                    y = ya if q < 4 else yb
                    k = 2 * (q % 4)
                    rows_t((c + q, d), ck(y[:, 0:2048])[:, k:k + 2, :], ck(y[:, 2048:4096])[:, k:k + 2, :], q == 0, q == n - 1)

            def turn(k, src):
                hr = 2 * k + 2
                pe.wait_ge(sem("h_ready"), hr)
                b = TB[k]
                for c in range(KD):
                    for i in range(NT):
                        o = (c % 2) * S + P * i
                        ins = pe.transpose(ps[:, b + c // 2, o:o + P], src[:, i, P * c:P * (c + 1)], ident[:, :])
                    if c % 2 == 1:
                        ins.then_inc(sem("turned"), 1)

            def parts(k, half=1):
                pe.wait_ge(sem("t_lo"), 2 * (k - (k > 3)) + half + 1)

            pe.wait_ge(s_const, 1)
            pe.wait_ge(s_par, 16 * N_PAR)
            pe.transpose(ps[:, 0, 0:R0], A[0:R0, 0:128], ident[0:R0, 0:R0]).then_inc(s_pt, 1)
            pe.wait_ge(s_ptc, 1)

            def lru(l, c0):
                group_f(c0, 0, new=2 * l)
                group_f(c0 + 2, 2)
                pe.wait_ge(sem("lru_uc"), l + 1)
                if l == 0:
                    pe.wait_ge(s_bd, 16 * N_BD)
                for m in range(2):
                    for c in range(4):
                        o = 1024 * l + 512 * m + P * c
                        ins = pe.matmul(ps[:, 4 + 2 * m + c // 2, (c % 2) * S:(c % 2 + 1) * S], gb[:, o:o + P], UC[:, c, :],
                                        start=True, stop=True)
                    ins.then_inc(sem("lru_gate"), 1)
                pe.wait_ge(sem("lru_ev"), 3 * l + 1)
                group_f(c0 + 4, 0)
                pe.wait_ge(sem("lru_ev"), 3 * l + 2)
                group_f(c0 + 6, 2)
                pe.wait_ge(sem("lru_ev"), 3 * l + 3)
                group_f(c0 + 8, 0)
                for n, q in enumerate(LRU_ROWS):
                    if n % 2 == 0:
                        pe.wait_ge(sem("lru_ylo"), 2 * l + n // 2 + 1)
                    k = 2 * q
                    rows_t((c0 + 10 + n, 0), ck(ya[:, 0:2048])[:, k:k + 2, :], ck(ya[:, 2048:4096])[:, k:k + 2, :], n == 0, n == 3)

            turn(0, HTOK)
            parts(0, 0)
            lru(0, U_LRU0)
            pe.wait_ge(s_par2, 16 * N_PAR2)
            pe.transpose(ps[:, 0, 0:R1], gb[0:R1, 2176:2304], ident[0:R1, 0:R1]).then_inc(s_pt, 1)
            pe.wait_ge(s_ptc, 2)
            turn(1, HTOK)
            parts(1, 0)

            HH, HL = ck(ya[:, 0:1024], 4), ck(ya[:, 1024:2048], 4)

            def down(c, d, g, first, last):
                pe.wait_ge(sem("f_lo"), g + 1)
                for q in range(2):
                    rows_t((c + q, d), HH[:, 2 * q:2 * q + 2, :], HL[:, 2 * q:2 * q + 2, :], first and q == 0, last and q == 1)

            group_f(U_FFN, 0, new=1)
            group_f(U_FFN + 2, 2)
            def ffn_step(g, dd, first):
                pe.wait_ge(sem("f_silu"), g)
                group_f(U_FFN + 4, 0, dd)
                pe.wait_ge(sem("f_h"), g)
                down(U_FFN + 6, dd, g - 1, first, False)
                group_f(U_FFN + 8, 2, dd)
            ffn_step(1, 0, True)
            with pe.Fori(2, NG) as g:
                ffn_step(g, pe.snap(g - 1), False)
            down(U_FFN + 40, 0, NG - 1, False, True)

            turn(2, HTOK)
            parts(2, 0)
            lru(1, U_LRU1)
            turn(3, HTOK)

            pe.wait_ge(sem("full_a"), 1)
            pe.wait_ge(sem("full_v"), 1)
            WR = gb[:, 2112:2176].rearrange("p (k n) -> p k n", k=8)
            for i in range(NT):
                for k in range(KD):
                    ins = pe.matmul(ps[:, 4, NE * i:NE * (i + 1)], hTf[:, k, P * i:P * (i + 1)], WR[:, k, :], start=k == 0, stop=k == KD - 1)
            ins.then_inc(sem("r_log"), 1)
            CH = ar(832, NT, NE)
            pe.wait_ge(sem("r_ch"), 1)
            pe.matmul(ps[:, 5, 0:8], ustr[:, :], CH[:, 0, :], start=True, stop=True)
            pe.matmul(ps[:, 5, 8:16], ones[:, :], CH[:, 0, :], start=True, stop=False)
            pe.matmul(ps[:, 5, 8:16], ustr[:, :], CH[:, 1, :], start=False, stop=True)
            pe.matmul(ps[:, 5, 16:24], ones[:, :], CH[:, 0, :], start=True, stop=False)
            pe.matmul(ps[:, 5, 16:24], ones[:, :], CH[:, 1, :], start=False, stop=True).then_inc(sem("r_pos"), 1)

            TKh = hhi[:, :].rearrange("p (i n) -> p i n", i=NT)
            TKl = hlo[:, :].rearrange("p (i n) -> p i n", i=NT)
            XEh, XEl = ck(ya[:, 0:1024]), ck(ya[:, 1024:2048])
            HTh, HTl = ck(ya[:, 2048:2560], 4), ck(ya[:, 2560:3072], 4)
            SR = ya[:, 3072:3328].rearrange("p (i s) -> p i s", i=NT)
            ST = ya[:, 3328:3584].rearrange("p (i s) -> p i s", i=NT)
            Yh, Yl = yb[:, 0:1024], yb[:, 1024:2048]
            MHF = ar(1536, 512)

            def gather(k):
                pe.wait_ge(sem("m_s"), k + 1)
                for c in range(KD):
                    o = ps[:, 5 + c // 4, P * (c % 4):P * (c % 4 + 1)]
                    n = 0
                    for i in range(NT):
                        for t in (TKh, TKl):
                            ins = pe.matmul(o, t[:, i, P * c:P * (c + 1)], SR[:, i, :], start=n == 0, stop=n == 3)
                            n += 1
                ins.then_inc(sem("m_gth"), 1)

            def moe_in(c, d, bank):
                for h in range(2):
                    u = (c + h, d)
                    lo_ready(u)
                    wh, wl = (x.rearrange("p (k n) -> p k n", k=4) for x in (hi_of(u), lo_of(u)))
                    for k in range(4):
                        ins = three(ps[:, bank, :], XEh[:, 4 * h + k, :], XEl[:, 4 * h + k, :], wh[:, k, :], wl[:, k, :],
                                    h == 0 and k == 0, h == 1 and k == 3, False)
                    ins.then_inc(w_used, 1)

            def moe_down(c, d, g, first, last):
                pe.wait_ge(sem("m_htlo"), g + 1)
                for q in range(2):
                    u = (c + q, d)
                    lo_ready(u)
                    wh, wl = (x.rearrange("p (k n) -> p k n", k=2) for x in (hi_of(u), lo_of(u)))
                    for k in range(2):
                        for h in range(2):
                            n = slice(512 * h, 512 * (h + 1))
                            ins = three(ps[:, 2 + h, :], HTh[:, 2 * q + k, :], HTl[:, 2 * q + k, :], wh[:, k, n], wl[:, k, n],
                                        first and q == 0 and k == 0, last and q == 1 and k == 1, False)
                    ins.then_inc(w_used, 1)

            def turn_h(g):
                pe.wait_ge(sem("m_h"), g + 1)
                for q in range(4):
                    ins = pe.transpose(ps[:, 4, P * q:P * (q + 1)], MHF[:, P * q:P * (q + 1)], ident[:, :])
                ins.then_inc(sem("m_tr"), 1)

            def scatter(k):
                pe.wait_ge(sem("m_ylo"), k + 1)
                pe.wait_ge(sem("m_st"), k + 1)
                for i in range(NT):
                    for h in range(2):
                        n = slice(512 * h, 512 * (h + 1))
                        pe.matmul(ps[:, 4 + 2 * i + h, :], ST[:, i, :], Yh[:, n], start=True, stop=False)
                        ins = pe.matmul(ps[:, 4 + 2 * i + h, :], ST[:, i, :], Yl[:, n], start=False, stop=True)
                ins.then_inc(sem("m_sct"), 1)

            pe.wait_ge(sem("htok_lo"), 1)
            gather(0)
            pe.wait_ge(sem("tab_ready"), 1)
            njobs = pe.value_load(tab[0:1, 3:4], min_val=NE, max_val=NJMAX)

            def moe_step(dj, dd, first, j=None):
                pe.wait_ge(sem("m_silu"), dd + 1)
                moe_in(U_MOE + 4, dd, 0)
                if first:
                    pe.wait_ge(sem("m_sev"), j + 1)
                    for i in range(NT):
                        ins = pe.transpose(ps[:, 7, P * i:P * (i + 1)], SR[:, i, :].bitcast(F32), ident[:, :])
                    ins.then_inc(sem("m_str"), 1)
                turn_h(dd)
                moe_in(U_MOE + 6, dd, 1)
                moe_down(U_MOE + 8, dd, dd, first, False)

            with pe.Fori(0, njobs) as j:
                dj = pe.snap(j * NG)
                pe.wait_ge(sem("m_xlo"), j + 1)
                moe_in(U_MOE, dj, 0)
                moe_in(U_MOE + 2, dj, 1)
                scatter(j)
                moe_step(dj, dj, True, j)
                with pe.Fori(2, NG) as g:
                    moe_step(dj, pe.snap(dj + g - 1), False)
                turn_h(dj + (NG - 1))
                gather(j + 1)
                moe_down(U_MOE + 40, dj, dj + (NG - 1), False, True)
            scatter(njobs)
            dn = pe.snap(njobs * NG)

            turn(4, HTOK)
            parts(4, 0)
            c = U_SSD
            WS = gbv(3072, KD, 32)
            CVV = ar(2592, 10, S)
            group_f(c, 0, dn, new=4)
            group_f(c + 2, 2, dn)
            pe.wait_ge(sem("e_ev"), 1)
            u = (c + 4, dn)
            lo_ready(u)
            wh, wl = (x.rearrange("p (k n) -> p k n", k=8) for x in (hi_of(u), lo_of(u)))
            for k in range(KD):
                for q in range(2):
                    ins = three(ps[:, 0, S * q:S * (q + 1)], XH[:, k, :], XL[:, k, :], wh[:, k, P * q:P * (q + 1)],
                                wl[:, k, P * q:P * (q + 1)], k == 0 and q == 0, k == KD - 1, True)
            ins.then_inc(w_used, 1)
            c += 5
            pe.wait_ge(sem("full_a"), 2)
            for i in range(NT):
                for k in range(KD):
                    ins = pe.matmul(ps[:, 4, 16 * i:16 * (i + 1)], hTf[:, k, P * i:P * (i + 1)], WS[:, k, 0:16], start=k == 0, stop=k == KD - 1)
            ins.then_inc(sem("d_ps"), 1)
            pe.wait_ge(sem("e_ev"), 2)
            group_t(c, 2, dn)
            pe.wait_ge(sem("e_ev"), 3)
            group_t(c + 2, 0, dn)
            c += 4
            DTA = gbv(2896, NT, 16)
            pe.wait_ge(sem("d_dta"), 1)
            for i in range(NT):
                pe.matmul(ps[:, 5, 16 * i:16 * (i + 1)], utri[:, :], DTA[:, i, :], start=True, stop=True)
            pe.matmul(ps[:, 5, 32:48], ones[:, :], DTA[:, 0, :], start=True, stop=True).then_inc(sem("d_cum"), 1)
            pe.wait_ge(sem("e_xbc"), 1)
            pe.wait_ge(sem("d_acs"), 1)
            for i in range(NT):
                for q in range(8):
                    ins = pe.transpose(ps[:, 4 + 2 * i + q // 4, P * (q % 4):P * (q % 4 + 1)], CVV[:, q, P * i:P * (i + 1)], ident[:, :])
            ins.then_inc(sem("s_xtr"), 1)
            pe.wait_ge(sem("e_xbc"), 2)
            pe.wait_ge(sem("s_xs"), 2)
            for gr in range(2):
                pr = slice(64 * gr, 64 * gr + 64)
                for i in range(NT):
                    t = slice(P * i, P * (i + 1))
                    pe.matmul(ps[:, 4 + gr, t], CVV[pr, 8, t], CVV[pr, 9, t], start=True, stop=True)
            pe.transpose(ps[:, 6, 0:P], CVV[:, 8, 0:P], ident[:, :]).then_inc(sem("s_cbt"), 1)
            pe.wait_ge(sem("s_cb"), 1)
            pe.wait_ge(sem("s_xdd"), 1)
            for gr in range(2):
                ins = pe.matmul(ps[:, 6 + gr, :], gbv(512, 128), ar(9248 + 512 * gr, 512), start=True, stop=True)
            ins.then_inc(sem("s_stp"), 1)
            XDT = ar(0, NT, D)

            def seg(q):
                if q >= 2:
                    pe.wait_ge(sem("s_seg"), q - 1)
                i = q // 4
                for h in range(4):
                    hh = 4 * (q % 4) + h
                    ins = pe.matmul(ps[:, 4 + q % 2, P * h:P * (h + 1)], DTA[:, i, hh:hh + 1].to_broadcast([P, P]), utri[:, :],
                                    start=True, stop=True)
                ins.then_inc(sem("s_segp"), 1)

            def y_diag(q):
                i = q // 4
                pe.wait_ge(sem("s_m"), q + 1)
                if q == 0:
                    pe.wait_ge(sem("s_st"), 1)
                if q == 4:
                    pe.wait_ge(sem("s_xdt1"), 1)
                    pe.wait_ge(sem("s_ye"), 1)
                for h in range(4):
                    hh = 4 * (q % 4) + h
                    ins = pe.matmul(ps[:, 6 + (q % 4) // 2, 64 * (hh % 8):64 * (hh % 8 + 1)], ar(9248 + 512 * (q % 2) + P * h, P),
                                    XDT[:, i, 64 * hh:64 * (hh + 1)], start=True, stop=True)
                ins.then_inc(sem("s_yq"), 1)

            seg(0)
            for q in range(8):
                if q < 7:
                    seg(q + 1)
                y_diag(q)
            pe.wait_ge(sem("s_seg"), 8)
            for gr in range(2):
                pr = slice(64 * gr, 64 * gr + 64)
                ins = pe.matmul(ps[:, 4 + gr, :], CVV[pr, 9, P:S], gb[pr, 640:1152], start=True, stop=True)
            ins.then_inc(sem("s_yoff"), 1)
            pe.wait_ge(sem("e_ev"), 4)
            group_f(c, 2, dn)
            pe.wait_ge(sem("e_ev"), 5)
            group_f(c + 2, 0, dn)
            c += 4
            pe.wait_ge(sem("e_ev"), 6)
            for k in range(KD):
                ins = pe.matmul(ps[0:16, 2, 0:S], WS[:, k, 16:32], hTf[:, k, :], start=k == 0, stop=k == KD - 1)
            ins.then_inc(sem("g_lr"), 1)
            turn(5, HTOK)
            pe.wait_ge(sem("g_lrc"), 1)
            parts(5)
            for q in range(4):
                ins = pe.matmul(ps[:, 4 + q // 2, (q % 2) * S:(q % 2 + 1) * S], gb[0:16, 3328 + P * q:3328 + P * (q + 1)], gb[0:16, 2048:2304],
                                start=True, stop=True)
            ins.then_inc(sem("g_x"), 1)
            for n in range(4):
                if n:
                    pe.wait_ge(sem("e_ev"), 6 + n)
                group_t(c, 2 if n % 2 == 0 else 0, dn)
                c += 2
            K = ar(1024, 4, S)
            Q1, K1 = ar(4608, 4, S), ar(5632, 4, S)
            K2 = ar(3584, NT, 512)
            V = gbv(0, NT, D)
            SCT = gb[:, 2048:3072]
            S1 = [None, gb[:, 3072:3584], gb[:, 3584:4096], ar(2048, 512)]
            pe.wait_ge(sem("g_k2"), 1)
            for i in range(NT):
                for q in range(4):
                    ins = pe.transpose(ps[:, 4 + i, P * q:P * (q + 1)], K[:, q, P * i:P * (i + 1)], ident[:, :])
            ins.then_inc(sem("g_k2p"), 1)
            pe.wait_ge(sem("g_q"), 1)
            pe.wait_ge(sem("e_ev"), 11)

            def scores(i):
                if i:
                    pe.wait_ge(sem("g_sct"), i)
                t = slice(P * i, P * (i + 1))
                for q in range(4):
                    for r in range(2):
                        pr = slice(64 * r, 64 * r + 64)
                        ins = pe.matmul(ps[:, 6 + r, P * q:P * (q + 1)], K1[pr, q, t], Q1[pr, q, t], start=True, stop=True)
                ins.then_inc(sem("g_sc"), 1)

            def kv(n):
                if n:
                    pe.wait_ge(sem("g_s"), n)
                else:
                    pe.wait_ge(sem("g_k2t"), 1)
                pr = slice(64 * (n % 2), 64 * (n % 2) + 64)
                for q in range(4):
                    ins = pe.matmul(ps[:, q // 2, (q % 2) * S:(q % 2 + 1) * S], K2[pr, n // 2, P * q:P * (q + 1)],
                                    V[pr, n // 2, S * q:S * (q + 1)], start=True, stop=True)
                ins.then_inc(sem("g_kv"), 1)

            def gla_out(i):
                pe.wait_ge(sem("g_sct"), i + 1)
                pe.wait_ge(sem("g_s"), 2 * i + 1)
                if i:
                    pe.wait_ge(sem("g_oe"), i)
                Q5 = ar(6656, 2048).rearrange("p (c i r t) -> p c i r t", c=4, i=2, r=2)
                for q in range(4):
                    for r in range(2):
                        pr = slice(64 * r, 64 * r + 64)
                        o = ps[:, 2 + r, P * q:P * (q + 1)]
                        hh = 2 * q + r
                        pe.matmul(o, SCT[:, 512 * r + P * q:512 * r + P * (q + 1)], V[:, i, P * hh:P * (hh + 1)], start=True, stop=False)
                        for m in range(2):
                            n = 2 * i + m
                            if n:
                                ins = pe.matmul(o, Q5[pr, q, i, m, :], S1[n][pr, P * q:P * (q + 1)], start=False, stop=m == 1)
                ins.then_inc(sem("g_o"), 1)

            scores(0)
            kv(0)
            gla_out(0)
            kv(1)
            scores(1)
            kv(2)
            gla_out(1)
            pe.wait_ge(sem("g_sct"), 2)
            out_proj(c, dn, 8, 0, 3)
            turn(6, ar(0, NT, D))
            out_proj(c, dn, 8, 3, 4)
            parts(6, 0)
            out_proj(c, dn, 8, 4, 6)
            parts(6)
            out_proj(c, dn, 8, 6, 8)
            c += 8

            turn(7, HTOK)
            parts(7, 0)
            MQ, MK, MV = ar(0, KD, S), ar(2048, KD, S), ar(4096, NT, D)

            def in_groups(n0, n1):
                for n in range(n0, n1):
                    if n >= 2:
                        pe.wait_ge(sem("o_ev"), n - 1)
                    if n < 4:
                        group_f(c + 2 * n, 2 * (n % 2), dn, new=7 if n == 0 else None)
                    else:
                        group_t(c + 2 * n, 2 * (n % 2), dn)

            def att_scores(c2):
                if c2 >= 2:
                    pe.wait_ge(sem("a_sm"), c2 - 1)
                for r in range(2):
                    pr = slice(64 * r, 64 * r + 64)
                    b = 4 + 2 * (c2 % 2) + r
                    pe.matmul(ps[:, b, 0:P], MQ[pr, c2, 0:P], MK[pr, c2, 0:P], start=True, stop=True)
                    ins = pe.matmul(ps[:, b, P:384], MQ[pr, c2, P:S], MK[pr, c2, :], start=True, stop=True)
                ins.then_inc(sem("a_sc"), 1)

            def att_turn(c2):
                pe.wait_ge(sem("a_exp"), c2 + 1)
                if c2:
                    pe.wait_ge(sem("a_ptc"), c2)
                PB = ar(8192 + 768 * (c2 % 2), 2, 384)
                for r in range(2):
                    for q in range(3):
                        ins = pe.transpose(ps[:, r, P * q:P * (q + 1)], PB[:, r, P * q:P * (q + 1)], ident[:, :])
                ins.then_inc(sem("a_pt"), 1)

            def att_out(c2):
                pe.wait_ge(sem("a_ptc"), c2 + 1)
                if c2 >= 2:
                    pe.wait_ge(sem("a_oe"), c2 - 1)
                PTB = gbv(768 * (c2 % 2), 2, 384)
                b = 2 + c2 % 2
                for r in range(2):
                    hh = slice(64 * (2 * c2 + r), 64 * (2 * c2 + r + 1))
                    pe.matmul(ps[:, b, 64 * r:64 * (r + 1)], PTB[:, r, 0:P], MV[:, 0, hh], start=True, stop=True)
                    o = ps[:, b, 128 + 64 * r:192 + 64 * r]
                    pe.matmul(o, PTB[:, r, P:256], MV[:, 0, hh], start=True, stop=False)
                    ins = pe.matmul(o, PTB[:, r, 256:384], MV[:, 1, hh], start=False, stop=True)
                ins.then_inc(sem("a_o"), 1)

            in_groups(0, 6)
            att_scores(0)
            att_scores(1)
            in_groups(6, 8)
            c += 16
            pe.wait_ge(sem("o_ev"), 7)
            for c2 in range(8):
                if 1 <= c2 < 7:
                    att_scores(c2 + 1)
                att_turn(c2)
                if c2 == 1:
                    pe.wait_ge(sem("o_ev"), 8)
                if c2:
                    att_out(c2 - 1)
            att_out(7)
            turn(8, hTf[:, :, :].rearrange("p c t -> p (c t)").rearrange("p (i n) -> p i n", i=NT))
            parts(8, 0)
            out_proj(c, dn, 4, 0, 2)
            parts(8)
            out_proj(c, dn, 4, 2, 4)


_INS = ["x", "norm_mix", "norm_ffn", "norm_final", "w_in", "conv_w", "lru_conv_w", "lru_conv_b", "lru_wa", "lru_ba",
        "lru_wx", "lru_bx", "lru_lambda", "w_out", "ffn_w_gate", "ffn_w_up", "ffn_w_down", "w_router", "moe_w_gate",
        "moe_w_up", "moe_w_down", "even_norm_2", "even_w_in_2", "even_conv_w_2", "even_conv_b_2", "even_a_log_2",
        "even_dt_bias_2", "even_d_skip_2", "even_ssd_norm_2", "even_gate_w2_2", "even_gate_b_2", "even_gla_norm_2",
        "even_w_out_2", "odd_norm_2", "odd_w_in_2", "odd_w_out_2", "final_norm_2"]


def kernel(**inputs):
    import numpy as np
    from concourse import bacc
    from concourse.bass_utils import run_bass_kernel_spmd

    nc = bacc.Bacc("TRN2", target_bir_lowering=False, num_devices=1, dynamic_dma_scratch_size=8192)
    arrays, aps = {}, {}
    for name in _INS:
        v = np.ascontiguousarray(inputs[name])
        arrays[f"in_{name}"] = v
        aps[name] = nc.dram_tensor(f"in_{name}", v.shape, mybir.dt.from_np(v.dtype), kind="ExternalInput").ap()
    out = nc.dram_tensor("out", (1, S, D), F32, kind="ExternalOutput").ap()
    build(nc, aps, out)
    return run_bass_kernel_spmd(nc, [arrays], core_ids=[0]).results[0]["out"]
```
